# Optimizing a Trainium2 kernel written in Bass

```python
import math
import jax, jax.numpy as jnp
from jax import lax
import numpy as np
import jax
import jax.numpy as jnp

D_MODEL = 1024
BATCH = 1
SEQ = 256
DEPTH = 1

N_MEM = 256
ATTN_HEADS = 8
HEAD_DIM = 64
D_ATTN = ATTN_HEADS * HEAD_DIM
D_CONV = D_MODEL - D_ATTN
CONV_WIDTH = 31
Q_BLOCK = 128
MEM_HEADS = 4
MEM_HEAD_DIM = D_MODEL // MEM_HEADS
N_GROUPS = 4
EXPERTS_PER_GROUP = 8
N_EXPERTS = N_GROUPS * EXPERTS_PER_GROUP
TOP_K_IN_GROUP = 2
D_EXPERT = D_MODEL // 2
EPS = 1e-6
OFF_Q = 0
OFF_K = OFF_Q + D_ATTN
OFF_V = OFF_K + D_ATTN
OFF_F = OFF_V + D_ATTN
OFF_C = OFF_F + ATTN_HEADS
D_IN = OFF_C + 2 * D_CONV


def rmsnorm(x, g):
    xf = x.astype(jnp.float32)
    y = xf * lax.rsqrt(jnp.mean(xf * xf, axis=-1, keepdims=True) + EPS)
    return (y * g.astype(jnp.float32)).astype(x.dtype)

def layernorm(x, g, b):
    xf = x.astype(jnp.float32)
    mu = jnp.mean(xf, axis=-1, keepdims=True)
    xc = xf - mu
    y = xc * lax.rsqrt(jnp.mean(xc * xc, axis=-1, keepdims=True) + EPS)
    return (y * g.astype(jnp.float32) + b.astype(jnp.float32)).astype(x.dtype)

def forgetting_attention(q, k, v, log_f):
    S = q.shape[2]
    c = jnp.cumsum(log_f, axis=-1)
    scale = 1.0 / math.sqrt(HEAD_DIM)
    outs = []
    for i in range(S // Q_BLOCK):
        lo, hi = i * Q_BLOCK, (i + 1) * Q_BLOCK
        s = jnp.einsum('bhqd,bhkd->bhqk', q[:, :, lo:hi], k[:, :, :hi]).astype(jnp.float32) * scale
        s = s + c[:, :, lo:hi, None] - c[:, :, None, :hi]
        causal = (lo + jnp.arange(Q_BLOCK))[:, None] >= jnp.arange(hi)[None, :]
        s = jnp.where(causal, s, -jnp.inf)
        p = jax.nn.softmax(s, axis=-1).astype(v.dtype)
        outs.append(jnp.einsum('bhqk,bhkd->bhqd', p, v[:, :, :hi]))
    return jnp.concatenate(outs, axis=2)

def conformer_conv(u, b_glu, w_dw, b_dw, ln_g, ln_b):
    u = u + b_glu
    a, gate = jnp.split(u, 2, axis=-1)
    z = a * jax.nn.sigmoid(gate)
    zp = jnp.pad(z, ((0, 0), (CONV_WIDTH - 1, 0), (0, 0)))
    z = lax.conv_general_dilated(zp, w_dw[:, None, :], window_strides=(1,), padding='VALID',
                                 dimension_numbers=('NWC', 'WIO', 'NWC'),
                                 feature_group_count=D_CONV) + b_dw
    z = layernorm(z, ln_g, ln_b)
    return jax.nn.silu(z)

def parallel_mixer(h, w_in, b_forget, b_glu, w_dw, b_dw, conv_ln_g, conv_ln_b, attn_out_g, w_out):
    B, S, _ = h.shape
    proj = h @ w_in
    def heads(t):
        return t.reshape(B, S, ATTN_HEADS, HEAD_DIM).transpose(0, 2, 1, 3)
    q = heads(proj[..., OFF_Q:OFF_K])
    k = heads(proj[..., OFF_K:OFF_V])
    v = heads(proj[..., OFF_V:OFF_F])
    log_f = jax.nn.log_sigmoid((proj[..., OFF_F:OFF_C] + b_forget).astype(jnp.float32))
    log_f = log_f.transpose(0, 2, 1)
    attn = forgetting_attention(q, k, v, log_f)
    attn = attn.transpose(0, 2, 1, 3).reshape(B, S, D_ATTN)
    attn = rmsnorm(attn, attn_out_g)
    conv = conformer_conv(proj[..., OFF_C:], b_glu, w_dw, b_dw, conv_ln_g, conv_ln_b)
    return jnp.concatenate([attn, conv], axis=-1) @ w_out

def memory_cross_attention(h, mem_n, w_mq, w_mkv, w_mo):
    B, S, _ = h.shape
    q = (h @ w_mq).reshape(B, S, MEM_HEADS, MEM_HEAD_DIM)
    kv = mem_n @ w_mkv
    k, v = jnp.split(kv, 2, axis=-1)
    k = k.reshape(B, -1, MEM_HEADS, MEM_HEAD_DIM)
    v = v.reshape(B, -1, MEM_HEADS, MEM_HEAD_DIM)
    s = jnp.einsum('bshd,bmhd->bhsm', q, k).astype(jnp.float32) / math.sqrt(MEM_HEAD_DIM)
    p = jax.nn.softmax(s, axis=-1).astype(v.dtype)
    o = jnp.einsum('bhsm,bmhd->bshd', p, v).reshape(B, S, D_MODEL)
    return o @ w_mo

def hierarchical_moe(h, w_route_group, b_route_group, w_route_expert, b_route_expert,
                     w_gate, w_up, w_down):
    B, S, D = h.shape
    t = h.reshape(-1, D)
    p_group = jax.nn.softmax((t @ w_route_group).astype(jnp.float32) + b_route_group, axis=-1)
    g_top, g_idx = lax.top_k(p_group, 1)
    e_logits = jnp.einsum('td,gde->tge', t, w_route_expert).astype(jnp.float32) + b_route_expert
    e_logits = jnp.take_along_axis(e_logits, g_idx[:, :, None], axis=1)[:, 0]
    p_exp = jax.nn.softmax(e_logits, axis=-1)
    e_top, e_idx = lax.top_k(p_exp, TOP_K_IN_GROUP)
    w = g_top * e_top / jnp.sum(e_top, axis=-1, keepdims=True)
    ids = g_idx * EXPERTS_PER_GROUP + e_idx
    gates = jnp.sum(jax.nn.one_hot(ids, N_EXPERTS, dtype=jnp.float32) * w[..., None], axis=1)
    gates = gates.astype(h.dtype).T

    def expert_step(y, args):
        wg, wu, wd, ge = args
        out = (jax.nn.silu(t @ wg) * (t @ wu)) @ wd
        return y + ge[:, None] * out, None

    y, _ = lax.scan(expert_step, jnp.zeros_like(t), (w_gate, w_up, w_down, gates))
    return y.reshape(B, S, D)

def first_inputs(seed: int = 0) -> dict:
    key = jax.random.key(seed)
    ks = iter(jax.random.split(key, 32))
    f32 = jnp.float32

    def nrm(shape, fan_in):
        return jax.random.normal(next(ks), shape, f32) * (fan_in ** -0.5)

    def gain(shape):
        return 1.0 + 0.02 * jax.random.normal(next(ks), shape, f32)

    def small(shape):
        return 0.01 * jax.random.normal(next(ks), shape, f32)

    L = DEPTH
    return {
        "x": jax.random.normal(next(ks), (BATCH, SEQ, D_MODEL), f32),
        "mem": jax.random.normal(next(ks), (BATCH, N_MEM, D_MODEL), f32),
        "norm_mix_g": gain((L, D_MODEL)),
        "w_in": nrm((L, D_MODEL, D_IN), D_MODEL),
        "b_forget": jax.random.uniform(next(ks), (L, ATTN_HEADS), f32, 1.0, 6.0),
        "b_glu": small((L, 2 * D_CONV)),
        "w_dw": nrm((L, CONV_WIDTH, D_CONV), CONV_WIDTH),
        "b_dw": small((L, D_CONV)),
        "conv_ln_g": gain((L, D_CONV)),
        "conv_ln_b": small((L, D_CONV)),
        "attn_out_g": gain((L, D_ATTN)),
        "w_out": nrm((L, D_ATTN + D_CONV, D_MODEL), D_ATTN + D_CONV),
        "norm_mem_g": gain((L, D_MODEL)),
        "mem_norm_g": gain((L, D_MODEL)),
        "w_mq": nrm((L, D_MODEL, D_MODEL), D_MODEL),
        "w_mkv": nrm((L, D_MODEL, 2 * D_MODEL), D_MODEL),
        "w_mo": nrm((L, D_MODEL, D_MODEL), D_MODEL),
        "norm_ffn_g": gain((L, D_MODEL)),
        "w_route_group": nrm((L, D_MODEL, N_GROUPS), D_MODEL),
        "b_route_group": small((L, N_GROUPS)),
        "w_route_expert": nrm((L, N_GROUPS, D_MODEL, EXPERTS_PER_GROUP), D_MODEL),
        "b_route_expert": small((L, N_GROUPS, EXPERTS_PER_GROUP)),
        "w_gate": nrm((L, N_EXPERTS, D_MODEL, D_EXPERT), D_MODEL),
        "w_up": nrm((L, N_EXPERTS, D_MODEL, D_EXPERT), D_MODEL),
        "w_down": nrm((L, N_EXPERTS, D_EXPERT, D_MODEL), D_EXPERT),
        "final_g": gain((D_MODEL,)),
    }

def first_block(x, mem, norm_mix_g, w_in, b_forget, b_glu, w_dw, b_dw, conv_ln_g, conv_ln_b,
              attn_out_g, w_out, norm_mem_g, mem_norm_g, w_mq, w_mkv, w_mo, norm_ffn_g,
              w_route_group, b_route_group, w_route_expert, b_route_expert,
              w_gate, w_up, w_down, final_g):
    for l in range(DEPTH):
        h = rmsnorm(x, norm_mix_g[l])
        x = x + parallel_mixer(h, w_in[l], b_forget[l], b_glu[l], w_dw[l], b_dw[l],
                               conv_ln_g[l], conv_ln_b[l], attn_out_g[l], w_out[l])
        h = rmsnorm(x, norm_mem_g[l])
        mem_n = rmsnorm(mem, mem_norm_g[l])
        x = x + memory_cross_attention(h, mem_n, w_mq[l], w_mkv[l], w_mo[l])
        h = rmsnorm(x, norm_ffn_g[l])
        x = x + hierarchical_moe(h, w_route_group[l], b_route_group[l], w_route_expert[l],
                                 b_route_expert[l], w_gate[l], w_up[l], w_down[l])
    return rmsnorm(x, final_g)


HG_HEADS = 8
HG_DK = 128
HG_DV = 128
HG_WIDTH = HG_HEADS * HG_DK
HG_VWIDTH = HG_HEADS * HG_DV
HG_CHUNK = 64
NSA_HEADS = 16
NSA_KV = 4
NSA_GROUP = NSA_HEADS // NSA_KV
NSA_DH = 64
NSA_WIDTH = NSA_HEADS * NSA_DH
NSA_KVW = NSA_KV * NSA_DH
CMP_LEN = 32
CMP_STRIDE = 16
CMP_HIDDEN = 256
SEL_BLOCK = 64
SEL_TOPK = 16
WINDOW = 512
Q_BLOCK_2 = 64
ROPE_THETA = 500000.0
ROPE_DIM = NSA_DH // 4
D_FF = 4 * D_MODEL
PLE_DIM = 256
NEG = -1e30

IN_SIZES = [HG_WIDTH, HG_WIDTH, HG_VWIDTH, HG_VWIDTH,
            NSA_WIDTH, 6 * NSA_KVW, 3 * NSA_HEADS,
            D_MODEL, D_MODEL]
N_IN = int(sum(IN_SIZES))
SPLIT_POINTS = [int(v) for v in np.cumsum(IN_SIZES)[:-1]]


def rms_norm(x, w):
    xf = x.astype(jnp.float32)
    y = xf * lax.rsqrt(jnp.mean(xf * xf, axis=-1, keepdims=True) + EPS)
    return y.astype(x.dtype) * w

def masked_softmax(s, mask):
    s = jnp.where(mask, s.astype(jnp.float32), NEG)
    pr = jax.nn.softmax(s, axis=-1)
    return jnp.where(mask, pr, 0.0)

def rope_tables(T):
    half = ROPE_DIM // 2
    inv = jnp.asarray(ROPE_THETA ** (-np.arange(half) * 2.0 / ROPE_DIM), jnp.float32)
    ang = jnp.arange(T, dtype=jnp.float32)[:, None] * inv[None, :]
    return jnp.cos(ang), jnp.sin(ang)

def apply_partial_rope(x, cos, sin):
    half = ROPE_DIM // 2
    extra = x.ndim - 3
    shp = (cos.shape[0],) + (1,) * extra + (half,)
    c = cos.reshape(shp).astype(x.dtype)
    s = sin.reshape(shp).astype(x.dtype)
    x1 = x[..., :half]
    x2 = x[..., half:ROPE_DIM]
    rest = x[..., ROPE_DIM:]
    return jnp.concatenate([x1 * c - x2 * s, x2 * c + x1 * s, rest], axis=-1)

def hgrn2_mixer(q, f_pre, i_in, g, lb, gnorm_w):
    B, T, _ = q.shape
    n = T // HG_CHUNK
    f32 = jnp.float32
    qf = jax.nn.silu(q.astype(f32)) * (HG_DK ** -0.5)
    forget = lb + (1.0 - lb) * jax.nn.sigmoid(f_pre.astype(f32))
    k = 1.0 - forget
    logf = jnp.log(forget)

    def heads(t, d):
        return t.reshape(B, n, HG_CHUNK, HG_HEADS, d).transpose(1, 0, 3, 2, 4)

    qc, kc, lc = heads(qf, HG_DK), heads(k, HG_DK), heads(logf, HG_DK)
    vc = heads(i_in.astype(f32), HG_DV)
    causal = jnp.tril(jnp.ones((HG_CHUNK, HG_CHUNK), dtype=bool))

    def step(S, inp):
        qj, kj, vj, lj = inp
        b = jnp.cumsum(lj, axis=2)
        o_inter = jnp.einsum('bhtk,bhkv->bhtv', qj * jnp.exp(b), S)
        rel = b[:, :, :, None, :] - b[:, :, None, :, :]
        decay = jnp.exp(jnp.where(causal[:, :, None], rel, -jnp.inf))
        A = jnp.einsum('bhtk,bhsk,bhtsk->bhts', qj, kj, decay)
        o = o_inter + jnp.einsum('bhts,bhsv->bhtv', A, vj)
        b_last = b[:, :, -1:, :]
        S = jnp.exp(b_last[:, :, 0, :, None]) * S + jnp.einsum(
            'bhsk,bhsv->bhkv', kj * jnp.exp(b_last - b), vj)
        return S, o

    S0 = jnp.zeros((B, HG_HEADS, HG_DK, HG_DV), f32)
    _, o = lax.scan(step, S0, (qc, kc, vc, lc))
    o = o.transpose(1, 0, 3, 2, 4).reshape(B, T, HG_HEADS, HG_DV)
    gh = g.astype(f32).reshape(B, T, HG_HEADS, HG_DV)
    o = rms_norm(o, gnorm_w.astype(f32)) * jax.nn.silu(gh)
    return o.reshape(B, T, HG_VWIDTH).astype(q.dtype)

def nsa_mixer(q, kc, vc, ks, vs, kw, vw, gates, pe_k, pe_v, wk1, wk2, wv1, wv2):
    B, T, _ = q.shape
    G, R, Dh = NSA_KV, NSA_GROUP, NSA_DH
    scale = Dh ** -0.5
    cos, sin = rope_tables(T)
    q = q.reshape(B, T, G, R, Dh) * scale
    q_rot = apply_partial_rope(q, cos, sin)
    kvh = lambda t: t.reshape(B, T, G, Dh)
    ks = apply_partial_rope(kvh(ks), cos, sin)
    kw = apply_partial_rope(kvh(kw), cos, sin)

    n_cmp = (T - CMP_LEN) // CMP_STRIDE + 1
    blk_idx = np.arange(n_cmp)[:, None] * CMP_STRIDE + np.arange(CMP_LEN)[None, :]
    cmp_end = blk_idx[:, -1]

    def compress(t, pe, w1, w2):
        blocks = kvh(t)[:, blk_idx] + pe[:, None, :]
        flat = blocks.transpose(0, 1, 3, 2, 4).reshape(B, n_cmp, G, CMP_LEN * Dh)
        out = jax.nn.gelu(flat @ w1) @ w2
        return out.transpose(0, 2, 1, 3)

    k_cmp = compress(kc, pe_k, wk1, wk2)
    v_cmp = compress(vc, pe_v, wv1, wv2)

    n_sel = T // SEL_BLOCK
    top = min(SEL_TOPK, n_sel)
    sel_start = np.arange(n_sel) * SEL_BLOCK
    overlap = jnp.asarray(((blk_idx[:, :1] < sel_start[None, :] + SEL_BLOCK)
                           & (cmp_end[:, None] >= sel_start[None, :])).astype(np.float32))
    ks_blocks = ks.transpose(0, 2, 1, 3).reshape(B, G, n_sel, SEL_BLOCK * Dh)
    vs_blocks = kvh(vs).transpose(0, 2, 1, 3).reshape(B, G, n_sel, SEL_BLOCK * Dh)
    sel_ids = jnp.arange(n_sel)

    pad = ((0, 0), (0, 0), (WINDOW, 0), (0, 0))
    kw_pad = jnp.pad(kw.transpose(0, 2, 1, 3), pad)
    vw_pad = jnp.pad(kvh(vw).transpose(0, 2, 1, 3), pad)

    q_all = q.transpose(0, 2, 3, 1, 4)
    qr_all = q_rot.transpose(0, 2, 3, 1, 4)

    def block(c):
        s0 = c * Q_BLOCK_2
        t_pos = s0 + jnp.arange(Q_BLOCK_2)
        qb = lax.dynamic_slice_in_dim(q_all, s0, Q_BLOCK_2, axis=3)
        qr = lax.dynamic_slice_in_dim(qr_all, s0, Q_BLOCK_2, axis=3)
        s = jnp.einsum('bgrqd,bgnd->bgrqn', qb, k_cmp)
        p_cmp = masked_softmax(s, cmp_end[None, :] <= t_pos[:, None])
        o_cmp = jnp.einsum('bgrqn,bgnd->bgrqd', p_cmp, v_cmp)
        imp = jnp.einsum('bgrqn,ns->bgqs', p_cmp, overlap)
        cur = t_pos // SEL_BLOCK
        forced = ((sel_ids[None, :] == 0) | (sel_ids[None, :] == cur[:, None])
                  | (sel_ids[None, :] == cur[:, None] - 1))
        causal_blk = sel_ids[None, :] * SEL_BLOCK <= t_pos[:, None]
        imp = jnp.where(forced, jnp.inf, imp)
        imp = jnp.where(causal_blk, imp, -jnp.inf)
        _, idx = lax.top_k(imp, top)
        flat_idx = idx.reshape(B, G, Q_BLOCK_2 * top, 1)
        kg = jnp.take_along_axis(ks_blocks, flat_idx, axis=2).reshape(
            B, G, Q_BLOCK_2, top * SEL_BLOCK, Dh)
        vg = jnp.take_along_axis(vs_blocks, flat_idx, axis=2).reshape(
            B, G, Q_BLOCK_2, top * SEL_BLOCK, Dh)
        key_pos = (idx[..., None] * SEL_BLOCK + jnp.arange(SEL_BLOCK)).reshape(
            B, G, Q_BLOCK_2, top * SEL_BLOCK)
        m_sel = (key_pos <= t_pos[None, None, :, None])[:, :, None]
        s = jnp.einsum('bgrqd,bgqkd->bgrqk', qr, kg)
        o_sel = jnp.einsum('bgrqk,bgqkd->bgrqd', masked_softmax(s, m_sel), vg)
        kwb = lax.dynamic_slice_in_dim(kw_pad, s0, WINDOW + Q_BLOCK_2, axis=2)
        vwb = lax.dynamic_slice_in_dim(vw_pad, s0, WINDOW + Q_BLOCK_2, axis=2)
        wpos = s0 - WINDOW + jnp.arange(WINDOW + Q_BLOCK_2)
        diff = t_pos[:, None] - wpos[None, :]
        m_win = (diff >= 0) & (diff < WINDOW) & (wpos[None, :] >= 0)
        s = jnp.einsum('bgrqd,bgkd->bgrqk', qr, kwb)
        o_win = jnp.einsum('bgrqk,bgkd->bgrqd', masked_softmax(s, m_win), vwb)
        return o_cmp, o_sel, o_win

    o_cmp, o_sel, o_win = lax.map(block, jnp.arange(T // Q_BLOCK_2))
    to_bthd = lambda o: o.transpose(1, 0, 4, 2, 3, 5).reshape(B, T, NSA_HEADS, Dh)
    gt = jax.nn.sigmoid(gates.astype(jnp.float32)).reshape(B, T, 3, NSA_HEADS, 1)
    out = (gt[:, :, 0] * to_bthd(o_cmp) + gt[:, :, 1] * to_bthd(o_sel)
           + gt[:, :, 2] * to_bthd(o_win))
    return out.reshape(B, T, NSA_WIDTH).astype(q.dtype)

def second_inputs(seed: int = 0) -> dict:
    key = jax.random.key(seed)
    k = jax.random.split(key, 24)
    f32 = jnp.float32
    nrm = lambda kk, shape, sc: jax.random.normal(kk, shape, f32) * sc
    gain = lambda kk, n: 1.0 + 0.05 * jax.random.normal(kk, (DEPTH, n), f32)
    return {
        "x": nrm(k[0], (BATCH, SEQ, D_MODEL), 1.0),
        "p": nrm(k[1], (DEPTH, BATCH, SEQ, PLE_DIM), 1.0),
        "w_in": nrm(k[2], (DEPTH, D_MODEL, N_IN), D_MODEL ** -0.5),
        "w_branch_a": nrm(k[3], (DEPTH, HG_VWIDTH, D_MODEL), HG_VWIDTH ** -0.5),
        "w_branch_b": nrm(k[4], (DEPTH, NSA_WIDTH, D_MODEL), NSA_WIDTH ** -0.5),
        "w_out": nrm(k[5], (DEPTH, D_MODEL, D_MODEL), D_MODEL ** -0.5),
        "norm_pre_mix": gain(k[6], D_MODEL),
        "norm_post_mix": gain(k[7], D_MODEL),
        "norm_pre_mlp": gain(k[8], D_MODEL),
        "norm_post_mlp": gain(k[9], D_MODEL),
        "hg_lb_logits": nrm(k[10], (DEPTH + 1, HG_WIDTH), 0.5),
        "hg_gnorm": gain(k[11], HG_DV),
        "cmp_pe_k": nrm(k[12], (DEPTH, CMP_LEN, NSA_DH), 0.1),
        "cmp_pe_v": nrm(k[13], (DEPTH, CMP_LEN, NSA_DH), 0.1),
        "cmp_wk1": nrm(k[14], (DEPTH, CMP_LEN * NSA_DH, CMP_HIDDEN), (CMP_LEN * NSA_DH) ** -0.5),
        "cmp_wk2": nrm(k[15], (DEPTH, CMP_HIDDEN, NSA_DH), CMP_HIDDEN ** -0.5),
        "cmp_wv1": nrm(k[16], (DEPTH, CMP_LEN * NSA_DH, CMP_HIDDEN), (CMP_LEN * NSA_DH) ** -0.5),
        "cmp_wv2": nrm(k[17], (DEPTH, CMP_HIDDEN, NSA_DH), CMP_HIDDEN ** -0.5),
        "w_up": nrm(k[18], (DEPTH, D_MODEL, D_FF), D_MODEL ** -0.5),
        "w_down": nrm(k[19], (DEPTH, D_FF, D_MODEL), D_FF ** -0.5),
        "w_ple": nrm(k[20], (DEPTH, PLE_DIM, D_MODEL), PLE_DIM ** -0.5),
        "w_ple_gate": nrm(k[21], (DEPTH, D_MODEL, D_MODEL), D_MODEL ** -0.5),
        "norm_ple": gain(k[22], D_MODEL),
    }

def second_block(x, p, w_in, w_branch_a, w_branch_b, w_out, norm_pre_mix, norm_post_mix,
              norm_pre_mlp, norm_post_mlp, hg_lb_logits, hg_gnorm, cmp_pe_k, cmp_pe_v,
              cmp_wk1, cmp_wk2, cmp_wv1, cmp_wv2, w_up, w_down, w_ple, w_ple_gate,
              norm_ple):
    lower_bounds = jnp.cumsum(jax.nn.softmax(hg_lb_logits.astype(jnp.float32), axis=0), axis=0)
    h = x
    for i in range(DEPTH):
        u = rms_norm(h, norm_pre_mix[i])
        proj = u @ w_in[i]
        hq, hf, hi, hg, nq, nkv, ngate, ga, gb = jnp.split(proj, SPLIT_POINTS, axis=-1)
        kc, vc, ks, vs, kw, vw = jnp.split(nkv, 6, axis=-1)
        y_a = hgrn2_mixer(hq, hf, hi, hg, lower_bounds[i], hg_gnorm[i])
        y_b = nsa_mixer(nq, kc, vc, ks, vs, kw, vw, ngate, cmp_pe_k[i], cmp_pe_v[i],
                        cmp_wk1[i], cmp_wk2[i], cmp_wv1[i], cmp_wv2[i])
        merged = (jax.nn.sigmoid(ga) * (y_a @ w_branch_a[i])
                  + jax.nn.sigmoid(gb) * (y_b @ w_branch_b[i]))
        h = h + rms_norm(merged @ w_out[i], norm_post_mix[i])
        v = rms_norm(h, norm_pre_mlp[i])
        ff = jnp.square(jax.nn.relu(v @ w_up[i])) @ w_down[i]
        h = h + rms_norm(ff, norm_post_mlp[i])
        e = (p[i] @ w_ple[i]) * jax.nn.sigmoid(h @ w_ple_gate[i])
        h = h + rms_norm(e, norm_ple[i])
    return h


def setup_inputs(seed=0):
    out = dict(first_inputs(seed))
    for name, value in second_inputs(seed + 1).items():
        if name != "x":
            out[name + "_2"] = value
    return out


def reference(
    x, mem, norm_mix_g, w_in, b_forget, b_glu, w_dw, b_dw, conv_ln_g, conv_ln_b, attn_out_g,
    w_out, norm_mem_g, mem_norm_g, w_mq, w_mkv, w_mo, norm_ffn_g, w_route_group, b_route_group,
    w_route_expert, b_route_expert, w_gate, w_up, w_down, final_g, p_2, w_in_2, w_branch_a_2,
    w_branch_b_2, w_out_2, norm_pre_mix_2, norm_post_mix_2, norm_pre_mlp_2, norm_post_mlp_2,
    hg_lb_logits_2, hg_gnorm_2, cmp_pe_k_2, cmp_pe_v_2, cmp_wk1_2, cmp_wk2_2, cmp_wv1_2,
    cmp_wv2_2, w_up_2, w_down_2, w_ple_2, w_ple_gate_2, norm_ple_2,
):
    x = first_block(
        x, mem, norm_mix_g, w_in, b_forget, b_glu, w_dw, b_dw, conv_ln_g, conv_ln_b, attn_out_g,
        w_out, norm_mem_g, mem_norm_g, w_mq, w_mkv, w_mo, norm_ffn_g, w_route_group,
        b_route_group, w_route_expert, b_route_expert, w_gate, w_up, w_down, final_g,
    )
    return second_block(
        x, p_2, w_in_2, w_branch_a_2, w_branch_b_2, w_out_2, norm_pre_mix_2, norm_post_mix_2,
        norm_pre_mlp_2, norm_post_mlp_2, hg_lb_logits_2, hg_gnorm_2, cmp_pe_k_2, cmp_pe_v_2,
        cmp_wk1_2, cmp_wk2_2, cmp_wv1_2, cmp_wv2_2, w_up_2, w_down_2, w_ple_2, w_ple_gate_2,
        norm_ple_2,
    )


_drawn_inputs = setup_inputs


def setup_inputs(seed=0):
    import zlib

    import numpy as np

    out = dict(_drawn_inputs(seed))
    spreads = {}
    factors = {'b_dw': 2.804,
     'conv_ln_b': 3.82,
     'norm_mem_g': 4.055,
     'mem_norm_g': 4.771,
     'b_route_group': 21.56,
     'b_route_expert': 36.922,
     'cmp_pe_k_2': 8.0,
     'b_glu': 2.862,
     'norm_ffn_g': 8.0}
    for name, (base, spread) in spreads.items():
        noise = np.random.default_rng([zlib.crc32(name.encode()), seed]).standard_normal(out[name].shape)
        drawn = base * np.exp(spread * noise) if base else spread * noise
        out[name] = jnp.asarray(drawn.astype(out[name].dtype))
    for name, factor in factors.items():
        out[name] = (out[name] * factor).astype(out[name].dtype)
    return out
```

```python
from contextlib import ExitStack

import numpy as np
import concourse.bass as bass
from concourse import mybir

F32 = mybir.dt.float32
I32 = mybir.dt.int32
U32 = mybir.dt.uint32
ALU = mybir.AluOpType
ACT = mybir.ActivationFunctionType
AX = mybir.AxisListType

P = 128
T, D = 256, 1024
TT, KT = T // P, D // P
EPS = 1e-6
BIG = 1e30
HEADS, HEAD_DIM = 8, 64
D_ATTN = HEADS * HEAD_DIM
D_CONV = D - D_ATTN
TAPS = 31
MEM_HEADS, MEM_DIM = 4, 256
GROUPS, PER_GROUP = 4, 8
EXPERTS = GROUPS * PER_GROUP
D_EXPERT = 512
CAP = 64
PASSES = T // CAP
PAIRS = EXPERTS // 2
MORE = PAIRS * (PASSES - 1)
HG_HEADS, CHUNK = 8, 64
NSA_HEADS, NSA_KV, NSA_DH = 16, 4, 64
CMP_LEN, CMP_STRIDE = 32, 16
N_CMP = (T - CMP_LEN) // CMP_STRIDE + 1
CMP_HIDDEN = 256
ROPE_DIM, ROPE_THETA = 16, 500000.0
D_FF = 4 * D
BANKS = 8
SLOT = 4096
PAGE = 2048
HEAD_OF = [0, 2, 4, 6, 1, 3, 5, 7]
DVE_CONV = 3
LEVELS = [1, 2, 4, 8, 16, 32, 64, 128]

PARAM_ROWS = [("norm_mix_g", 8), ("norm_mem_g", 8), ("mem_norm_g", 8), ("norm_ffn_g", 8),
              ("norm_pre_mix_2", 8), ("norm_pre_mlp_2", 8), ("attn_out_g", 4), ("b_glu", 8),
              ("b_dw", 4), ("conv_ln_g", 4), ("conv_ln_b", 4), ("hg_lb_logits_2", 16),
              ("cmp_pe_k_2", 16), ("cmp_pe_v_2", 16)]


def shape_constants():
    cols, parts = {}, []

    def put(name, a):
        a = np.asarray(a, np.float32).reshape(P, -1)
        start = sum(x.shape[1] for x in parts)
        cols[name] = (start, start + a.shape[1])
        parts.append(a)

    p = np.arange(P)
    put("ident", np.eye(P))
    put("ones", np.ones((P, T)))
    put("causal", np.concatenate([np.zeros((P, P)), np.where(p[None, :] <= p[:, None], 0.0, -BIG)], 1))
    put("earlier", p[:, None] < p[None, :])
    for L in LEVELS[:-1]:
        same = p[:, None] // (2 * L) == p[None, :] // (2 * L)
        put(f"level{L}", same & (p[:, None] // L % 2 == 0) & (p[None, :] // L % 2 == 1))
    put("chunk_reset", np.tile(np.arange(T) % CHUNK != 0, (P, 1)))
    put("slots", np.tile(np.arange(T + CAP), (P, 1)))
    half = ROPE_DIM // 2
    inv = (ROPE_THETA ** (-np.arange(half) * 2.0 / ROPE_DIM)).astype(np.float32)
    angle = np.arange(T, dtype=np.float32)[:, None] * inv[None, :]
    to_half = lambda a: a.reshape(TT, P, -1).transpose(1, 0, 2)
    put("cos", to_half(np.cos(angle)))
    put("sin", to_half(np.sin(angle)))
    end = np.arange(N_CMP) * CMP_STRIDE + CMP_LEN - 1
    seen = to_half((end[None, :] <= np.arange(T)[:, None]).astype(np.float32))
    put("cmp_seen", seen)
    put("cmp_bias", (seen - 1.0) * np.float32(BIG))
    return np.concatenate(parts, 1), cols


def two_blocks_kernel(nc, d, const_cols, out):
    ctx = ExitStack()
    with ctx:
        sb = lambda name, shape, dt=F32: ctx.enter_context(nc.sbuf_tensor(name, shape, dt))
        n_const = d["consts"].shape[1]
        ring = sb("ring", [P, 6 * SLOT])
        arena = sb("arena", [P, 12 * PAGE])
        consts = sb("consts", [P, n_const])
        cols = sb("cols", [P, 256])
        small = sb("small", [P, 512])
        route_w = sb("route_w", [P, KT, 36])
        route_b = sb("route_b", [P, 36])
        forget_w = sb("forget_w", [P, KT, HEADS])
        forget_b = sb("forget_b", [HEADS, 1])
        pos = sb("pos", [P, TT, EXPERTS])
        gate = sb("gate", [P, TT, EXPERTS])
        busiest = sb("busiest", [P, 1], I32)
        ps = ctx.enter_context(nc.psum_tensor("ps", [P, BANKS, 512], F32))

        sems = {}

        def sem(name):
            if name not in sems:
                sems[name] = ctx.enter_context(nc.semaphore(name))
            return sems[name]

        for b in range(BANKS):
            sem(f"bank_filled{b}"), sem(f"bank_drained{b}")

        def page(i, start=0, size=PAGE):
            if i < 12:
                return arena[:, i * PAGE + start:i * PAGE + start + size]
            at = 3 * SLOT + (i - 12) * PAGE
            return ring[:, at + start:at + start + size]

        def grid(flat, a):
            return flat.rearrange("p (a b) -> p a b", a=a)

        def const(name):
            a, b = const_cols[name]
            return consts[:, a:b]

        ident = const("ident")
        param_col, at = {}, 0
        for name, n in PARAM_ROWS:
            param_col[name] = at
            at += n
        n_rows = at

        def col(name, k=0, n=1):
            return cols[:, param_col[name] + k:param_col[name] + k + n]

        def tap(w, cb):
            k = P + w * 4 + cb
            return cols[:, k:k + 1]

        x = grid(page(0), TT)
        normed = grid(page(1), TT)
        xT = grid(page(2), KT)
        qk1 = page(3)
        qT1, kT1 = grid(qk1[:, 0:1024], 4), grid(qk1[:, 1024:2048], 4)
        memT = grid(page(11), KT)
        mem_k, mem_v = grid(page(4), KT), grid(page(5), TT)
        mem_tok = grid(page(9), TT)
        mem_normed = grid(page(10), TT)
        v1 = grid(page(6, 0, 1024), TT)
        glu = grid(page(6, 1024, 1024), 4)
        ZW = TAPS - 1 + T
        z = grid(page(7, 0, 4 * ZW), 4)
        attn1 = grid(page(8, 1024, 1024), TT)
        conv = grid(page(8, 0, 1024), 4)
        catT = grid(page(2), KT)
        decay = page(7, 4 * ZW, 512)
        log_f, key_bias = decay[0:HEADS, 0:256], decay[0:HEADS, 256:512]
        qT2 = grid(page(3), KT)
        prob2 = page(6).rearrange("p (t h m) -> p t h m", t=TT, h=MEM_HEADS)
        prob2T = page(7).rearrange("p (h m q) -> p h m q", h=MEM_HEADS, m=TT)
        oT2 = grid(page(8), KT)
        logits = grid(page(6, 0, 72), TT)
        scratch_route = page(6, 128, 1920)
        picked = grid(page(3, 0, 1024), KT)
        choose = grid(page(3, 1024, 256), TT)
        choose_gated = grid(page(3, 1280, 256), TT)
        spread = page(3, 1536, 256)
        hidden = page(4, 0, D_EXPERT)
        hiddenT = grid(page(4, 512, 512), 4)
        expert_out = page(4, 1024, 1024)
        hq, hb, hk = page(3), page(4), page(5)
        hx = [page(6), page(7)]
        scores_diag, scores_cross = page(8), page(9, 0, 1024)
        hv, hg = grid(page(10), TT), grid(page(11), TT)
        gnorm = page(9, 1024, 128)
        w_gates = page(9, 1152, KT * 48).rearrange("p (k n) -> p k n", k=KT)
        sel_gates = grid(page(9, 1536, 96), TT)
        nq, nq_rot = grid(page(12), TT), grid(page(13), TT)
        nkv = ring[:, 3 * SLOT + 2 * PAGE:3 * SLOT + 2 * PAGE + TT * 1536].rearrange("p (t n) -> p t n", t=TT)
        mix_a, mix_b = grid(page(16), TT), grid(page(17), TT)
        nqT, nq_rotT = grid(page(3), KT), grid(page(4), KT)
        ksT, kwT = grid(page(5, 0, 1024), 4), grid(page(5, 1024, 1024), 4)
        kc2, vc2 = grid(page(10, 0, 1024), 4), grid(page(10, 1024, 1024), 4)
        y_b = grid(page(1), TT)
        y_aT = grid(page(11), KT)
        y_bT = grid(page(2), KT)
        cmp_p = page(9, 0, 1024).rearrange("p (t h n) -> p t h n", t=TT, h=NSA_HEADS)
        cmp_pT = page(13, 0, 1024).rearrange("p (t g q) -> p t g q", t=TT, g=NSA_KV)
        CMP = page(15)
        cmp_wk2 = CMP[:, 1024:1280].rearrange("p (c u n) -> p c u n", c=2, u=2)
        cmp_wv2 = CMP[:, 1280:1408].rearrange("p (c n) -> p c n", c=2)
        cmp_hid = CMP[:, 1408:1648].rearrange("p (s c n) -> p s c n", s=2, c=2)
        cmp_kT = CMP[:, 1648:1708]
        cmp_pe = CMP[:, 1708:1712]
        cmp_sum = CMP[:, 1712:1776]
        cmp_v = page(13, 1024, 1024).rearrange("p (g n) -> p g n", g=NSA_KV)
        ffT = [grid(page(3 + n), KT) for n in range(4)]
        mlp_out = grid(page(7), TT)
        p_tok = grid(page(8, 0, 512), TT)
        pT = grid(page(8, 512, 512), TT)
        ple = grid(page(9), TT)
        ple_gate = grid(page(10), TT)
        gain_final, gain_mix = page(5, 0, 1024), page(12, 0, 1024)
        gain_mlp, gain_ple = page(12, 1024, 1024), page(13, 0, 1024)

        rows = lambda w, k: w.rearrange("(k p) n -> p k n", k=k)
        units, unit_at = [], {}

        def unit(name, src, k, n, n_slots):
            slot = len(units) % n_slots if n_slots == 6 else (len(units) - first_late) % 3
            unit_at[name] = (len(units), slot, k, n)
            units.append((name, src, slot, k, n))

        off_c = 3 * D_ATTN + HEADS
        for name, start in (("conv_g", off_c + D_CONV), ("conv_a", off_c), ("q", 0), ("k", D_ATTN), ("v", 2 * D_ATTN)):
            unit(name, rows(d["w_in"][0], KT)[:, :, start:start + 512], KT, 512, 6)
        for c in range(4):
            unit(f"mem_kv{c}", rows(d["w_mkv"][0], KT)[:, :, c * 512:c * 512 + 512], KT, 512, 6)
        for key, w in (("out", "w_out"), ("mem_q", "w_mq"), ("mem_o", "w_mo")):
            for c in range(2):
                unit(f"{key}{c}", rows(d[w][0], KT)[:, :, c * 512:c * 512 + 512], KT, 512, 6)
        n_early = len(units)
        expert_slot = [(n_early + n) % 6 for n in range(6)]
        first_late = n_early
        off = [0, 512, 1024, 1536, 2048, 2560, 3072, 3584, 4096, 4608, 5120, 5632, 6144, 6704, 7216, 7728, 8240]
        names2 = ["hq0", "hq1", "hf0", "hf1", "hi0", "hi1", "hg0", "hg1", "nq0", "nq1",
                  "kv0", "kv1", "kv2", "ga0", "ga1", "gb0", "gb1"]
        for name, start in zip(names2, off):
            unit(name, rows(d["w_in_2"][0], KT)[:, :, start:start + 512], KT, 512, 3)
        for c in range(2):
            unit(f"branch_a{c}", rows(d["w_branch_a_2"][0], KT)[:, :, c * 512:c * 512 + 512], KT, 512, 3)
        for c in "kv":
            unit(f"cmp_{c}", rows(d[f"cmp_w{c}1_2"][0], 16), 16, CMP_HIDDEN, 3)
        for key, w in (("branch_b", "w_branch_b_2"), ("out2_", "w_out_2")):
            for c in range(2):
                unit(f"{key}{c}", rows(d[w][0], KT)[:, :, c * 512:c * 512 + 512], KT, 512, 3)
        for c in range(8):
            unit(f"up{c}", rows(d["w_up_2"][0], KT)[:, :, c * 512:c * 512 + 512], KT, 512, 3)
        for c in range(2):
            for k in range(4):
                unit(f"down{c}{k}", rows(d["w_down_2"][0][k * D:k * D + D], KT)[:, :, c * 512:c * 512 + 512], KT, 512, 3)
        unit("ple", rows(d["w_ple_2"][0], 2), 2, D, 3)
        for c in range(2):
            unit(f"ple_gate{c}", rows(d["w_ple_gate_2"][0], KT)[:, :, c * 512:c * 512 + 512], KT, 512, 3)

        landed_value, loads = {}, [0] * 6
        for n, (name, _, slot, _, _) in enumerate(units):
            if n == n_early:
                before_experts = list(loads)
                loads = [v + 16 * PAIRS for v in loads]
            loads[slot] += 16
            landed_value[name] = loads[slot]

        def slot_view(slot, k, n):
            return ring[:, slot * SLOT:slot * SLOT + k * n].rearrange("p (k n) -> p k n", k=k)

        expert_w = [slot_view(expert_slot[n], *((KT, 512) if n < 4 else (4, 1024))) for n in range(6)]

        fills, unit_last_fill = {}, {}

        def filled_by(eng, name):
            n = fills[name]
            eng.wait_ge(sem(f"bank_filled{n % BANKS}"), n // BANKS + 1)
            return ps[:, n % BANKS, :]

        def drained_by(eng, *names):
            for name in names:
                n = fills[name]
                eng.wait_ge(sem(f"bank_drained{n % BANKS}"), n // BANKS + 1)

        blocks1 = [dict(name=f"fa{t}", t=t, nk=P * (t + 1), n=t, scale=HEAD_DIM ** -0.5,
                        p=page(9 + t, 0, HEADS * P * (t + 1)).rearrange("p (h k) -> p h k", h=HEADS),
                        pt=(page(9, 1024, 1024) if t == 0 else page(1)).rearrange("p (n q) -> p n q", q=P),
                        q=lambda h, t=t: qT1[64 * (h % 2):64 * (h % 2) + 64, h // 2, t * P:t * P + P],
                        k=lambda h, nk: kT1[64 * (h % 2):64 * (h % 2) + 64, h // 2, 0:nk],
                        v=lambda h, j: v1[:, j, h * 64:h * 64 + 64], bias=True) for t in range(TT)]
        blocks2 = []
        for branch, (kT, v0) in enumerate(((ksT, 768), (kwT, 1280))):
            for t in range(TT):
                for half in range(2):
                    n = len(blocks2)
                    blocks2.append(dict(
                        name=f"nsa{branch}{t}{half}", t=t, nk=P * (t + 1), n=2 + n, scale=1.0, branch=branch, half=half,
                        p=page((6, 7)[n % 2], 0, HEADS * P * (t + 1)).rearrange("p (h k) -> p h k", h=HEADS),
                        pt=page((8, 12)[n % 2], 0, HEADS * P * (t + 1)).rearrange("p (n q) -> p n q", q=P),
                        q=lambda h, t=t, half=half: nq_rotT[64 * (h % 2):64 * (h % 2) + 64, 4 * half + h // 2, t * P:t * P + P],
                        k=lambda h, nk, kT=kT, half=half: kT[64 * (h % 2):64 * (h % 2) + 64, 2 * half + h // 4, 0:nk],
                        v=lambda h, j, v0=v0, half=half: nkv[:, j, v0 + (2 * half + h // 4) * 64:v0 + (2 * half + h // 4) * 64 + 64],
                        bias=False))

        def stat(k, n):
            return small[:, k:k + n]

        def block_stats(blk):
            return [stat(64 + 24 * blk["n"] + 8 * j, 8) for j in range(3)]

        with nc.Block() as block:

            @block.tensor
            def _(pe):
                def open_bank(name):
                    n = fills[name] = len(fills)
                    if n >= BANKS:
                        pe.wait_ge(sem(f"bank_drained{n % BANKS}"), n // BANKS)
                    return ps[:, n % BANKS, :]

                def close_bank(ins, name):
                    ins.then_inc(sem(f"bank_filled{fills[name] % BANKS}"), 1)

                def use(name):
                    _, slot, k, n = unit_at[name]
                    pe.wait_ge(sem(f"weights_landed{slot}"), landed_value[name])
                    return slot_view(slot, k, n)

                def feature_major(name, tag, rhs):
                    w = use(name)
                    for c in range(2):
                        bank = open_bank(f"{tag}{c}")
                        for half in range(2):
                            at = (2 * c + half) * P
                            for k in range(KT):
                                mm = nc.tensor.matmul(bank[:, half * T:half * T + T], w[:, k, at:at + P], rhs[:, k, :],
                                                      start=k == 0, stop=k == KT - 1)
                        close_bank(mm, f"{tag}{c}")
                    unit_last_fill[name] = f"{tag}1"

                def token_major(name, tag, lhs):
                    w = use(name)
                    for t in range(TT):
                        bank = open_bank(f"{tag}{t}")
                        for k in range(KT):
                            mm = nc.tensor.matmul(bank, lhs[:, k, t * P:t * P + P], w[:, k, :],
                                                  start=k == 0, stop=k == KT - 1)
                        close_bank(mm, f"{tag}{t}")
                    unit_last_fill[name] = f"{tag}1"

                def transposes(tag, src):
                    for j in range(4):
                        bank = open_bank(f"{tag}{j}")
                        for k in (2 * j, 2 * j + 1):
                            for t in range(TT):
                                at = (k % 2) * T + t * P
                                mm = nc.tensor.transpose(bank[:, at:at + P], src[:, t, k * P:k * P + P], ident)
                        close_bank(mm, f"{tag}{j}")

                def scores(blk):
                    nk = blk["nk"]
                    per = 512 // nk
                    for f in range(HEADS // per):
                        name = f"{blk['name']}S{f}"
                        bank = open_bank(name)
                        for j in range(per):
                            h = HEAD_OF[f * per + j]
                            o = bank[:, j * nk:j * nk + nk]
                            mm = nc.tensor.matmul(o, blk["q"](h), blk["k"](h, nk), start=True, stop=not blk["bias"])
                            if blk["bias"]:
                                mm = nc.tensor.matmul(o, ident[0:HEADS, h:h + 1].to_broadcast([HEADS, P]),
                                                      key_bias[:, 0:nk], start=False, stop=True)
                        close_bank(mm, name)

                def turn_probs(blk):
                    pe.wait_ge(sem("probs_ready"), blk["n"] + 1)
                    tiles = HEADS * blk["nk"] // P
                    flat = blk["p"].rearrange("p h (j k) -> p (h j) k", k=P)
                    for f in range(tiles // 4):
                        name = f"{blk['name']}T{f}"
                        bank = open_bank(name)
                        for j in range(4):
                            mm = nc.tensor.transpose(bank[:, j * P:j * P + P], flat[:, 4 * f + j, :], ident)
                        close_bank(mm, name)

                def weigh_values(blk):
                    nj = blk["nk"] // P
                    drained_by(pe, *[f"{blk['name']}T{f}" for f in range(HEADS * nj // 4)])
                    bank = open_bank(f"{blk['name']}O")
                    for n, h in enumerate(HEAD_OF):
                        for j in range(nj):
                            mm = nc.tensor.matmul(bank[:, h * 64:h * 64 + 64], blk["pt"][:, n * nj + j, :], blk["v"](h, j),
                                                  start=j == 0, stop=j == nj - 1)
                    close_bank(mm, f"{blk['name']}O")

                def attend(blks):
                    for i in range(len(blks) + 2):
                        if i < len(blks):
                            scores(blks[i])
                        if 1 <= i <= len(blks):
                            turn_probs(blks[i - 1])
                        if i >= 2:
                            weigh_values(blks[i - 2])

                pe.wait_ge(sem("consts_landed"), 16)
                pe.wait_ge(sem("params_landed"), 16 * (len(PARAM_ROWS) + 1))
                bank = open_bank("params")
                nc.tensor.transpose(bank[:, 0:n_rows], page(8, 0, P)[0:n_rows, :], ident[0:n_rows, 0:n_rows])
                close_bank(nc.tensor.transpose(bank[:, P:P + 4 * TAPS], page(8, P, P)[0:4 * TAPS, :],
                                               ident[0:4 * TAPS, 0:4 * TAPS]), "params")
                pe.wait_ge(sem("x_normed"), 2)
                transposes("mixT", normed)
                drained_by(pe, *[f"mixT{j}" for j in range(4)])
                feature_major("conv_g", "conv_g", xT)
                feature_major("conv_a", "conv_a", xT)
                feature_major("q", "q", xT)
                feature_major("k", "k", xT)
                pe.wait_ge(sem("forget_landed"), 32)
                bank = open_bank("forget")
                for k in range(KT):
                    mm = nc.tensor.matmul(bank[0:HEADS, 0:T], forget_w[:, k, :], xT[:, k, :], start=k == 0, stop=k == KT - 1)
                close_bank(mm, "forget")
                token_major("v", "v", xT)
                pe.wait_ge(sem("mem_normed"), 2)
                transposes("memT", mem_normed)
                drained_by(pe, *[f"memT{j}" for j in range(4)])
                for c in range(2):
                    feature_major(f"mem_kv{c}", f"mem_k{c}", memT)
                pe.wait_ge(sem("key_bias_ready"), 1)
                drained_by(pe, "q0", "q1", "k0", "k1", "v0", "v1")
                for blk in blocks1:
                    scores(blk)
                token_major("mem_kv2", "mem_v0", memT)
                for blk in blocks1:
                    turn_probs(blk)
                def channel_sums(name, src):
                    bank = open_bank(name)
                    for cb in range(4):
                        mm = nc.tensor.matmul(bank[:, 0:T], const("ones")[:, 0:P], src[:, cb, :], start=cb == 0, stop=cb == 3)
                    close_bank(mm, name)

                pe.wait_ge(sem("conv_ready"), 1)
                pe.wait_ge(sem("conv_pool_ready"), 1)
                channel_sums("conv_mean", conv)
                for blk in blocks1:
                    weigh_values(blk)
                pe.wait_ge(sem("conv_ready"), 2)
                channel_sums("conv_var", glu)
                token_major("mem_kv3", "mem_v1", memT)
                for t in range(TT):
                    pe.wait_ge(sem("attn1_normed"), t + 1)
                    bank = open_bank(f"attn1T{t}")
                    for k in range(4):
                        mm = nc.tensor.transpose(bank[:, k * P:k * P + P], attn1[:, t, k * P:k * P + P], ident)
                    close_bank(mm, f"attn1T{t}")
                drained_by(pe, "attn1T0", "attn1T1")
                pe.wait_ge(sem("conv_done"), 4)
                for c in range(2):
                    token_major(f"out{c}", f"out{c}", catT)
                pe.wait_ge(sem("x_normed"), 4)
                transposes("crossT", normed)
                drained_by(pe, *[f"crossT{j}" for j in range(4)])
                for c in range(2):
                    feature_major(f"mem_q{c}", f"mem_q{c}", xT)
                drained_by(pe, "mem_q00", "mem_q01", "mem_q10", "mem_q11")
                for t in range(TT):
                    for f in range(2):
                        bank = open_bank(f"crossS{t}{f}")
                        for j in range(2):
                            h = 2 * f + j
                            for c in range(2):
                                mm = nc.tensor.matmul(bank[:, j * T:j * T + T], qT2[:, 2 * h + c, t * P:t * P + P],
                                                      mem_k[:, 2 * h + c, :], start=c == 0, stop=c == 1)
                        close_bank(mm, f"crossS{t}{f}")
                for t in range(TT):
                    pe.wait_ge(sem("cross_probs_ready"), t + 1)
                    for f in range(2):
                        bank = open_bank(f"crossT{t}{f}")
                        for j in range(4):
                            h, m = 2 * f + j // 2, j % 2
                            mm = nc.tensor.transpose(bank[:, j * P:j * P + P], prob2[:, t, h, m * P:m * P + P], ident)
                        close_bank(mm, f"crossT{t}{f}")
                drained_by(pe, "crossT00", "crossT01", "crossT10", "crossT11")
                for f in range(4):
                    bank = open_bank(f"crossO{f}")
                    for c in range(2):
                        for m in range(TT):
                            mm = nc.tensor.matmul(bank[:, c * T:c * T + T], mem_v[:, m, (2 * f + c) * P:(2 * f + c) * P + P],
                                                  prob2T[:, f, m, :], start=m == 0, stop=m == TT - 1)
                    close_bank(mm, f"crossO{f}")
                drained_by(pe, *[f"crossO{f}" for f in range(4)])
                for c in range(2):
                    token_major(f"mem_o{c}", f"mem_o{c}", oT2)
                pe.wait_ge(sem("x_normed"), 6)
                transposes("ffnT", normed)
                drained_by(pe, *[f"ffnT{j}" for j in range(4)])
                pe.wait_ge(sem("route_landed"), 16 * (GROUPS + 3))
                bank = open_bank("route")
                for t in range(TT):
                    for k in range(KT):
                        mm = nc.tensor.matmul(bank[:, t * 36:t * 36 + 36], xT[:, k, t * P:t * P + P], route_w[:, k, :],
                                              start=k == 0, stop=k == KT - 1)
                close_bank(mm, "route")
                pe.wait_ge(sem("choice_ready"), 1)
                chosen = grid(scratch_route[:, 0:64], TT)
                bank = open_bank("rank")
                ones = const("ones")[:, 0:P]
                nc.tensor.matmul(bank[:, 0:32], const("earlier"), chosen[:, 0, :], start=True, stop=True)
                nc.tensor.matmul(bank[:, 32:64], const("earlier"), chosen[:, 1, :], start=True, stop=False)
                nc.tensor.matmul(bank[:, 32:64], ones, chosen[:, 0, :], start=False, stop=True)
                nc.tensor.matmul(bank[:, 64:96], ones, chosen[:, 0, :], start=True, stop=False)
                close_bank(nc.tensor.matmul(bank[:, 64:96], ones, chosen[:, 1, :], start=False, stop=True), "rank")

                def experts(tag, n_pairs, landed_sems, landed_base):
                    s = lambda name: sem(f"{tag}_{name}")

                    def gather(n, first=False):
                        pe.wait_ge(s("choose_ready"), n + 1)
                        for f, b in ((0, 0), (1, 7)):
                            if not first:
                                pe.wait_ge(s("picked_drained"), 2 * n - 1 + f)
                            for k in range(4 * f, 4 * f + 4):
                                for t in range(TT):
                                    mm = nc.tensor.matmul(ps[:, b, (k % 4) * P:(k % 4) * P + P], normed[:, t, k * P:k * P + P],
                                                          choose[:, t, :], start=t == 0, stop=t == TT - 1)
                            mm.then_inc(s("picked_filled"), 1)

                    def product(n, first, tiles, name):
                        for e in range(2):
                            slot = expert_slot[first + e]
                            pe.wait_ge(landed_sems[slot], landed_base[slot] + (n + 1) * 16)
                        w, src = expert_w[first:first + 2], hiddenT if first == 4 else picked
                        n_k = src.shape[1]
                        for c, bank in enumerate(tiles):
                            for k in range(n_k):
                                for e in range(2):
                                    mm = nc.tensor.matmul(ps[e * CAP:e * CAP + CAP, bank, :], src[:, k, e * CAP:e * CAP + CAP],
                                                          w[e][:, k, c * 512:c * 512 + 512], start=k == 0, stop=k == n_k - 1)
                                    if c == len(tiles) - 1 and k == n_k - 1:
                                        mm.then_inc(s(name), 1)

                    def scatter(n):
                        pe.wait_ge(s("spread_ready"), n + 1)
                        pe.wait_ge(s("out_ready"), 2 * n + 2)
                        for t in range(TT):
                            for c in range(2):
                                if t:
                                    pe.wait_ge(s("sum_drained"), 4 * n + c + 1)
                                nc.tensor.matmul(ps[:, 5 + c, :], spread[:, t * P:t * P + P],
                                                 expert_out[:, c * 512:c * 512 + 512], start=True, stop=True).then_inc(s("sum_filled"), 1)

                    gather(0, first=True)
                    with pe.Fori(0, n_pairs) as n:
                        pe.wait_ge(s("picked_drained"), 2 * n + 2)
                        product(n, 0, [1], "gate_filled")
                        scatter(n)
                        product(n, 2, [2], "up_filled")
                        gather(n + 1)
                        pe.wait_ge(s("hidden_ready"), n + 1)
                        for k in range(4):
                            mm = nc.tensor.transpose(ps[:, 1, k * P:k * P + P], hidden[:, k * P:k * P + P], ident)
                        mm.then_inc(s("hidden_turned"), 1)
                        pe.wait_ge(s("gated_choose_ready"), n + 1)
                        pe.wait_ge(s("sum_drained"), 4 * n + 4)
                        for t in range(TT):
                            mm = nc.tensor.transpose(ps[:, 5, t * P:t * P + P], choose_gated[:, t, :], ident)
                        mm.then_inc(s("spread_filled"), 1)
                        pe.wait_ge(s("hiddenT_ready"), n + 1)
                        product(n, 4, [3, 4], "down_filled")
                    scatter(n_pairs)
                    pe.wait_ge(s("sum_drained"), 4 * n_pairs + 4)

                for b in range(BANKS):
                    pe.wait_ge(sem(f"bank_drained{b}"), len([v for v in fills.values() if v % BANKS == b]))
                landed = [sem(f"weights_landed{b}") for b in range(6)]
                experts("moe", PAIRS, landed, before_experts)
                pe.wait_ge(sem("busiest_ready"), 1)
                count = pe.value_load(busiest[0:1, 0:1], min_val=0, max_val=T)
                with pe.If(count > CAP):
                    experts("more", MORE, [sem(f"more_landed{b}") for b in range(6)], [0] * 6)

                pe.wait_ge(sem("x_normed"), 8)
                transposes("mix2T", normed)
                drained_by(pe, *[f"mix2T{j}" for j in range(4)])
                for c in range(2):
                    feature_major(f"hq{c}", f"hq{c}", xT)
                for c in range(2):
                    feature_major(f"hf{c}", f"hf{c}", xT)
                for c in range(2):
                    token_major(f"hi{c}", f"hi{c}", xT)
                for c in range(2):
                    token_major(f"hg{c}", f"hg{c}", xT)

                def level(n):
                    pe.wait_ge(sem("level_ready"), n + 1)
                    if n and LEVELS[n - 1] == P:
                        src = grid(hx[n % 2], HG_HEADS)
                        for f in range(2):
                            bank = open_bank(f"level{n}_{f}")
                            for j in range(4):
                                h = 4 * f + j
                                mm = nc.tensor.matmul(bank[:, j * P:j * P + P], src[:, h, 0:P], src[:, h, P:T], start=True, stop=True)
                            close_bank(mm, f"level{n}_{f}")
                        return
                    left, right = (grid(hk, HG_HEADS), grid(hq, HG_HEADS)) if n == 0 else [grid(hx[n % 2], HG_HEADS)] * 2
                    for f in range(4):
                        bank = open_bank(f"level{n}_{f}")
                        for j in range(4):
                            h, t = 2 * f + j // 2, j % 2
                            mm = nc.tensor.matmul(bank[:, j * P:j * P + P], left[:, h, t * P:t * P + P], right[:, h, t * P:t * P + P],
                                                  start=True, stop=True)
                        close_bank(mm, f"level{n}_{f}")

                late = ["nq0", "nq1", "kv0", "kv1", "kv2", "ga0", "ga1", "gb0", "gb1"]
                for n in range(len(LEVELS) + 1):
                    token_major(late[n], late[n], xT)
                    if n == 2:
                        pe.wait_ge(sem("gates_landed"), 16)
                        bank = open_bank("sel_gates")
                        for t in range(TT):
                            for k in range(KT):
                                mm = nc.tensor.matmul(bank[:, t * 48:t * 48 + 48], xT[:, k, t * P:t * P + P], w_gates[:, k, :],
                                                      start=k == 0, stop=k == KT - 1)
                        close_bank(mm, "sel_gates")
                    level(n)
                drained_by(pe, *[f"level{len(LEVELS)}_{f}" for f in range(2)])
                drained_by(pe, *[f"hi{c}{t}" for c in range(2) for t in range(TT)])
                diag = scores_diag.rearrange("p (h t q) -> p h t q", h=HG_HEADS, t=TT)
                cross = grid(scores_cross, HG_HEADS)
                for t in range(TT):
                    for f in range(2):
                        bank = open_bank(f"rec{t}{f}")
                        for j in range(4):
                            h = 4 * f + j
                            o = bank[:, j * P:j * P + P]
                            mm = nc.tensor.matmul(o, diag[:, h, t, :], hv[:, t, h * P:h * P + P], start=True, stop=t == 0)
                            if t:
                                mm = nc.tensor.matmul(o, cross[:, h, :], hv[:, 0, h * P:h * P + P], start=False, stop=True)
                        close_bank(mm, f"rec{t}{f}")
                pe.wait_ge(sem("nq_ready"), 1)
                transposes("nqT", nq)
                pe.wait_ge(sem("rotated"), 3 * TT)
                transposes("nq_rotT", nq_rot)
                for key, start in (("kc", 0), ("vc", 256), ("ks", 512), ("kw", 1024)):
                    for f in range(2):
                        bank = open_bank(f"{key}T{f}")
                        for j in range(2):
                            g = 2 * f + j
                            for t in range(TT):
                                for u in range(2):
                                    mm = nc.tensor.matmul(bank[64 * u:64 * u + 64, j * T + t * P:j * T + t * P + P],
                                                          nkv[:, t, start + g * 64:start + g * 64 + 64], ident, start=True, stop=True)
                        close_bank(mm, f"{key}T{f}")
                pe.wait_ge(sem("y_a_ready"), 1)
                transposes("y_aT", normed)
                drained_by(pe, *[f"y_aT{j}" for j in range(4)])
                for c in range(2):
                    token_major(f"branch_a{c}", f"branch_a{c}", y_aT)
                drained_by(pe, "kcT0", "kcT1", "vcT0", "vcT1")
                pe.wait_ge(sem("cmp_w2_landed"), 48)
                for s, (key, src) in enumerate((("k", kc2), ("v", vc2))):
                    w = use(f"cmp_{key}")
                    bank = open_bank(f"cmp_hid_{key}")
                    for c in range(2):
                        for j in range(CMP_LEN // 2):
                            mm = nc.tensor.matmul(bank[:, c * 64:c * 64 + 4 * N_CMP], w[:, j, c * P:c * P + P],
                                                  src[:, :, 2 * j:2 * j + CMP_STRIDE * (N_CMP - 1) + 1:CMP_STRIDE],
                                                  start=j == 0, stop=j == CMP_LEN // 2 - 1)
                        for j in range(CMP_LEN // 2):
                            mm = nc.tensor.matmul(bank[:, 128 + c:129 + c], w[:, j, c * P:c * P + P], col(f"cmp_pe_{key}_2", j),
                                                  start=j == 0, stop=j == CMP_LEN // 2 - 1)
                    close_bank(mm, f"cmp_hid_{key}")
                    unit_last_fill[f"cmp_{key}"] = f"cmp_hid_{key}"
                drained_by(pe, "cmp_hid_k", "cmp_hid_v")
                bank = open_bank("cmp_kT")
                for c in range(2):
                    mm = nc.tensor.matmul(bank[:, 0:4 * N_CMP], cmp_wk2[:, c, :, :].rearrange("p u n -> p (u n)"), cmp_hid[:, 0, c, :],
                                          start=c == 0, stop=c == 1)
                close_bank(mm, "cmp_kT")
                bank = open_bank("cmp_v")
                for g in range(NSA_KV):
                    for c in range(2):
                        mm = nc.tensor.matmul(bank[0:N_CMP, g * 64:g * 64 + 64], cmp_hid[:, 1, c, g * N_CMP:g * N_CMP + N_CMP],
                                              cmp_wv2[:, c, :], start=c == 0, stop=c == 1)
                close_bank(mm, "cmp_v")
                drained_by(pe, "cmp_kT", *[f"nqT{j}" for j in range(4)])
                for t in range(TT):
                    for odd in range(2):
                        bank = open_bank(f"cmpS{t}{odd}")
                        for i in range(NSA_HEADS // 2):
                            r, g = 64 * odd, i // 2
                            mm = nc.tensor.matmul(bank[:, i * N_CMP:i * N_CMP + N_CMP], nqT[r:r + 64, i, t * P:t * P + P],
                                                  cmp_kT[r:r + 64, g * N_CMP:g * N_CMP + N_CMP], start=True, stop=True)
                        close_bank(mm, f"cmpS{t}{odd}")
                for t in range(TT):
                    pe.wait_ge(sem("cmp_probs_ready"), t + 1)
                    bank = open_bank(f"cmpT{t}")
                    for g in range(NSA_KV):
                        mm = nc.tensor.transpose(bank[:, g * P:g * P + P],
                                                 cmp_p[:, t, 4 * g:4 * g + 4, :].rearrange("p h n -> p (h n)"), ident)
                    close_bank(mm, f"cmpT{t}")
                drained_by(pe, "cmpT0", "cmpT1")
                pe.wait_ge(sem("cmp_v_ready"), 1)
                for t in range(TT):
                    for f in range(2):
                        bank = open_bank(f"cmpO{t}{f}")
                        for j in range(2):
                            mm = nc.tensor.matmul(bank[:, j * 256:j * 256 + 256], cmp_pT[:, t, 2 * f + j, :], cmp_v[:, 2 * f + j, :],
                                                  start=True, stop=True)
                        close_bank(mm, f"cmpO{t}{f}")
                drained_by(pe, *[f"nq_rotT{j}" for j in range(4)], "ksT0", "ksT1", "kwT0", "kwT1")
                attend(blocks2)
                pe.wait_ge(sem("y_b_ready"), 1)
                transposes("y_bT", y_b)
                drained_by(pe, *[f"y_bT{j}" for j in range(4)])
                for c in range(2):
                    token_major(f"branch_b{c}", f"branch_b{c}", y_bT)
                pe.wait_ge(sem("merged_ready"), 1)
                transposes("mergedT", mix_a)
                drained_by(pe, *[f"mergedT{j}" for j in range(4)])
                for c in range(2):
                    token_major(f"out2_{c}", f"out2_{c}", xT)
                pe.wait_ge(sem("x_normed"), 10)
                transposes("mlpT", normed)
                drained_by(pe, *[f"mlpT{j}" for j in range(4)])
                for c in range(8):
                    feature_major(f"up{c}", f"up{c}", xT)
                for c in range(2):
                    tiles = [open_bank(f"down{c}{t}") for t in range(TT)]
                    for k4 in range(4):
                        w = use(f"down{c}{k4}")
                        if c == 0:
                            pe.wait_ge(sem("ff_ready"), 4 * k4 + 4)
                        for t in range(TT):
                            for k in range(KT):
                                mm = nc.tensor.matmul(tiles[t], ffT[k4][:, k, t * P:t * P + P], w[:, k, :],
                                                      start=k4 == 0 and k == 0, stop=k4 == 3 and k == KT - 1)
                            if k4 == 3:
                                close_bank(mm, f"down{c}{t}")
                        if k4 < 3:
                            mm.then_inc(sem("down_used"), 1)
                        unit_last_fill[f"down{c}{k4}"] = f"down{c}1" if k4 == 3 else 3 * c + k4 + 1
                pe.wait_ge(sem("p_landed"), 16)
                bank = open_bank("pT")
                for k in range(2):
                    for t in range(TT):
                        mm = nc.tensor.transpose(bank[:, k * T + t * P:k * T + t * P + P], p_tok[:, t, k * P:k * P + P], ident)
                close_bank(mm, "pT")
                drained_by(pe, "pT")
                w = use("ple")
                for c in range(2):
                    for t in range(TT):
                        bank = open_bank(f"ple{c}{t}")
                        for k in range(2):
                            mm = nc.tensor.matmul(bank, pT[:, k, t * P:t * P + P], w[:, k, c * 512:c * 512 + 512], start=k == 0, stop=k == 1)
                        close_bank(mm, f"ple{c}{t}")
                unit_last_fill["ple"] = "ple11"
                pe.wait_ge(sem("x_ready"), TT)
                transposes("pleT", x)
                drained_by(pe, *[f"pleT{j}" for j in range(4)])
                for c in range(2):
                    token_major(f"ple_gate{c}", f"ple_gate{c}", xT)

            counts, roots = {}, []

            def counted(eng, ins, name, wait):
                counts[name] = counts.get(name, 0) + 1
                ins.then_inc(sem(name), 1)
                if wait:
                    eng.wait_ge(sem(name), counts[name])

            def drains(eng, ins, fill, wait):
                n = fills[fill]
                ins.then_inc(sem(f"bank_drained{n % BANKS}"), 1)
                if wait:
                    eng.wait_ge(sem(f"bank_drained{n % BANKS}"), n // BANKS + 1)

            @block.vector
            def _(dve):
                V = nc.vector

                def step(ins, name="dve_step", wait=True):
                    counted(dve, ins, name, wait)

                def drain(ins, fill, wait=False):
                    drains(dve, ins, fill, wait)

                def wide(ap, shape):
                    return ap.to_broadcast(shape)

                def inverse_root(v):
                    roots.append(v)
                    dve.wait_ge(sem("root_ready"), len(roots))
                    step(V.reciprocal(v, v))

                def inverse_rms(dst, sums, width):
                    step(V.tensor_scalar(dst, sums, 1.0 / width, EPS, ALU.mult, ALU.add), "variance_ready", wait=False)
                    inverse_root(dst)

                def normalize(src, dst, k, name):
                    sums, inv = stat(k, 2), stat(k + 2, 2)
                    for t in range(TT):
                        step(V.tensor_tensor_reduce(dst[:, t, :], src[:, t, :], src[:, t, :], 1.0, 0.0, ALU.mult, ALU.add,
                                                    sums[:, t:t + 1]))
                    inverse_rms(inv, sums, src.shape[2])
                    for t in range(TT):
                        step(V.tensor_scalar(dst[:, t, :], src[:, t, :], inv[:, t:t + 1], None, ALU.mult), name)

                def turned(tag, dst, gain=None):
                    for j in (1, 3):
                        bank = filled_by(dve, f"{tag}{j}")
                        for k in (2 * j, 2 * j + 1):
                            src = bank[:, (k % 2) * T:(k % 2) * T + T]
                            ins = V.tensor_copy(dst[:, k, :], src) if gain is None else \
                                V.tensor_scalar(dst[:, k, :], src, col(gain, k), None, ALU.mult)
                        drain(ins, f"{tag}{j}")

                def softmax(blk):
                    nk = blk["nk"]
                    per = 512 // nk
                    mask = const("causal")[:, T - nk:T].unsqueeze(1)
                    for f in range(HEADS // per):
                        bank = filled_by(dve, f"{blk['name']}S{f}")
                        drain(V.tensor_tensor(blk["p"][:, f * per:f * per + per, :], grid(bank, per), wide(mask, [P, per, nk]), ALU.add),
                              f"{blk['name']}S{f}", wait=True)
                    top, _, _ = block_stats(blk)
                    step(V.tensor_reduce(top, blk["p"], AX.X, ALU.max))
                    step(V.tensor_scalar(top, top, -blk["scale"], None, ALU.mult), "max_ready")

                def probs_turned(blk):
                    flat = blk["pt"]
                    for f in range(1, HEADS * blk["nk"] // P // 4, 2):
                        bank = filled_by(dve, f"{blk['name']}T{f}")
                        drain(V.tensor_copy(flat[:, 4 * f:4 * f + 4, :], grid(bank, 4)), f"{blk['name']}T{f}")

                def by_head(flat):
                    return flat.rearrange("p (i r e) -> p i r e", r=2, e=HEAD_DIM)

                def factors(inv):
                    return wide(inv.rearrange("p (r i) -> p i r", r=2).unsqueeze(3), [P, HEADS // 2, 2, HEAD_DIM])

                def inverse_sums(blk):
                    dve.wait_ge(sem("probs_ready"), blk["n"] + 1)
                    _, sums, inv = block_stats(blk)
                    step(V.reciprocal(inv, sums))

                bank = filled_by(dve, "params")
                V.tensor_copy(cols[:, 0:n_rows], bank[:, 0:n_rows])
                drain(V.tensor_copy(cols[:, P:P + 4 * TAPS], bank[:, P:P + 4 * TAPS]), "params", wait=True)
                dve.wait_ge(sem("x_landed"), 16)
                normalize(x, normed, 4, "x_normed")
                turned("mixT", xT, "norm_mix_g")
                step(V.memset(z[:, :, 0:TAPS - 1], 0.0))
                for f in range(2):
                    drained_by(dve, f"conv_g{f}")
                    bank = filled_by(dve, f"conv_a{f}")
                    for cb in (2 * f, 2 * f + 1):
                        ins = V.scalar_tensor_tensor(out=z[:, cb, TAPS - 1:ZW], in0=bank[:, (cb % 2) * T:(cb % 2) * T + T],
                                                     scalar=col("b_glu", cb), in1=glu[:, cb, :], op0=ALU.add, op1=ALU.mult)
                    drain(ins, f"conv_a{f}", wait=True)
                for cb in range(DVE_CONV):
                    step(V.tensor_scalar(conv[:, cb, :], z[:, cb, 0:T], tap(0, cb), col("b_dw", cb), ALU.mult, ALU.add), wait=False)

                def convolve(taps):
                    for w in taps:
                        for cb in range(DVE_CONV):
                            dve.wait_ge(sem("dve_step"), counts["dve_step"] - DVE_CONV + 1)
                            ins = V.scalar_tensor_tensor(out=conv[:, cb, :], in0=z[:, cb, w:w + T], scalar=tap(w, cb),
                                                         in1=conv[:, cb, :], op0=ALU.mult, op1=ALU.add)
                            step(ins, "conv_ready" if w == TAPS - 1 and cb == DVE_CONV - 1 else "dve_step", wait=False)

                dve.wait_ge(sem("mem_landed"), 16)
                normalize(mem_tok, mem_normed, 0, "mem_normed")
                convolve(range(1, 6))
                for f in range(2):
                    bank = filled_by(dve, f"q{f}")
                    drain(V.tensor_copy(qT1[:, 2 * f:2 * f + 2, :], grid(bank, 2)), f"q{f}")
                convolve(range(6, 11))
                dve.wait_ge(sem("forget_landed"), 32)
                bank = filled_by(dve, "forget")
                tmp = page(4, 0, 1024)[0:HEADS, :].rearrange("p (n t) -> p n t", n=4)
                drain(V.tensor_scalar(tmp[:, 0, :], bank[0:HEADS, 0:T], forget_b[:, 0:1], None, ALU.add), "forget", wait=True)
                step(V.tensor_scalar(tmp[:, 1, :], tmp[:, 0, :], -1.0, None, ALU.mult))
                step(V.tensor_tensor(tmp[:, 1, :], tmp[:, 1, :], tmp[:, 0, :], ALU.max), "forget_abs")
                step(V.tensor_scalar(tmp[:, 0, :], tmp[:, 0, :], 0.0, None, ALU.min))
                dve.wait_ge(sem("forget_log"), 1)
                step(V.tensor_tensor(log_f, tmp[:, 0, :], tmp[:, 2, :], ALU.subtract))
                step(V.tensor_tensor_scan(tmp[:, 3, :], const("ones")[0:HEADS, 0:T], log_f, 0.0, ALU.mult, ALU.add))
                step(V.tensor_scalar(key_bias, tmp[:, 3, :], -(HEAD_DIM ** 0.5), None, ALU.mult), "key_bias_ready")
                convolve(range(11, 16))
                turned("memT", memT, "mem_norm_g")
                for c in range(2):
                    for f in range(2):
                        bank = filled_by(dve, f"mem_k{c}{f}")
                        drain(V.tensor_copy(mem_k[:, 4 * c + 2 * f:4 * c + 2 * f + 2, :], grid(bank, 2)), f"mem_k{c}{f}")
                        convolve(range(16 + 4 * (2 * c + f), min(20 + 4 * (2 * c + f), TAPS)))
                softmax(blocks1[0])
                softmax(blocks1[1])
                for blk in blocks1:
                    inverse_sums(blk)
                    probs_turned(blk)

                def attn1_out(blk):
                    t = blk["t"]
                    _, _, inv = block_stats(blk)
                    bank = filled_by(dve, f"{blk['name']}O")
                    drain(V.tensor_tensor(by_head(attn1[:, t, :]), by_head(bank), factors(inv), ALU.mult), f"{blk['name']}O", wait=True)
                    junk = page(9, 0, 512)
                    sums, inv_rms = stat(8 + t, 1), stat(10 + t, 1)
                    step(V.tensor_tensor_reduce(junk, attn1[:, t, :], attn1[:, t, :], 1.0, 0.0, ALU.mult, ALU.add, sums))
                    inverse_rms(inv_rms, sums, D_ATTN)
                    step(V.tensor_scalar(attn1[:, t, :], attn1[:, t, :], inv_rms, None, ALU.mult), "attn1_normed")

                bank = filled_by(dve, "conv_mean")
                mean = page(9, 512, 256)
                drain(V.tensor_scalar(mean, bank[:, 0:T], 1.0 / D_CONV, None, ALU.mult), "conv_mean", wait=True)
                step(V.tensor_tensor(conv, conv, wide(mean.unsqueeze(1), [P, 4, T]), ALU.subtract))
                step(V.tensor_tensor(glu, conv, conv, ALU.mult), "conv_ready")
                attn1_out(blocks1[0])
                attn1_out(blocks1[1])
                bank = filled_by(dve, "conv_var")
                drain(V.tensor_scalar(mean, bank[:, 0:T], 1.0 / D_CONV, None, ALU.mult), "conv_var", wait=True)
                step(V.tensor_scalar(mean, mean, EPS, None, ALU.add), "variance_ready", wait=False)
                inverse_root(mean)
                step(V.tensor_tensor(conv, conv, wide(mean.unsqueeze(1), [P, 4, T]), ALU.mult), "conv_normed")
                for t in range(TT):
                    bank = filled_by(dve, f"attn1T{t}")
                    for k in range(4):
                        ins = V.tensor_scalar(catT[:, k, t * P:t * P + P], bank[:, k * P:k * P + P], col("attn_out_g", k), None, ALU.mult)
                    drain(ins, f"attn1T{t}")

                def add_to_x(tag):
                    for c in range(2):
                        for t in range(TT):
                            bank = filled_by(dve, f"{tag}{c}{t}")
                            drain(V.tensor_tensor(x[:, t, c * 512:c * 512 + 512], x[:, t, c * 512:c * 512 + 512], bank, ALU.add),
                                  f"{tag}{c}{t}", wait=True)

                add_to_x("out")
                normalize(x, normed, 12, "x_normed")
                turned("crossT", xT, "norm_mem_g")
                for c in range(2):
                    bank = filled_by(dve, f"mem_q{c}1")
                    drain(V.tensor_copy(qT2[:, 4 * c + 2:4 * c + 4, :], grid(bank, 2)), f"mem_q{c}1")
                top2 = grid(stat(16, 8), TT)
                sum2, inv2 = grid(stat(24, 8), TT), grid(stat(32, 8), TT)
                for t in range(TT):
                    for f in range(2):
                        bank = filled_by(dve, f"crossS{t}{f}")
                        step(V.tensor_reduce(top2[:, t, 2 * f:2 * f + 2], grid(bank, 2), AX.X, ALU.max))
                        step(V.tensor_scalar(top2[:, t, 2 * f:2 * f + 2], top2[:, t, 2 * f:2 * f + 2], -(MEM_DIM ** -0.5), None, ALU.mult),
                             "cross_max_ready")
                for t in range(TT):
                    drained_by(dve, f"crossS{t}0", f"crossS{t}1")
                    step(V.reciprocal(inv2[:, t, :], sum2[:, t, :]))
                    step(V.tensor_tensor(prob2[:, t, :, :], prob2[:, t, :, :], wide(inv2[:, t, :].unsqueeze(2), [P, MEM_HEADS, T]), ALU.mult),
                         "cross_probs_ready")
                for t in range(TT):
                    bank = filled_by(dve, f"crossT{t}1")
                    drain(V.tensor_copy(prob2T[:, 2:4, :, t * P:t * P + P], bank.rearrange("p (h m q) -> p h m q", h=2, m=2)), f"crossT{t}1")
                for f in (1, 3):
                    bank = filled_by(dve, f"crossO{f}")
                    drain(V.tensor_copy(oT2[:, 2 * f:2 * f + 2, :], grid(bank, 2)), f"crossO{f}")
                add_to_x("mem_o")
                normalize(x, normed, 40, "x_normed")
                turned("ffnT", xT, "norm_ffn_g")
                chosen = grid(scratch_route[:, 0:64], TT)
                r = lambda k, n: scratch_route[:, 64 + k:64 + k + n]
                dve.wait_ge(sem("route_landed"), 16 * (GROUPS + 3))
                bank = filled_by(dve, "route")
                drain(V.tensor_tensor(logits, grid(bank[:, 0:72], TT), wide(route_b[:, :].unsqueeze(1), [P, TT, 36]), ALU.add), "route", wait=True)

                def first_largest(values, n, k, top):
                    hot, run = r(k, n), r(k + 32, n)
                    step(V.tensor_reduce(top, values, AX.X, ALU.max))
                    step(V.tensor_scalar(hot, values, top, None, ALU.is_equal))
                    step(V.tensor_tensor_scan(run, const("ones")[:, 0:n], hot, 0.0, ALU.mult, ALU.add))
                    step(V.tensor_scalar(run, run, 1.0, None, ALU.is_equal))
                    step(V.tensor_tensor(hot, hot, run, ALU.mult))
                    return hot

                for t in range(TT):
                    base = 512 * t
                    tops = stat(44 + 8 * t, 8)
                    group = first_largest(logits[:, t, 0:4], 4, base, tops[:, 0:1])
                    step(V.tensor_scalar(tops[:, 1:2], tops[:, 0:1], -1.0, None, ALU.mult), "group_max_ready")
                    step(V.tensor_scalar(r(base + 64, 4), group, -1.0, BIG, ALU.add, ALU.mult))
                    masked = r(base + 96, 32)
                    step(V.tensor_tensor(grid(masked, 4), grid(logits[:, t, 4:36], 4), wide(r(base + 64, 4).unsqueeze(2), [P, 4, 8]), ALU.add))
                    one = first_largest(masked, 32, base + 128, tops[:, 2:3])
                    rest = r(base + 192, 32)
                    step(V.scalar_tensor_tensor(out=rest, in0=one, scalar=-3.0 * BIG, in1=masked, op0=ALU.mult, op1=ALU.add))
                    two = first_largest(rest, 32, base + 224, tops[:, 3:4])
                    step(V.tensor_tensor(chosen[:, t, :], one, two, ALU.add), "choice_ready" if t == 1 else "dve_step")
                    step(V.tensor_tensor(tops[:, 4:5], tops[:, 3:4], tops[:, 2:3], ALU.subtract), "second_ready")
                    dve.wait_ge(sem("route_exp"), 2 * t + 2)
                    step(V.scalar_tensor_tensor(out=tops[:, 6:7], in0=tops[:, 4:5], scalar=1.0, in1=tops[:, 5:6], op0=ALU.add, op1=ALU.mult))
                    step(V.reciprocal(tops[:, 6:7], tops[:, 6:7]))
                    step(V.scalar_tensor_tensor(out=gate[:, t, :], in0=two, scalar=tops[:, 4:5], in1=one, op0=ALU.mult, op1=ALU.add))
                    step(V.tensor_scalar(gate[:, t, :], gate[:, t, :], tops[:, 6:7], None, ALU.mult))
                bank = filled_by(dve, "rank")
                step(V.scalar_tensor_tensor(out=pos[:, :, :], in0=grid(bank[:, 0:64], TT), scalar=1.0, in1=chosen, op0=ALU.add, op1=ALU.mult))
                step(V.tensor_scalar(pos[:, :, :], pos[:, :, :], -1.0, None, ALU.add))
                drain(V.tensor_reduce(stat(60, 1), bank[:, 64:96], AX.X, ALU.max), "rank", wait=True)
                step(V.tensor_copy(busiest[:, :], stat(60, 1)), "busiest_ready")

                def experts(tag, first, n_pairs):
                    s = lambda name: sem(f"{tag}_{name}")

                    def pick(n, e, dst, gated_too):
                        expert = bass.ds(2 * ((n + first) % PAIRS) + e, 1)
                        slots = const("slots")[:, bass.ds(CAP * ((n + first) // PAIRS), CAP)]
                        for t in range(TT):
                            o = dst[:, t, e * CAP:e * CAP + CAP]
                            if gated_too:
                                ins = V.tensor_scalar(o, slots, pos[:, t, expert], gate[:, t, expert], ALU.is_equal, ALU.mult)
                            else:
                                ins = V.tensor_scalar(o, slots, pos[:, t, expert], None, ALU.is_equal)
                        return ins

                    def build_choose(n):
                        pick(n, 0, choose, False)
                        pick(n, 1, choose, False).then_inc(s("choose_ready"), 1)

                    def build_gated(n):
                        pick(n, 0, choose_gated, True)
                        pick(n, 1, choose_gated, True).then_inc(s("gated_choose_ready"), 1)

                    def drain_picked(n):
                        for f, b in ((0, 0), (1, 7)):
                            dve.wait_ge(s("picked_filled"), 2 * n + f + 1)
                            V.tensor_tensor(picked[:, 4 * f:4 * f + 4, :], grid(ps[:, b, :], 4),
                                            wide(col("norm_ffn_g", 4 * f, 4).unsqueeze(2), [P, 4, P]), ALU.mult).then_inc(s("picked_drained"), 1)

                    def drain_sums(n):
                        for t in range(TT):
                            for c in range(2):
                                dve.wait_ge(s("sum_filled"), 4 * n + 2 * t + c + 1)
                                V.tensor_tensor(x[:, t, c * 512:c * 512 + 512], x[:, t, c * 512:c * 512 + 512], ps[:, 5 + c, :],
                                                ALU.add).then_inc(s("sum_drained"), 1)

                    def gate_hidden(n):
                        dve.wait_ge(s("silu_ready"), n + 1)
                        dve.wait_ge(s("up_filled"), 2 * n + 2)
                        V.tensor_tensor(hidden, hidden, ps[:, 2, :], ALU.mult).then_inc(s("hidden_ready"), 1)

                    V.memset(spread, 0.0).then_inc(s("spread_ready"), 1)
                    for c in range(2):
                        V.memset(expert_out[:, c * 512:c * 512 + 512], 0.0).then_inc(s("out_ready"), 1)
                    build_choose(0)
                    build_gated(0)
                    drain_picked(0)
                    build_choose(1)
                    with dve.Fori(0, n_pairs) as i:
                        drain_sums(i)
                        gate_hidden(i)
                        dve.wait_ge(s("sum_drained"), 4 * i + 4)
                        drain_picked(i + 1)
                        build_choose(i + 2)
                        dve.wait_ge(s("spread_filled"), i + 1)
                        build_gated(i + 1)
                    drain_sums(n_pairs)
                    dve.wait_ge(s("sum_drained"), 4 * n_pairs + 4)

                experts("moe", 0, PAIRS)
                count = dve.value_load(busiest[0:1, 0:1], min_val=0, max_val=T)
                with dve.If(count > CAP):
                    experts("more", PAIRS, MORE)

                dve.wait_ge(sem("final_gain_landed"), 16)
                normalize(x, normed, 40, "final_normed")
                for t in range(TT):
                    step(V.tensor_tensor(x[:, t, :], normed[:, t, :], gain_final, ALU.mult))
                normalize(x, normed, 44, "x_normed")
                e0, e1, lb, rest = stat(0, 8), stat(8, 8), stat(16, 8), stat(24, 8)
                l0, l1 = col("hg_lb_logits_2", 0, 8), col("hg_lb_logits_2", 8, 8)
                step(V.tensor_tensor(lb, l0, l1, ALU.max))
                step(V.tensor_tensor(e0, l0, lb, ALU.subtract))
                step(V.tensor_tensor(e1, l1, lb, ALU.subtract), "lb_ready")
                dve.wait_ge(sem("lb_exp"), 2)
                step(V.tensor_tensor(rest, e0, e1, ALU.add))
                step(V.reciprocal(rest, rest))
                step(V.tensor_tensor(lb, e0, rest, ALU.mult))
                step(V.tensor_scalar(rest, lb, -1.0, 1.0, ALU.mult, ALU.add))
                turned("mix2T", xT, "norm_pre_mix_2")
                for c in range(2):
                    for f in range(2):
                        at = (4 * c + 2 * f) * T
                        dve.wait_ge(sem("hq_sigmoid"), 2 * c + f + 1)
                        bank = filled_by(dve, f"hq{c}{f}")
                        drain(V.scalar_tensor_tensor(out=hq[:, at:at + 512], in0=bank, scalar=P ** -0.5, in1=hx[0][:, at:at + 512],
                                                     op0=ALU.mult, op1=ALU.mult), f"hq{c}{f}", wait=True)
                drained_by(dve, "hf00", "hf01", "hf10", "hf11")
                for h in range(HG_HEADS):
                    step(V.tensor_scalar(hb[:, h * T:h * T + T], hb[:, h * T:h * T + T], rest[:, h:h + 1], lb[:, h:h + 1], ALU.mult, ALU.add),
                         "forget2_ready", wait=False)
                dve.wait_ge(sem("forget2_ready"), HG_HEADS)
                step(V.tensor_scalar(hk, hb, -1.0, 1.0, ALU.mult, ALU.add), "level_ready")
                dve.wait_ge(sem("log_forget"), 1)
                for h in range(HG_HEADS):
                    step(V.tensor_tensor_scan(hb[:, h * T:h * T + T], const("chunk_reset"), hx[0][:, h * T:h * T + T], 0.0, ALU.mult, ALU.add),
                         wait=h == HG_HEADS - 1)

                def level_drains(n):
                    if n and LEVELS[n - 1] == P:
                        for f in range(2):
                            bank = filled_by(dve, f"level{n}_{f}")
                            drain(V.tensor_copy(scores_cross[:, f * 512:f * 512 + 512], bank), f"level{n}_{f}")
                        return
                    mask = const("ident") if n == 0 else const(f"level{LEVELS[n - 1]}")
                    mask = mask.unsqueeze(1)
                    for f in range(4):
                        bank = filled_by(dve, f"level{n}_{f}")
                        dst = grid(scores_diag[:, f * 512:f * 512 + 512], 4)
                        if n == 0:
                            drain(V.tensor_tensor(dst, grid(bank, 4), wide(mask, [P, 4, P]), ALU.mult), f"level{n}_{f}", wait=True)
                        else:
                            drain(V.copy_predicated(dst, wide(mask.bitcast(U32), [P, 4, P]), grid(bank, 4)), f"level{n}_{f}", wait=True)

                for n, L in enumerate(LEVELS, 1):
                    halves = lambda flat: flat.rearrange("p (n r l) -> p n r l", r=2, l=L)
                    n_blocks = HG_HEADS * T // (2 * L)
                    b, e = halves(hb), halves(hx[n % 2])
                    mid = wide(b[:, :, 0, L - 1:L], [P, n_blocks, L])
                    if L >= CHUNK:
                        step(V.tensor_tensor(b[:, :, 1, :], b[:, :, 1, :], mid, ALU.add))
                    step(V.tensor_tensor(e[:, :, 0, :], mid, b[:, :, 0, :], ALU.subtract), wait=False)
                    step(V.tensor_tensor(e[:, :, 1, :], b[:, :, 1, :], mid, ALU.subtract), "exponent_ready")
                    level_drains(n - 1)
                    dve.wait_ge(sem("decay_ready"), n)
                    step(V.tensor_tensor(e[:, :, 0, :], e[:, :, 0, :], halves(hk)[:, :, 0, :], ALU.mult), wait=False)
                    step(V.tensor_tensor(e[:, :, 1, :], e[:, :, 1, :], halves(hq)[:, :, 1, :], ALU.mult), "level_ready")
                level_drains(len(LEVELS))
                dve.wait_ge(sem("gnorm_landed"), 16)
                drained_by(dve, *[f"hg{c}{t}" for c in range(2) for t in range(TT)])
                for t in range(TT):
                    g = grid(hg[:, t, :], HG_HEADS)
                    step(V.tensor_tensor(g, g, wide(gnorm.unsqueeze(1), [P, HG_HEADS, P]), ALU.mult), wait=False)
                drained_by(dve, "nq00", "nq01", "nq10", "nq11", *[f"kv{c}{t}" for c in range(3) for t in range(TT)])
                for t in range(TT):
                    step(V.tensor_scalar(nq[:, t, :], nq[:, t, :], NSA_DH ** -0.5, None, ALU.mult), "nq_scaled")
                step(V.tensor_copy(nq_rot[:, :, :], nq[:, :, :]), "nq_ready")
                half = ROPE_DIM // 2
                tmp = [grid(page(6, 256 * n, 256), TT) for n in range(4)]
                for src, dst, n in ((nq, nq_rot, NSA_HEADS), (nkv[:, :, 512:768], nkv[:, :, 512:768], NSA_KV),
                                    (nkv[:, :, 1024:1280], nkv[:, :, 1024:1280], NSA_KV)):
                    for t in range(TT):
                        sv = src[:, t, :].rearrange("p (h e) -> p h e", e=NSA_DH)
                        dv = dst[:, t, :].rearrange("p (h e) -> p h e", e=NSA_DH)
                        cos = wide(grid(const("cos"), TT)[:, t, :].unsqueeze(1), [P, n, half])
                        sin = wide(grid(const("sin"), TT)[:, t, :].unsqueeze(1), [P, n, half])
                        a = [w[:, t, 0:n * half].rearrange("p (h e) -> p h e", e=half) for w in tmp]
                        x1, x2 = sv[:, :, 0:half], sv[:, :, half:ROPE_DIM]
                        step(V.tensor_tensor(a[0], x1, cos, ALU.mult), wait=False)
                        step(V.tensor_tensor(a[1], x2, sin, ALU.mult), wait=False)
                        step(V.tensor_tensor(a[2], x2, cos, ALU.mult), wait=False)
                        step(V.tensor_tensor(a[3], x1, sin, ALU.mult))
                        step(V.tensor_tensor(dv[:, :, 0:half], a[0], a[1], ALU.subtract), wait=False)
                        step(V.tensor_tensor(dv[:, :, half:ROPE_DIM], a[2], a[3], ALU.add), "rotated")
                for t in range(TT):
                    for f in range(2):
                        bank = filled_by(dve, f"rec{t}{f}")
                        drain(V.tensor_copy(normed[:, t, f * 512:f * 512 + 512], bank), f"rec{t}{f}", wait=True)
                for t in range(TT):
                    o = grid(normed[:, t, :], HG_HEADS)
                    sq = grid(page(6 + t, 1024, 1024), HG_HEADS)
                    sums = stat(0 + 16 * t, 8)
                    step(V.tensor_tensor(sq, o, o, ALU.mult))
                    step(V.tensor_reduce(sums, sq, AX.X, ALU.add))
                    inverse_rms(sums, sums, P)
                    step(V.tensor_tensor(o, o, wide(sums.unsqueeze(2), [P, HG_HEADS, P]), ALU.mult))
                    step(V.tensor_tensor(normed[:, t, :], normed[:, t, :], hg[:, t, :], ALU.mult), "y_a_ready" if t else "dve_step")
                turned("nqT", nqT)
                turned("nq_rotT", nq_rotT)
                for key, dst in (("kc", kc2), ("vc", vc2)):
                    for f in range(2):
                        bank = filled_by(dve, f"{key}T{f}")
                        src = grid(bank, 2)
                        V.tensor_copy(dst[0:64, 2 * f:2 * f + 2, :], src[0:64, :, :])
                        drain(V.tensor_copy(dst[64:128, 2 * f:2 * f + 2, 0:T - 1], src[64:128, :, 1:T]), f"{key}T{f}")
                turned("y_aT", y_aT)
                dve.wait_ge(sem("mix_gates_ready"), 2)
                for c in range(2):
                    for t in range(TT):
                        bank = filled_by(dve, f"branch_a{c}{t}")
                        m = mix_a[:, t, c * 512:c * 512 + 512]
                        drain(V.tensor_tensor(m, m, bank, ALU.mult), f"branch_a{c}{t}")
                for s_, key in enumerate("kv"):
                    bank = filled_by(dve, f"cmp_hid_{key}")
                    step(V.tensor_copy(cmp_pe[:, 2 * s_:2 * s_ + 2], bank[:, 128:130]), "cmp_pe_ready")
                bank = filled_by(dve, "cmp_kT")
                drain(V.tensor_copy(cmp_kT, bank[:, 0:4 * N_CMP]), "cmp_kT")
                step(V.memset(page(13, 1024, 1024), 0.0))
                bank = filled_by(dve, "cmp_v")
                for h in range(4):
                    ins = V.tensor_copy(cmp_v[32 * h:32 * h + N_CMP, :, h * 64:h * 64 + 64], grid(bank[0:N_CMP, 0:256], 4))
                    if h < 3:
                        step(ins)
                    else:
                        drain(ins, "cmp_v", wait=True)
                step(V.memset(page(9, 0, 1024), 0.0), "cmp_v_ready")
                seen, bias = grid(const("cmp_seen"), TT), grid(const("cmp_bias"), TT)
                tops = [stat(0, 16), stat(16, 16)]
                for t in range(TT):
                    live = cmp_p[:, t, :, 0:N_CMP]
                    for odd in range(2):
                        bank = filled_by(dve, f"cmpS{t}{odd}")
                        drain(V.tensor_tensor(live[:, odd:NSA_HEADS:2, :], grid(bank[:, 0:NSA_HEADS // 2 * N_CMP], NSA_HEADS // 2),
                                              wide(bias[:, t, :].unsqueeze(1), [P, NSA_HEADS // 2, N_CMP]), ALU.add), f"cmpS{t}{odd}", wait=True)
                    step(V.tensor_reduce(tops[t], live, AX.X, ALU.max))
                    step(V.tensor_tensor(live, live, wide(tops[t].unsqueeze(2), [P, NSA_HEADS, N_CMP]), ALU.subtract), "cmp_shifted")
                for t in range(TT):
                    live = cmp_p[:, t, :, 0:N_CMP]
                    dve.wait_ge(sem("cmp_exp_ready"), t + 1)
                    step(V.tensor_reduce(tops[t], live, AX.X, ALU.add))
                    step(V.reciprocal(tops[t], tops[t]))
                    step(V.tensor_tensor(live, live, wide(tops[t].unsqueeze(2), [P, NSA_HEADS, N_CMP]), ALU.mult))
                    step(V.tensor_tensor(live, live, wide(seen[:, t, :].unsqueeze(1), [P, NSA_HEADS, N_CMP]), ALU.mult), "cmp_probs_ready")
                dve.wait_ge(sem("sel_gates_ready"), 1)
                for t in range(TT):
                    for f in range(2):
                        bank = filled_by(dve, f"cmpO{t}{f}")
                        g = sel_gates[:, t, 8 * f:8 * f + 8].unsqueeze(2)
                        drain(V.tensor_tensor(grid(y_b[:, t, f * 512:f * 512 + 512], HEADS), grid(bank, HEADS), wide(g, [P, HEADS, 64]), ALU.mult),
                              f"cmpO{t}{f}", wait=True)

                def nsa_out(blk):
                    t, half_, branch = blk["t"], blk["half"], blk["branch"]
                    _, _, inv = block_stats(blk)
                    at = 16 * (branch + 1) + 8 * half_
                    in_order = inv.rearrange("p (r i) -> p r i", r=2)
                    step(V.tensor_tensor(in_order, in_order, sel_gates[:, t, at:at + 8].rearrange("p (i r) -> p r i", r=2), ALU.mult))
                    bank = filled_by(dve, f"{blk['name']}O")
                    tmp_ = page(9, 1024, 512)
                    drain(V.tensor_tensor(by_head(tmp_), by_head(bank), factors(inv), ALU.mult), f"{blk['name']}O", wait=True)
                    y = y_b[:, t, half_ * 512:half_ * 512 + 512]
                    last = blk is blocks2[-1]
                    step(V.tensor_tensor(y, y, tmp_, ALU.add), "y_b_ready" if last else "dve_step")

                for i in range(len(blocks2) + 2):
                    if i < len(blocks2):
                        softmax(blocks2[i])
                    if 1 <= i <= len(blocks2):
                        inverse_sums(blocks2[i - 1])
                        probs_turned(blocks2[i - 1])
                    if i >= 2:
                        nsa_out(blocks2[i - 2])
                turned("y_bT", y_bT)
                for c in range(2):
                    for t in range(TT):
                        bank = filled_by(dve, f"branch_b{c}{t}")
                        cut = slice(c * 512, c * 512 + 512)
                        drain(V.tensor_tensor(mix_b[:, t, cut], mix_b[:, t, cut], bank, ALU.mult), f"branch_b{c}{t}", wait=True)
                        step(V.tensor_tensor(mix_a[:, t, cut], mix_a[:, t, cut], mix_b[:, t, cut], ALU.add),
                             "merged_ready" if c and t else "dve_step")
                turned("mergedT", xT)

                def add_normed(src, k, gain, done="dve_step"):
                    normalize(src, normed, k, "post_normed")
                    for t in range(TT):
                        step(V.tensor_tensor(normed[:, t, :], normed[:, t, :], gain, ALU.mult))
                        step(V.tensor_tensor(x[:, t, :], x[:, t, :], normed[:, t, :], ALU.add), done)

                drained_by(dve, *[f"out2_{c}{t}" for c in range(2) for t in range(TT)])
                dve.wait_ge(sem("gains_landed"), 48)
                add_normed(mlp_out, 0, gain_mix)
                normalize(x, normed, 4, "x_normed")
                turned("mlpT", xT, "norm_pre_mlp_2")
                for c in range(8):
                    for f in range(2):
                        drained_by(dve, f"up{c}{f}")
                        k = 4 * (c % 2) + 2 * f
                        dst = ffT[c // 2][:, k:k + 2, :]
                        step(V.tensor_tensor(dst, dst, dst, ALU.mult), "ff_ready", wait=False)
                drained_by(dve, *[f"down{c}{t}" for c in range(2) for t in range(TT)])
                add_normed(mlp_out, 8, gain_mlp, "x_ready")
                bank = filled_by(dve, "pT")
                drain(V.tensor_copy(pT, grid(bank, 2)), "pT")
                turned("pleT", xT)
                for c in range(2):
                    for t in range(TT):
                        drained_by(dve, f"ple{c}{t}", f"ple_gate{c}{t}")
                        e = ple[:, t, c * 512:c * 512 + 512]
                        step(V.tensor_tensor(e, e, ple_gate[:, t, c * 512:c * 512 + 512], ALU.mult))
                normalize(ple, normed, 12, "post_normed")
                for t in range(TT):
                    step(V.tensor_tensor(normed[:, t, :], normed[:, t, :], gain_ple, ALU.mult))
                    step(V.tensor_tensor(x[:, t, :], x[:, t, :], normed[:, t, :], ALU.add), "result_ready")

            @block.scalar
            def _(act):
                S = nc.scalar

                def step(ins, name="act_step", wait=True):
                    counted(act, ins, name, wait)

                def drain(ins, fill, wait=False):
                    drains(act, ins, fill, wait)

                def turned(tag, dst, gain=None):
                    for j in (0, 2):
                        bank = filled_by(act, f"{tag}{j}")
                        for k in (2 * j, 2 * j + 1):
                            src = bank[:, (k % 2) * T:(k % 2) * T + T]
                            ins = S.copy(dst[:, k, :], src) if gain is None else \
                                S.activation(dst[:, k, :], src, ACT.Copy, scale=col(gain, k))
                        drain(ins, f"{tag}{j}")

                def root(times=1):
                    for _ in range(times):
                        n = counts.get("root_ready", 0)
                        act.wait_ge(sem("variance_ready"), n + 1)
                        step(S.activation(roots[n], roots[n], ACT.Sqrt), "root_ready", wait=False)

                def exponentials(blk):
                    act.wait_ge(sem("max_ready"), blk["n"] + 1)
                    top, sums, _ = block_stats(blk)
                    for h in range(HEADS):
                        ins = S.activation(blk["p"][:, h, :], blk["p"][:, h, :], ACT.Exp, bias=top[:, h:h + 1], scale=blk["scale"],
                                           accum_out=sums[:, h:h + 1])
                    step(ins, "probs_ready")

                def probs_turned(blk):
                    for f in range(0, HEADS * blk["nk"] // P // 4, 2):
                        bank = filled_by(act, f"{blk['name']}T{f}")
                        drain(S.copy(blk["pt"][:, 4 * f:4 * f + 4, :], grid(bank, 4)), f"{blk['name']}T{f}")

                def copy_out(fill, dst, func=ACT.Copy):
                    bank = filled_by(act, fill)
                    drain(S.activation(dst, bank, func), fill)

                root()
                drained_by(act, "params")
                turned("mixT", xT, "norm_mix_g")
                for f in range(2):
                    bank = filled_by(act, f"conv_g{f}")
                    for cb in (2 * f, 2 * f + 1):
                        ins = S.activation(glu[:, cb, :], bank[:, (cb % 2) * T:(cb % 2) * T + T], ACT.Sigmoid, bias=col("b_glu", 4 + cb))
                    drain(ins, f"conv_g{f}")
                root()
                for f in range(2):
                    bank = filled_by(act, f"k{f}")
                    drain(S.copy(kT1[:, 2 * f:2 * f + 2, :], grid(bank, 2)), f"k{f}")
                for t in range(TT):
                    copy_out(f"v{t}", v1[:, t, :])
                act.wait_ge(sem("forget_abs"), 1)
                tmp = page(4, 0, 1024)[0:HEADS, :].rearrange("p (n t) -> p n t", n=4)
                step(S.activation(tmp[:, 2, :], tmp[:, 1, :], ACT.Exp, scale=-1.0))
                step(S.activation(tmp[:, 2, :], tmp[:, 2, :], ACT.Ln, bias=1.0), "forget_log")
                turned("memT", memT, "mem_norm_g")
                exponentials(blocks1[0])
                exponentials(blocks1[1])
                for t in range(TT):
                    copy_out(f"mem_v0{t}", mem_v[:, t, 0:512])
                probs_turned(blocks1[0])
                probs_turned(blocks1[1])
                root(3)
                act.wait_ge(sem("conv_normed"), 1)
                for cb in range(4):
                    step(S.activation(catT[:, 4 + cb, :], conv[:, cb, :], ACT.Silu, bias=col("conv_ln_b", cb), scale=col("conv_ln_g", cb)),
                         "conv_done", wait=False)
                for t in range(TT):
                    copy_out(f"mem_v1{t}", mem_v[:, t, 512:1024])
                root()
                turned("crossT", xT, "norm_mem_g")
                for c in range(2):
                    bank = filled_by(act, f"mem_q{c}0")
                    drain(S.copy(qT2[:, 4 * c:4 * c + 2, :], grid(bank, 2)), f"mem_q{c}0")
                top2, sum2 = grid(stat(16, 8), TT), grid(stat(24, 8), TT)
                for t in range(TT):
                    for f in range(2):
                        act.wait_ge(sem("cross_max_ready"), 2 * t + f + 1)
                        bank = filled_by(act, f"crossS{t}{f}")
                        for j in range(2):
                            h = 2 * f + j
                            ins = S.activation(prob2[:, t, h, :], bank[:, j * T:j * T + T], ACT.Exp, bias=top2[:, t, h:h + 1],
                                               scale=MEM_DIM ** -0.5, accum_out=sum2[:, t, h:h + 1])
                        drain(ins, f"crossS{t}{f}")
                for t in range(TT):
                    bank = filled_by(act, f"crossT{t}0")
                    drain(S.copy(prob2T[:, 0:2, :, t * P:t * P + P], bank.rearrange("p (h m q) -> p h m q", h=2, m=2)), f"crossT{t}0")
                for f in (0, 2):
                    bank = filled_by(act, f"crossO{f}")
                    drain(S.copy(oT2[:, 2 * f:2 * f + 2, :], grid(bank, 2)), f"crossO{f}")
                root()
                turned("ffnT", xT, "norm_ffn_g")
                for t in range(TT):
                    tops = stat(44 + 8 * t, 8)
                    act.wait_ge(sem("group_max_ready"), t + 1)
                    step(S.activation(stat(504, 4), logits[:, t, 0:4], ACT.Exp, bias=tops[:, 1:2], accum_out=tops[:, 5:6]), "route_exp")
                    act.wait_ge(sem("second_ready"), t + 1)
                    step(S.activation(tops[:, 4:5], tops[:, 4:5], ACT.Exp), "route_exp")

                def experts(tag, n_pairs):
                    s = lambda name: sem(f"{tag}_{name}")

                    act.wait_ge(s("out_ready"), 2)
                    with act.Fori(0, n_pairs) as i:
                        act.wait_ge(s("gate_filled"), 2 * i + 2)
                        S.activation(hidden, ps[:, 1, :], ACT.Silu).then_inc(s("silu_ready"), 1)
                        act.wait_ge(s("hidden_turned"), i + 1)
                        S.copy(hiddenT, grid(ps[:, 1, :], 4)).then_inc(s("hiddenT_ready"), 1)
                        act.wait_ge(s("spread_filled"), i + 1)
                        S.copy(spread, ps[:, 5, 0:T]).then_inc(s("spread_ready"), 1)
                        act.wait_ge(s("down_filled"), 2 * i + 2)
                        for c in range(2):
                            S.copy(expert_out[:, c * 512:c * 512 + 512], ps[:, 3 + c, :]).then_inc(s("out_ready"), 1)

                experts("moe", PAIRS)
                act.wait_ge(sem("busiest_ready"), 1)
                count = act.value_load(busiest[0:1, 0:1], min_val=0, max_val=T)
                with act.If(count > CAP):
                    experts("more", MORE)

                root(2)
                e0, e1 = stat(0, 8), stat(8, 8)
                act.wait_ge(sem("lb_ready"), 1)
                step(S.activation(e0, e0, ACT.Exp), "lb_exp", wait=False)
                step(S.activation(e1, e1, ACT.Exp), "lb_exp")
                turned("mix2T", xT, "norm_pre_mix_2")
                for c in range(2):
                    for f in range(2):
                        at = (4 * c + 2 * f) * T
                        bank = filled_by(act, f"hq{c}{f}")
                        step(S.activation(hx[0][:, at:at + 512], bank, ACT.Sigmoid), "hq_sigmoid", wait=False)
                for c in range(2):
                    for f in range(2):
                        at = (4 * c + 2 * f) * T
                        copy_out(f"hf{c}{f}", hb[:, at:at + 512], ACT.Sigmoid)
                for c in range(2):
                    for t in range(TT):
                        copy_out(f"hi{c}{t}", hv[:, t, c * 512:c * 512 + 512])
                for c in range(2):
                    for t in range(TT):
                        copy_out(f"hg{c}{t}", hg[:, t, c * 512:c * 512 + 512], ACT.Silu)
                act.wait_ge(sem("forget2_ready"), HG_HEADS)
                drained_by(act, "hq00", "hq01", "hq10", "hq11")
                step(S.activation(hx[0], hb, ACT.Ln), "log_forget")

                def decay_of(n):
                    act.wait_ge(sem("exponent_ready"), n)
                    step(S.activation(hx[n % 2], hx[n % 2], ACT.Exp), "decay_ready", wait=False)

                def late(n):
                    name = ["nq0", "nq1", "kv0", "kv1", "kv2", "ga0", "ga1", "gb0", "gb1"][n]
                    for t in range(TT):
                        if name[0] == "n":
                            dst = nq[:, t, n * 512:n * 512 + 512]
                        elif name[0] == "k":
                            dst = nkv[:, t, (n - 2) * 512:(n - 2) * 512 + 512]
                        else:
                            dst = (mix_a if name[1] == "a" else mix_b)[:, t, (n - 5) % 2 * 512:(n - 5) % 2 * 512 + 512]
                        copy_out(f"{name}{t}", dst)
                    if n == 2:
                        bank = filled_by(act, "sel_gates")
                        drain(S.copy(sel_gates, grid(bank[:, 0:96], TT)), "sel_gates", wait=True)

                late(0)
                for n in range(1, len(LEVELS) + 1):
                    decay_of(n)
                    late(n)
                drained_by(act, *[f"g{b}{c}{t}" for b in "ab" for c in range(2) for t in range(TT)])
                step(S.activation(sel_gates, sel_gates, ACT.Sigmoid), "sel_gates_ready", wait=False)
                step(S.activation(page(16), page(16), ACT.Sigmoid), "mix_gates_ready", wait=False)
                step(S.activation(page(17), page(17), ACT.Sigmoid), "mix_gates_ready", wait=False)
                root(2)
                turned("nqT", nqT)
                turned("nq_rotT", nq_rotT)
                for key, dst in (("ks", ksT), ("kw", kwT)):
                    for f in range(2):
                        bank = filled_by(act, f"{key}T{f}")
                        drain(S.copy(dst[:, 2 * f:2 * f + 2, :], grid(bank, 2)), f"{key}T{f}")
                turned("y_aT", y_aT)
                for s_, key in enumerate("kv"):
                    act.wait_ge(sem("cmp_pe_ready"), s_ + 1)
                    bank = filled_by(act, f"cmp_hid_{key}")
                    for c in range(2):
                        ins = S.activation(cmp_hid[:, s_, c, :], bank[:, c * 64:c * 64 + 4 * N_CMP], ACT.Gelu_apprx_tanh,
                                           bias=cmp_pe[:, 2 * s_ + c:2 * s_ + c + 1])
                    drain(ins, f"cmp_hid_{key}")
                for t in range(TT):
                    act.wait_ge(sem("cmp_shifted"), t + 1)
                    live = cmp_p[:, t, :, 0:N_CMP]
                    step(S.activation(live, live, ACT.Exp), "cmp_exp_ready", wait=False)
                for t in range(TT):
                    bank = filled_by(act, f"cmpT{t}")
                    drain(S.copy(cmp_pT[:, t, :, :], grid(bank, NSA_KV)), f"cmpT{t}")
                for i in range(len(blocks2) + 1):
                    if i < len(blocks2):
                        exponentials(blocks2[i])
                    if i >= 1:
                        probs_turned(blocks2[i - 1])
                turned("y_bT", y_bT)
                turned("mergedT", xT)
                for c in range(2):
                    for t in range(TT):
                        copy_out(f"out2_{c}{t}", mlp_out[:, t, c * 512:c * 512 + 512])
                root(2)
                turned("mlpT", xT, "norm_pre_mlp_2")
                for c in range(8):
                    for f in range(2):
                        k = 4 * (c % 2) + 2 * f
                        bank = filled_by(act, f"up{c}{f}")
                        drain(S.activation(ffT[c // 2][:, k:k + 2, :], grid(bank, 2), ACT.Relu), f"up{c}{f}")
                for c in range(2):
                    for t in range(TT):
                        copy_out(f"down{c}{t}", mlp_out[:, t, c * 512:c * 512 + 512])
                root()
                for c in range(2):
                    for t in range(TT):
                        copy_out(f"ple{c}{t}", ple[:, t, c * 512:c * 512 + 512])
                turned("pleT", xT)
                for c in range(2):
                    for t in range(TT):
                        copy_out(f"ple_gate{c}{t}", ple_gate[:, t, c * 512:c * 512 + 512], ACT.Sigmoid)
                root()
                assert counts["root_ready"] == len(roots)

            @block.gpsimd
            def _(pool):
                with nc.allow_non_contiguous_dma("small weights, read once"):
                    f0 = 3 * D_ATTN
                    pool.dma_start(forget_w[:, :, :], rows(d["w_in"][0], KT)[:, :, f0:f0 + HEADS]).then_inc(sem("forget_landed"), 16)
                    pool.dma_start(forget_b[:, :], d["b_forget"].rearrange("l h -> h l")).then_inc(sem("forget_landed"), 16)
                    pool.dma_start(route_w[:, :, 0:GROUPS], rows(d["w_route_group"][0], KT)).then_inc(sem("route_landed"), 16)
                    for g in range(GROUPS):
                        pool.dma_start(route_w[:, :, 4 + 8 * g:12 + 8 * g], rows(d["w_route_expert"][0, g], KT)).then_inc(sem("route_landed"), 16)
                    pool.dma_start(route_b[:, 0:4], d["b_route_group"][0].partition_broadcast(P)).then_inc(sem("route_landed"), 16)
                    pool.dma_start(route_b[:, 4:36], d["b_route_expert"][0].rearrange("g e -> (g e)").partition_broadcast(P)).then_inc(sem("route_landed"), 16)
                for f in range(2):
                    drained_by(pool, f"conv_a{f}")
                others = range(DVE_CONV, 4)
                for cb in others:
                    nc.gpsimd.tensor_scalar(conv[:, cb, :], z[:, cb, 0:T], tap(0, cb), col("b_dw", cb), ALU.mult, ALU.add).then_inc(sem("pool_added"), 1)
                for w in range(1, TAPS):
                    for n, cb in enumerate(others):
                        nc.gpsimd.tensor_scalar(glu[:, cb, :], z[:, cb, w:w + T], tap(w, cb), None, ALU.mult).then_inc(sem("pool_scaled"), 1)
                    for n, cb in enumerate(others):
                        pool.wait_ge(sem("pool_scaled"), len(others) * (w - 1) + n + 1)
                        pool.wait_ge(sem("pool_added"), len(others) * (w - 1) + n + 1)
                        ins = nc.gpsimd.tensor_tensor(conv[:, cb, :], conv[:, cb, :], glu[:, cb, :], ALU.add)
                        ins.then_inc(sem("conv_pool_ready" if w == TAPS - 1 and cb == 3 else "pool_added"), 1)
                    if w < TAPS - 1:
                        pool.wait_ge(sem("pool_added"), len(others) * (w + 1))
                filled_by(pool, "route")
                pool.dma_start(gain_final, d["final_g"].partition_broadcast(P)).then_inc(sem("final_gain_landed"), 16)
                filled_by(pool, "hq00")
                pool.dma_start(gnorm, d["hg_gnorm_2"][0].partition_broadcast(P)).then_inc(sem("gnorm_landed"), 16)
                pool.dma_start(w_gates, rows(d["w_in_2"][0], KT)[:, :, 6656:6704]).then_inc(sem("gates_landed"), 16)
                with nc.allow_non_contiguous_dma("small weights, read once"):
                    for u in range(2):
                        pool.dma_start(cmp_wk2[:, :, u, :], rows(d["cmp_wk2_2"][0], 2)).then_inc(sem("cmp_w2_landed"), 16)
                    pool.dma_start(cmp_wv2, rows(d["cmp_wv2_2"][0], 2)).then_inc(sem("cmp_w2_landed"), 16)
                pool.wait_ge(sem("y_b_ready"), 1)
                filled_by(pool, "y_bT0")
                for dst, name in ((gain_mix, "norm_post_mix_2"), (gain_mlp, "norm_post_mlp_2"), (gain_ple, "norm_ple_2")):
                    pool.dma_start(dst, d[name][0].partition_broadcast(P)).then_inc(sem("gains_landed"), 16)
                pool.dma_start(p_tok, d["p_2"][0, 0].rearrange("(t p) n -> p t n", p=P)).then_inc(sem("p_landed"), 16)

            @block.sync
            def _(sp):
                sp.dma_start(x, d["x"][0].rearrange("(t p) n -> p t n", p=P)).then_inc(sem("x_landed"), 16)
                sp.dma_start(consts[:, :], d["consts"]).then_inc(sem("consts_landed"), 16)
                row = 0
                for name, n in PARAM_ROWS:
                    v = d[name]
                    src = v.rearrange("l (r a) e -> (l r) (a e)", a=2) if name.startswith("cmp_pe") else v.rearrange("l (r e) -> (l r) e", e=P)
                    sp.dma_start(page(8, 0, P)[row:row + n, :], src).then_inc(sem("params_landed"), 16)
                    row += n
                sp.dma_start(page(8, P, P)[0:4 * TAPS, :], d["w_dw"].rearrange("l w (r e) -> (l w r) e", e=P)).then_inc(sem("params_landed"), 16)

                def load(n):
                    name, src, slot, k, w = units[n]
                    last = [m for m in range(n) if units[m][2] == slot]
                    if last and not (n >= n_early and last[-1] < n_early):
                        done = unit_last_fill[units[last[-1]][0]]
                        if isinstance(done, int):
                            sp.wait_ge(sem("down_used"), done)
                        else:
                            filled_by(sp, done)
                    sp.dma_start(slot_view(slot, k, w), src).then_inc(sem(f"weights_landed{slot}"), 16)

                for n in range(n_early):
                    load(n)
                    if n == 1:
                        sp.dma_start(mem_tok, d["mem"][0].rearrange("(t p) n -> p t n", p=P)).then_inc(sem("mem_landed"), 16)

                wg = d["w_gate"][0].rearrange("e (k p) n -> p e k n", p=P)
                wu = d["w_up"][0].rearrange("e (k p) n -> p e k n", p=P)
                wd = d["w_down"][0].rearrange("e (k p) n -> p e k n", p=P)

                def load_expert(which, e, landed):
                    src = (wg, wu, wd)[which // 2]
                    sp.dma_start(expert_w[which].unsqueeze(1), src[:, bass.ds(e, 1), :, :]).then_inc(landed[expert_slot[which]], 16)

                def load_pairs(tag, n_pairs, landed, first_waits):
                    for which in range(6):
                        first_waits(expert_slot[which])
                        load_expert(which, which % 2, landed)
                    with sp.Fori(1, n_pairs) as i:
                        for which in range(6):
                            sp.wait_ge(sem(f"{tag}_{('gate', 'up', 'down')[which // 2]}_filled"), 2 * i)
                            load_expert(which, 2 * (i % PAIRS) + which % 2, landed)

                def early_done(slot):
                    last = [m for m in range(n_early) if units[m][2] == slot][-1]
                    filled_by(sp, unit_last_fill[units[last][0]])

                def experts_done(tag, n_pairs):
                    for name in ("gate", "up", "down"):
                        sp.wait_ge(sem(f"{tag}_{name}_filled"), 2 * n_pairs)

                load_pairs("moe", PAIRS, [sem(f"weights_landed{b}") for b in range(6)], early_done)
                sp.wait_ge(sem("busiest_ready"), 1)
                count = sp.value_load(busiest[0:1, 0:1], min_val=0, max_val=T)
                experts_done("moe", PAIRS)
                with sp.If(count > CAP):
                    load_pairs("more", MORE, [sem(f"more_landed{b}") for b in range(6)], lambda slot: None)
                    experts_done("more", MORE)
                for n in range(n_early, len(units)):
                    load(n)
                for t in range(TT):
                    sp.wait_ge(sem("result_ready"), t + 1)
                    sp.dma_start(out[0, t * P:t * P + P, :], x[:, t, :]).then_inc(sem("out_stored"), 16)
                sp.wait_ge(sem("out_stored"), 16 * TT)


_INPUTS = ["x", "mem", "norm_mix_g", "w_in", "b_forget", "b_glu", "w_dw", "b_dw", "conv_ln_g", "conv_ln_b", "attn_out_g",
           "w_out", "norm_mem_g", "mem_norm_g", "w_mq", "w_mkv", "w_mo", "norm_ffn_g", "w_route_group", "b_route_group",
           "w_route_expert", "b_route_expert", "w_gate", "w_up", "w_down", "final_g", "p_2", "w_in_2", "w_branch_a_2",
           "w_branch_b_2", "w_out_2", "norm_pre_mix_2", "norm_post_mix_2", "norm_pre_mlp_2", "norm_post_mlp_2",
           "hg_lb_logits_2", "hg_gnorm_2", "cmp_pe_k_2", "cmp_pe_v_2", "cmp_wk1_2", "cmp_wk2_2", "cmp_wv1_2", "cmp_wv2_2",
           "w_up_2", "w_down_2", "w_ple_2", "w_ple_gate_2", "norm_ple_2"]


def kernel(**inputs):
    import concourse.bacc as bacc
    from concourse.bass_utils import run_bass_kernel_spmd

    nc = bacc.Bacc("TRN2", target_bir_lowering=False, num_devices=1)
    arrays, d = {}, {}
    for name in _INPUTS:
        a = np.ascontiguousarray(inputs[name])
        arrays[f"in_{name}"] = a
        d[name] = nc.dram_tensor(f"in_{name}", a.shape, mybir.dt.from_np(a.dtype), kind="ExternalInput").ap()
    table, const_cols = shape_constants()
    arrays["in_consts"] = table
    d["consts"] = nc.dram_tensor("in_consts", table.shape, F32, kind="ExternalInput").ap()
    out = nc.dram_tensor("out", (1, T, D), F32, kind="ExternalOutput").ap()
    two_blocks_kernel(nc, d, const_cols, out)
    r = run_bass_kernel_spmd(nc, [arrays], core_ids=[0])
    return r.results[0]["out"]
```

```python
from contextlib import ExitStack

import numpy as np
import concourse.bass as bass
from concourse import mybir

F32 = mybir.dt.float32
I32 = mybir.dt.int32
U32 = mybir.dt.uint32
ALU = mybir.AluOpType
ACT = mybir.ActivationFunctionType
AX = mybir.AxisListType

P = 128
T, D = 256, 1024
TT, KT = T // P, D // P
EPS = 1e-6
BIG = 1e30
HEADS, HEAD_DIM = 8, 64
D_ATTN = HEADS * HEAD_DIM
D_CONV = D - D_ATTN
TAPS = 31
MEM_HEADS, MEM_DIM = 4, 256
GROUPS, PER_GROUP = 4, 8
EXPERTS = GROUPS * PER_GROUP
D_EXPERT = 512
CAP = 64
PASSES = T // CAP
PAIRS = EXPERTS // 2
MORE = PAIRS * (PASSES - 1)
HG_HEADS, CHUNK = 8, 64
NSA_HEADS, NSA_KV, NSA_DH = 16, 4, 64
CMP_LEN, CMP_STRIDE = 32, 16
N_CMP = (T - CMP_LEN) // CMP_STRIDE + 1
CMP_HIDDEN = 256
ROPE_DIM, ROPE_THETA = 16, 500000.0
D_FF = 4 * D
BANKS = 8
SLOT = 4096
PAGE = 2048
HEAD_OF = [0, 2, 4, 6, 1, 3, 5, 7]
DVE_CONV = 3
LEVELS = [1, 2, 4, 8, 16, 32, 64, 128]

PARAM_ROWS = [("norm_mix_g", 8), ("norm_mem_g", 8), ("mem_norm_g", 8), ("norm_ffn_g", 8),
              ("norm_pre_mix_2", 8), ("norm_pre_mlp_2", 8), ("attn_out_g", 4), ("b_glu", 8),
              ("b_dw", 4), ("conv_ln_g", 4), ("conv_ln_b", 4), ("hg_lb_logits_2", 16),
              ("cmp_pe_k_2", 16), ("cmp_pe_v_2", 16)]


def shape_constants():
    cols, parts = {}, []

    def put(name, a):
        a = np.asarray(a, np.float32).reshape(P, -1)
        start = sum(x.shape[1] for x in parts)
        cols[name] = (start, start + a.shape[1])
        parts.append(a)

    p = np.arange(P)
    put("ident", np.eye(P))
    put("ones", np.ones((P, T)))
    put("causal", np.concatenate([np.zeros((P, P)), np.where(p[None, :] <= p[:, None], 0.0, -BIG)], 1))
    put("earlier", p[:, None] < p[None, :])
    for L in LEVELS[:-1]:
        same = p[:, None] // (2 * L) == p[None, :] // (2 * L)
        put(f"level{L}", same & (p[:, None] // L % 2 == 0) & (p[None, :] // L % 2 == 1))
    put("chunk_reset", np.tile(np.arange(T) % CHUNK != 0, (P, 1)))
    put("slots", np.tile(np.arange(T + CAP), (P, 1)))
    half = ROPE_DIM // 2
    inv = (ROPE_THETA ** (-np.arange(half) * 2.0 / ROPE_DIM)).astype(np.float32)
    angle = np.arange(T, dtype=np.float32)[:, None] * inv[None, :]
    to_half = lambda a: a.reshape(TT, P, -1).transpose(1, 0, 2)
    put("cos", to_half(np.cos(angle)))
    put("sin", to_half(np.sin(angle)))
    end = np.arange(N_CMP) * CMP_STRIDE + CMP_LEN - 1
    seen = to_half((end[None, :] <= np.arange(T)[:, None]).astype(np.float32))
    put("cmp_seen", seen)
    put("cmp_bias", (seen - 1.0) * np.float32(BIG))
    return np.concatenate(parts, 1), cols


def two_blocks_kernel(nc, d, const_cols, out):
    ctx = ExitStack()
    with ctx:
        sb = lambda name, shape, dt=F32: ctx.enter_context(nc.sbuf_tensor(name, shape, dt))
        n_const = d["consts"].shape[1]
        ring = sb("ring", [P, 6 * SLOT])
        arena = sb("arena", [P, 12 * PAGE])
        consts = sb("consts", [P, n_const])
        cols = sb("cols", [P, 256])
        small = sb("small", [P, 512])
        route_w = sb("route_w", [P, KT, 36])
        route_b = sb("route_b", [P, 36])
        forget_w = sb("forget_w", [P, KT, HEADS])
        forget_b = sb("forget_b", [HEADS, 1])
        pos = sb("pos", [P, TT, EXPERTS])
        gate = sb("gate", [P, TT, EXPERTS])
        busiest = sb("busiest", [P, 1], I32)
        ps = ctx.enter_context(nc.psum_tensor("ps", [P, BANKS, 512], F32))

        sems = {}

        def sem(name):
            if name not in sems:
                sems[name] = ctx.enter_context(nc.semaphore(name))
            return sems[name]

        for b in range(BANKS):
            sem(f"bank_filled{b}"), sem(f"bank_drained{b}")

        def page(i, start=0, size=PAGE):
            if i < 12:
                return arena[:, i * PAGE + start:i * PAGE + start + size]
            at = 3 * SLOT + (i - 12) * PAGE
            return ring[:, at + start:at + start + size]

        def grid(flat, a):
            return flat.rearrange("p (a b) -> p a b", a=a)

        def const(name):
            a, b = const_cols[name]
            return consts[:, a:b]

        ident = const("ident")
        param_col, at = {}, 0
        for name, n in PARAM_ROWS:
            param_col[name] = at
            at += n
        n_rows = at

        def col(name, k=0, n=1):
            return cols[:, param_col[name] + k:param_col[name] + k + n]

        def tap(w, cb):
            k = P + w * 4 + cb
            return cols[:, k:k + 1]

        x = grid(page(0), TT)
        normed = grid(page(1), TT)
        xT = grid(page(2), KT)
        qk1 = page(3)
        qT1, kT1 = grid(qk1[:, 0:1024], 4), grid(qk1[:, 1024:2048], 4)
        memT = grid(page(11), KT)
        mem_k, mem_v = grid(page(4), KT), grid(page(5), TT)
        mem_tok = grid(page(9), TT)
        mem_normed = grid(page(10), TT)
        v1 = grid(page(6, 0, 1024), TT)
        glu = grid(page(6, 1024, 1024), 4)
        ZW = TAPS - 1 + T
        z = grid(page(7, 0, 4 * ZW), 4)
        attn1 = grid(page(8, 1024, 1024), TT)
        conv = grid(page(8, 0, 1024), 4)
        catT = grid(page(2), KT)
        decay = page(7, 4 * ZW, 512)
        log_f, key_bias = decay[0:HEADS, 0:256], decay[0:HEADS, 256:512]
        qT2 = grid(page(3), KT)
        prob2 = page(6).rearrange("p (t h m) -> p t h m", t=TT, h=MEM_HEADS)
        prob2T = page(7).rearrange("p (h m q) -> p h m q", h=MEM_HEADS, m=TT)
        oT2 = grid(page(8), KT)
        logits = grid(page(6, 0, 72), TT)
        scratch_route = page(6, 128, 1920)
        picked = grid(page(3, 0, 1024), KT)
        choose = grid(page(3, 1024, 256), TT)
        choose_gated = grid(page(3, 1280, 256), TT)
        spread = page(3, 1536, 256)
        hidden = page(4, 0, D_EXPERT)
        hiddenT = grid(page(4, 512, 512), 4)
        expert_out = page(4, 1024, 1024)
        hq, hb, hk = page(3), page(4), page(5)
        hx = [page(6), page(7)]
        scores_diag, scores_cross = page(8), page(9, 0, 1024)
        hv, hg = grid(page(10), TT), grid(page(11), TT)
        gnorm = page(9, 1024, 128)
        w_gates = page(9, 1152, KT * 48).rearrange("p (k n) -> p k n", k=KT)
        sel_gates = grid(page(9, 1536, 96), TT)
        nq, nq_rot = grid(page(12), TT), grid(page(13), TT)
        nkv = ring[:, 3 * SLOT + 2 * PAGE:3 * SLOT + 2 * PAGE + TT * 1536].rearrange("p (t n) -> p t n", t=TT)
        mix_a, mix_b = grid(page(16), TT), grid(page(17), TT)
        nqT, nq_rotT = grid(page(3), KT), grid(page(4), KT)
        ksT, kwT = grid(page(5, 0, 1024), 4), grid(page(5, 1024, 1024), 4)
        windows = page(7, 0, 4 * 4 * N_CMP * 8).rearrange("p (s b m j) -> p s b m j", s=2, b=2, j=8)
        y_b = grid(page(1), TT)
        y_aT = grid(page(11), KT)
        y_bT = grid(page(2), KT)
        cmp_p = page(9, 0, 1024).rearrange("p (t h n) -> p t h n", t=TT, h=NSA_HEADS)
        cmp_pT = page(13, 0, 1024).rearrange("p (t g q) -> p t g q", t=TT, g=NSA_KV)
        CMP = page(15)
        cmp_wk2 = CMP[:, 1024:1280].rearrange("p (c u n) -> p c u n", c=2, u=2)
        cmp_wv2 = CMP[:, 1280:1408].rearrange("p (c n) -> p c n", c=2)
        cmp_hid = CMP[:, 1408:1664]
        cmp_hidT = CMP[:, 1664:1920].rearrange("p (c n) -> p c n", c=2)
        cmp_kT = CMP[:, 1920:1980]
        cmp_v = page(13, 1024, 1024).rearrange("p (g n) -> p g n", g=NSA_KV)
        ffT = [grid(page(3 + n), KT) for n in range(4)]
        mlp_out = grid(page(7), TT)
        p_tok = grid(page(8, 0, 512), TT)
        pT = grid(page(8, 512, 512), TT)
        ple = grid(page(9), TT)
        ple_gate = grid(page(10), TT)
        gain_final, gain_mix = page(5, 0, 1024), page(12, 0, 1024)
        gain_mlp, gain_ple = page(12, 1024, 1024), page(13, 0, 1024)

        rows = lambda w, k: w.rearrange("(k p) n -> p k n", k=k)
        units, unit_at = [], {}

        def unit(name, src, k, n, n_slots):
            slot = len(units) % n_slots if n_slots == 6 else (len(units) - first_late) % 3
            unit_at[name] = (len(units), slot, k, n)
            units.append((name, src, slot, k, n))

        off_c = 3 * D_ATTN + HEADS
        for name, start in (("conv_g", off_c + D_CONV), ("conv_a", off_c), ("q", 0), ("k", D_ATTN), ("v", 2 * D_ATTN)):
            unit(name, rows(d["w_in"][0], KT)[:, :, start:start + 512], KT, 512, 6)
        for c in range(4):
            unit(f"mem_kv{c}", rows(d["w_mkv"][0], KT)[:, :, c * 512:c * 512 + 512], KT, 512, 6)
        for key, w in (("out", "w_out"), ("mem_q", "w_mq"), ("mem_o", "w_mo")):
            for c in range(2):
                unit(f"{key}{c}", rows(d[w][0], KT)[:, :, c * 512:c * 512 + 512], KT, 512, 6)
        n_early = len(units)
        expert_slot = [(n_early + n) % 6 for n in range(6)]
        first_late = n_early
        off = [0, 512, 1024, 1536, 2048, 2560, 3072, 3584, 4096, 4608, 5120, 5632, 6144, 6704, 7216, 7728, 8240]
        names2 = ["hq0", "hq1", "hf0", "hf1", "hi0", "hi1", "hg0", "hg1", "nq0", "nq1",
                  "kv0", "kv1", "kv2", "ga0", "ga1", "gb0", "gb1"]
        for name, start in zip(names2, off):
            unit(name, rows(d["w_in_2"][0], KT)[:, :, start:start + 512], KT, 512, 3)
        for c in "kv":
            unit(f"cmp_{c}", rows(d[f"cmp_w{c}1_2"][0], 16), 16, CMP_HIDDEN, 3)
        for c in range(2):
            unit(f"branch_a{c}", rows(d["w_branch_a_2"][0], KT)[:, :, c * 512:c * 512 + 512], KT, 512, 3)
        for key, w in (("branch_b", "w_branch_b_2"), ("out2_", "w_out_2")):
            for c in range(2):
                unit(f"{key}{c}", rows(d[w][0], KT)[:, :, c * 512:c * 512 + 512], KT, 512, 3)
        for c in range(8):
            unit(f"up{c}", rows(d["w_up_2"][0], KT)[:, :, c * 512:c * 512 + 512], KT, 512, 3)
        for c in range(2):
            for k in range(4):
                unit(f"down{c}{k}", rows(d["w_down_2"][0][k * D:k * D + D], KT)[:, :, c * 512:c * 512 + 512], KT, 512, 3)
        unit("ple", rows(d["w_ple_2"][0], 2), 2, D, 3)
        for c in range(2):
            unit(f"ple_gate{c}", rows(d["w_ple_gate_2"][0], KT)[:, :, c * 512:c * 512 + 512], KT, 512, 3)

        landed_value, loads = {}, [0] * 6
        for n, (name, _, slot, _, _) in enumerate(units):
            if n == n_early:
                before_experts = list(loads)
                loads = [v + 16 * PAIRS for v in loads]
            loads[slot] += 16
            landed_value[name] = loads[slot]

        def slot_view(slot, k, n):
            return ring[:, slot * SLOT:slot * SLOT + k * n].rearrange("p (k n) -> p k n", k=k)

        expert_w = [slot_view(expert_slot[n], *((KT, 512) if n < 4 else (4, 1024))) for n in range(6)]

        fills, unit_last_fill = {}, {}

        def filled_by(eng, name):
            n = fills[name]
            eng.wait_ge(sem(f"bank_filled{n % BANKS}"), n // BANKS + 1)
            return ps[:, n % BANKS, :]

        def drained_by(eng, *names):
            for name in names:
                n = fills[name]
                eng.wait_ge(sem(f"bank_drained{n % BANKS}"), n // BANKS + 1)

        blocks1 = [dict(name=f"fa{t}", t=t, nk=P * (t + 1), n=t, scale=HEAD_DIM ** -0.5,
                        p=page(9 + t, 0, HEADS * P * (t + 1)).rearrange("p (h k) -> p h k", h=HEADS),
                        pt=(page(9, 1024, 1024) if t == 0 else page(1)).rearrange("p (n q) -> p n q", q=P),
                        q=lambda h, t=t: qT1[64 * (h % 2):64 * (h % 2) + 64, h // 2, t * P:t * P + P],
                        k=lambda h, nk: kT1[64 * (h % 2):64 * (h % 2) + 64, h // 2, 0:nk],
                        v=lambda h, j: v1[:, j, h * 64:h * 64 + 64], bias=True) for t in range(TT)]
        blocks2 = []
        for branch, (kT, v0) in enumerate(((ksT, 768), (kwT, 1280))):
            for t in range(TT):
                for half in range(2):
                    n = len(blocks2)
                    blocks2.append(dict(
                        name=f"nsa{branch}{t}{half}", t=t, nk=P * (t + 1), n=2 + n, scale=1.0, branch=branch, half=half,
                        p=page((6, 7, 10)[n % 3], 0, HEADS * P * (t + 1)).rearrange("p (h k) -> p h k", h=HEADS),
                        pt=page((8, 12)[n % 2], 0, HEADS * P * (t + 1)).rearrange("p (n q) -> p n q", q=P),
                        q=lambda h, t=t, half=half: nq_rotT[64 * (h % 2):64 * (h % 2) + 64, 4 * half + h // 2, t * P:t * P + P],
                        k=lambda h, nk, kT=kT, half=half: kT[64 * (h % 2):64 * (h % 2) + 64, 2 * half + h // 4, 0:nk],
                        v=lambda h, j, v0=v0, half=half: nkv[:, j, v0 + (2 * half + h // 4) * 64:v0 + (2 * half + h // 4) * 64 + 64],
                        bias=False))

        def stat(k, n):
            return small[:, k:k + n]

        def block_stats(blk):
            return [stat(64 + 24 * blk["n"] + 8 * j, 8) for j in range(3)]

        with nc.Block() as block:

            @block.tensor
            def _(pe):
                def open_bank(name):
                    n = fills[name] = len(fills)
                    if n >= BANKS:
                        pe.wait_ge(sem(f"bank_drained{n % BANKS}"), n // BANKS)
                    return ps[:, n % BANKS, :]

                def close_bank(ins, name):
                    ins.then_inc(sem(f"bank_filled{fills[name] % BANKS}"), 1)

                def use(name):
                    _, slot, k, n = unit_at[name]
                    pe.wait_ge(sem(f"weights_landed{slot}"), landed_value[name])
                    return slot_view(slot, k, n)

                def feature_major(name, tag, rhs):
                    w = use(name)
                    for c in range(2):
                        bank = open_bank(f"{tag}{c}")
                        for half in range(2):
                            at = (2 * c + half) * P
                            for k in range(KT):
                                mm = nc.tensor.matmul(bank[:, half * T:half * T + T], w[:, k, at:at + P], rhs[:, k, :],
                                                      start=k == 0, stop=k == KT - 1)
                        close_bank(mm, f"{tag}{c}")
                    unit_last_fill[name] = f"{tag}1"

                def token_major(name, tag, lhs):
                    w = use(name)
                    for t in range(TT):
                        bank = open_bank(f"{tag}{t}")
                        for k in range(KT):
                            mm = nc.tensor.matmul(bank, lhs[:, k, t * P:t * P + P], w[:, k, :],
                                                  start=k == 0, stop=k == KT - 1)
                        close_bank(mm, f"{tag}{t}")
                    unit_last_fill[name] = f"{tag}1"

                def transposes(tag, src):
                    for j in range(4):
                        bank = open_bank(f"{tag}{j}")
                        for k in (2 * j, 2 * j + 1):
                            for t in range(TT):
                                at = (k % 2) * T + t * P
                                mm = nc.tensor.transpose(bank[:, at:at + P], src[:, t, k * P:k * P + P], ident)
                        close_bank(mm, f"{tag}{j}")

                def turn_half(tag, src, t):
                    for f in range(2):
                        bank = open_bank(f"{tag}{t}{f}")
                        for j in range(4):
                            k = 4 * f + j
                            mm = nc.tensor.transpose(bank[:, j * P:j * P + P], src[:, t, k * P:k * P + P], ident)
                        close_bank(mm, f"{tag}{t}{f}")

                def half_turned(tag, t):
                    drained_by(pe, f"{tag}{t}0", f"{tag}{t}1")

                def token_pair(names, lhs, before_part):
                    w = [use(name) for name in names]
                    for t in range(TT):
                        for c, name in enumerate(names):
                            if (t, c) in before_part:
                                before_part[t, c]()
                            bank = open_bank(f"{name}{t}")
                            for k in range(KT):
                                mm = nc.tensor.matmul(bank, lhs[:, k, t * P:t * P + P], w[c][:, k, :], start=k == 0, stop=k == KT - 1)
                            close_bank(mm, f"{name}{t}")
                    for name in names:
                        unit_last_fill[name] = f"{name}1"

                def feature_pair(names, rhs, turn_second, second_turned):
                    w = [use(names[0])]
                    banks = {}
                    for t in range(TT):
                        for u, name in enumerate(names):
                            if t == 0 and u == 1:
                                turn_second()
                                w.append(use(name))
                            if t == 1 and u == 0:
                                second_turned()
                            for c in range(2):
                                if t == 0:
                                    banks[u, c] = open_bank(f"{name}{c}")
                                for half in range(2):
                                    at, to = (2 * c + half) * P, half * T + t * P
                                    for k in range(KT):
                                        mm = nc.tensor.matmul(banks[u, c][:, to:to + P], w[u][:, k, at:at + P], rhs[:, k, t * P:t * P + P],
                                                              start=k == 0, stop=k == KT - 1)
                                if t == 1:
                                    close_bank(mm, f"{name}{c}")
                    for name in names:
                        unit_last_fill[name] = f"{name}1"

                def normed_half(tag, t, count):
                    pe.wait_ge(sem("x_normed"), count)
                    turn_half(tag, normed, t)

                def scores(blk):
                    nk = blk["nk"]
                    per = 512 // nk
                    for f in range(HEADS // per):
                        name = f"{blk['name']}S{f}"
                        bank = open_bank(name)
                        for j in range(per):
                            h = HEAD_OF[f * per + j]
                            o = bank[:, j * nk:j * nk + nk]
                            mm = nc.tensor.matmul(o, blk["q"](h), blk["k"](h, nk), start=True, stop=not blk["bias"])
                            if blk["bias"]:
                                mm = nc.tensor.matmul(o, ident[0:HEADS, h:h + 1].to_broadcast([HEADS, P]),
                                                      key_bias[:, 0:nk], start=False, stop=True)
                        close_bank(mm, name)

                def turn_probs(blk):
                    pe.wait_ge(sem("probs_ready"), blk["n"] + 1)
                    tiles = HEADS * blk["nk"] // P
                    flat = blk["p"].rearrange("p h (j k) -> p (h j) k", k=P)
                    for f in range(tiles // 4):
                        name = f"{blk['name']}T{f}"
                        bank = open_bank(name)
                        for j in range(4):
                            mm = nc.tensor.transpose(bank[:, j * P:j * P + P], flat[:, 4 * f + j, :], ident)
                        close_bank(mm, name)

                def weigh_values(blk):
                    nj = blk["nk"] // P
                    drained_by(pe, *[f"{blk['name']}T{f}" for f in range(HEADS * nj // 4)])
                    bank = open_bank(f"{blk['name']}O")
                    for n, h in enumerate(HEAD_OF):
                        for j in range(nj):
                            mm = nc.tensor.matmul(bank[:, h * 64:h * 64 + 64], blk["pt"][:, n * nj + j, :], blk["v"](h, j),
                                                  start=j == 0, stop=j == nj - 1)
                    close_bank(mm, f"{blk['name']}O")

                pe.wait_ge(sem("consts_landed"), 16)
                pe.wait_ge(sem("params_landed"), 16 * (len(PARAM_ROWS) + 1))
                bank = open_bank("params")
                nc.tensor.transpose(bank[:, 0:n_rows], page(8, 0, P)[0:n_rows, :], ident[0:n_rows, 0:n_rows])
                close_bank(nc.tensor.transpose(bank[:, P:P + 4 * TAPS], page(8, P, P)[0:4 * TAPS, :],
                                               ident[0:4 * TAPS, 0:4 * TAPS]), "params")
                normed_half("mixT", 0, 1)
                half_turned("mixT", 0)
                feature_pair(["conv_g", "conv_a"], xT, lambda: normed_half("mixT", 1, 2), lambda: half_turned("mixT", 1))
                feature_major("q", "q", xT)
                feature_major("k", "k", xT)
                pe.wait_ge(sem("forget_landed"), 32)
                bank = open_bank("forget")
                for k in range(KT):
                    mm = nc.tensor.matmul(bank[0:HEADS, 0:T], forget_w[:, k, :], xT[:, k, :], start=k == 0, stop=k == KT - 1)
                close_bank(mm, "forget")
                token_major("v", "v", xT)
                pe.wait_ge(sem("mem_normed"), 2)
                transposes("memT", mem_normed)
                drained_by(pe, *[f"memT{j}" for j in range(4)])
                for c in range(2):
                    feature_major(f"mem_kv{c}", f"mem_k{c}", memT)
                pe.wait_ge(sem("key_bias_ready"), 1)
                drained_by(pe, "q0", "q1", "k0", "k1", "v0", "v1")
                for blk in blocks1:
                    scores(blk)
                token_major("mem_kv2", "mem_v0", memT)
                for blk in blocks1:
                    turn_probs(blk)
                def channel_sums(name, src):
                    bank = open_bank(name)
                    for cb in range(4):
                        mm = nc.tensor.matmul(bank[:, 0:T], const("ones")[:, 0:P], src[:, cb, :], start=cb == 0, stop=cb == 3)
                    close_bank(mm, name)

                pe.wait_ge(sem("conv_ready"), 1)
                pe.wait_ge(sem("conv_pool_ready"), 1)
                channel_sums("conv_mean", conv)
                for blk in blocks1:
                    weigh_values(blk)
                pe.wait_ge(sem("conv_ready"), 2)
                channel_sums("conv_var", glu)
                token_major("mem_kv3", "mem_v1", memT)
                for t in range(TT):
                    pe.wait_ge(sem("attn1_normed"), t + 1)
                    bank = open_bank(f"attn1T{t}")
                    for k in range(4):
                        mm = nc.tensor.transpose(bank[:, k * P:k * P + P], attn1[:, t, k * P:k * P + P], ident)
                    close_bank(mm, f"attn1T{t}")
                drained_by(pe, "attn1T0", "attn1T1")
                pe.wait_ge(sem("conv_done"), 4)
                token_pair(["out0", "out1"], catT, {(1, 1): lambda: normed_half("normT", 0, 3)})
                half_turned("normT", 0)
                feature_pair(["mem_q0", "mem_q1"], xT, lambda: normed_half("normT", 1, 4), lambda: half_turned("normT", 1))
                drained_by(pe, "mem_q00", "mem_q01", "mem_q10", "mem_q11")
                for t in range(TT):
                    for f in range(2):
                        bank = open_bank(f"crossS{t}{f}")
                        for j in range(2):
                            h = 2 * f + j
                            for c in range(2):
                                mm = nc.tensor.matmul(bank[:, j * T:j * T + T], qT2[:, 2 * h + c, t * P:t * P + P],
                                                      mem_k[:, 2 * h + c, :], start=c == 0, stop=c == 1)
                        close_bank(mm, f"crossS{t}{f}")
                for t in range(TT):
                    pe.wait_ge(sem("cross_probs_ready"), t + 1)
                    for f in range(2):
                        bank = open_bank(f"crossT{t}{f}")
                        for j in range(4):
                            h, m = 2 * f + j // 2, j % 2
                            mm = nc.tensor.transpose(bank[:, j * P:j * P + P], prob2[:, t, h, m * P:m * P + P], ident)
                        close_bank(mm, f"crossT{t}{f}")
                drained_by(pe, "crossT00", "crossT01", "crossT10", "crossT11")
                for f in range(4):
                    bank = open_bank(f"crossO{f}")
                    for c in range(2):
                        for m in range(TT):
                            mm = nc.tensor.matmul(bank[:, c * T:c * T + T], mem_v[:, m, (2 * f + c) * P:(2 * f + c) * P + P],
                                                  prob2T[:, f, m, :], start=m == 0, stop=m == TT - 1)
                    close_bank(mm, f"crossO{f}")
                drained_by(pe, *[f"crossO{f}" for f in range(4)])
                def route(t):
                    half_turned("ffnT", t)
                    bank = open_bank(f"route{t}")
                    for k in range(KT):
                        mm = nc.tensor.matmul(bank[:, 0:36], xT[:, k, t * P:t * P + P], route_w[:, k, :], start=k == 0, stop=k == KT - 1)
                    close_bank(mm, f"route{t}")

                def route_first():
                    normed_half("ffnT", 0, 5)
                    pe.wait_ge(sem("route_landed"), 16 * (GROUPS + 3))
                    route(0)

                token_pair(["mem_o0", "mem_o1"], oT2, {(1, 1): route_first})
                normed_half("ffnT", 1, 6)
                route(1)
                pe.wait_ge(sem("choice_ready"), 1)
                chosen = grid(scratch_route[:, 0:64], TT)
                bank = open_bank("rank")
                ones = const("ones")[:, 0:P]
                nc.tensor.matmul(bank[:, 0:32], const("earlier"), chosen[:, 0, :], start=True, stop=True)
                nc.tensor.matmul(bank[:, 32:64], const("earlier"), chosen[:, 1, :], start=True, stop=False)
                nc.tensor.matmul(bank[:, 32:64], ones, chosen[:, 0, :], start=False, stop=True)
                nc.tensor.matmul(bank[:, 64:96], ones, chosen[:, 0, :], start=True, stop=False)
                close_bank(nc.tensor.matmul(bank[:, 64:96], ones, chosen[:, 1, :], start=False, stop=True), "rank")

                def experts(tag, n_pairs, landed_sems, landed_base):
                    s = lambda name: sem(f"{tag}_{name}")

                    def gather(n, first=False):
                        pe.wait_ge(s("choose_ready"), n + 1)
                        for f, b in ((0, 0), (1, 7)):
                            if not first:
                                pe.wait_ge(s("picked_drained"), 2 * n - 1 + f)
                            for k in range(4 * f, 4 * f + 4):
                                for t in range(TT):
                                    mm = nc.tensor.matmul(ps[:, b, (k % 4) * P:(k % 4) * P + P], normed[:, t, k * P:k * P + P],
                                                          choose[:, t, :], start=t == 0, stop=t == TT - 1)
                            mm.then_inc(s("picked_filled"), 1)

                    def product(n, first, tiles, name):
                        for e in range(2):
                            slot = expert_slot[first + e]
                            pe.wait_ge(landed_sems[slot], landed_base[slot] + (n + 1) * 16)
                        w, src = expert_w[first:first + 2], hiddenT if first == 4 else picked
                        n_k = src.shape[1]
                        for c, bank in enumerate(tiles):
                            for k in range(n_k):
                                for e in range(2):
                                    mm = nc.tensor.matmul(ps[e * CAP:e * CAP + CAP, bank, :], src[:, k, e * CAP:e * CAP + CAP],
                                                          w[e][:, k, c * 512:c * 512 + 512], start=k == 0, stop=k == n_k - 1)
                                    if c == len(tiles) - 1 and k == n_k - 1:
                                        mm.then_inc(s(name), 1)

                    def scatter(n):
                        pe.wait_ge(s("spread_ready"), n + 1)
                        pe.wait_ge(s("out_ready"), 2 * n + 2)
                        for t in range(TT):
                            for c in range(2):
                                if t:
                                    pe.wait_ge(s("sum_drained"), 4 * n + c + 1)
                                nc.tensor.matmul(ps[:, 5 + c, :], spread[:, t * P:t * P + P],
                                                 expert_out[:, c * 512:c * 512 + 512], start=True, stop=True).then_inc(s("sum_filled"), 1)

                    gather(0, first=True)
                    with pe.Fori(0, n_pairs) as n:
                        pe.wait_ge(s("picked_drained"), 2 * n + 2)
                        product(n, 0, [1], "gate_filled")
                        scatter(n)
                        product(n, 2, [2], "up_filled")
                        gather(n + 1)
                        pe.wait_ge(s("hidden_ready"), n + 1)
                        for k in range(4):
                            mm = nc.tensor.transpose(ps[:, 1, k * P:k * P + P], hidden[:, k * P:k * P + P], ident)
                        mm.then_inc(s("hidden_turned"), 1)
                        pe.wait_ge(s("gated_choose_ready"), n + 1)
                        pe.wait_ge(s("sum_drained"), 4 * n + 4)
                        for t in range(TT):
                            mm = nc.tensor.transpose(ps[:, 5, t * P:t * P + P], choose_gated[:, t, :], ident)
                        mm.then_inc(s("spread_filled"), 1)
                        pe.wait_ge(s("hiddenT_ready"), n + 1)
                        product(n, 4, [3, 4], "down_filled")
                    scatter(n_pairs)
                    pe.wait_ge(s("sum_drained"), 4 * n_pairs + 4)

                for b in range(BANKS):
                    pe.wait_ge(sem(f"bank_drained{b}"), len([v for v in fills.values() if v % BANKS == b]))
                landed = [sem(f"weights_landed{b}") for b in range(6)]
                experts("moe", PAIRS, landed, before_experts)
                pe.wait_ge(sem("busiest_ready"), 1)
                count = pe.value_load(busiest[0:1, 0:1], min_val=0, max_val=T)
                with pe.If(count > CAP):
                    experts("more", MORE, [sem(f"more_landed{b}") for b in range(6)], [0] * 6)

                normed_half("mix2T", 0, 7)
                half_turned("mix2T", 0)
                feature_pair(["hq0", "hq1"], xT, lambda: normed_half("mix2T", 1, 8), lambda: half_turned("mix2T", 1))
                for c in range(2):
                    feature_major(f"hf{c}", f"hf{c}", xT)
                for c in range(2):
                    token_major(f"hi{c}", f"hi{c}", xT)
                for c in range(2):
                    token_major(f"hg{c}", f"hg{c}", xT)

                def level(n):
                    pe.wait_ge(sem("level_ready"), n + 1)
                    if n and LEVELS[n - 1] == P:
                        src = grid(hx[n % 2], HG_HEADS)
                        for f in range(2):
                            bank = open_bank(f"level{n}_{f}")
                            for j in range(4):
                                h = 4 * f + j
                                mm = nc.tensor.matmul(bank[:, j * P:j * P + P], src[:, h, 0:P], src[:, h, P:T], start=True, stop=True)
                            close_bank(mm, f"level{n}_{f}")
                        return
                    left, right = (grid(hk, HG_HEADS), grid(hq, HG_HEADS)) if n == 0 else [grid(hx[n % 2], HG_HEADS)] * 2
                    for f in range(4):
                        bank = open_bank(f"level{n}_{f}")
                        for j in range(4):
                            h, t = 2 * f + j // 2, j % 2
                            mm = nc.tensor.matmul(bank[:, j * P:j * P + P], left[:, h, t * P:t * P + P], right[:, h, t * P:t * P + P],
                                                  start=True, stop=True)
                        close_bank(mm, f"level{n}_{f}")

                late = ["nq0", "nq1", "kv0", "kv1", "kv2", "ga0", "ga1", "gb0", "gb1"]
                for n in range(len(LEVELS) + 1):
                    token_major(late[n], late[n], xT)
                    if n == 2:
                        pe.wait_ge(sem("gates_landed"), 16)
                        bank = open_bank("sel_gates")
                        for t in range(TT):
                            for k in range(KT):
                                mm = nc.tensor.matmul(bank[:, t * 48:t * 48 + 48], xT[:, k, t * P:t * P + P], w_gates[:, k, :],
                                                      start=k == 0, stop=k == KT - 1)
                        close_bank(mm, "sel_gates")
                    level(n)
                def both_halves(key, start):
                    for f in range(2):
                        bank = open_bank(f"{key}T{f}")
                        for j in range(2):
                            g = 2 * f + j
                            for t in range(TT):
                                for u in range(2):
                                    mm = nc.tensor.matmul(bank[64 * u:64 * u + 64, j * T + t * P:j * T + t * P + P],
                                                          nkv[:, t, start + g * 64:start + g * 64 + 64], ident, start=True, stop=True)
                        close_bank(mm, f"{key}T{f}")

                drained_by(pe, *[f"{u}{t}" for u in ("nq0", "nq1", "kv0") for t in range(TT)])
                both_halves("kc", 0)
                both_halves("vc", 256)
                transposes("nqT", nq)
                pe.wait_ge(sem("rotated"), 3 * TT)
                transposes("nq_rotT", nq_rot)
                both_halves("ks", 512)
                both_halves("kw", 1024)
                drained_by(pe, *[f"level{len(LEVELS)}_{f}" for f in range(2)])
                drained_by(pe, *[f"hi{c}{t}" for c in range(2) for t in range(TT)])
                diag = scores_diag.rearrange("p (h t q) -> p h t q", h=HG_HEADS, t=TT)
                cross = grid(scores_cross, HG_HEADS)
                for t in range(TT):
                    for f in range(2):
                        bank = open_bank(f"rec{t}{f}")
                        for j in range(4):
                            h = 4 * f + j
                            o = bank[:, j * P:j * P + P]
                            mm = nc.tensor.matmul(o, diag[:, h, t, :], hv[:, t, h * P:h * P + P], start=True, stop=t == 0)
                            if t:
                                mm = nc.tensor.matmul(o, cross[:, h, :], hv[:, 0, h * P:h * P + P], start=False, stop=True)
                        close_bank(mm, f"rec{t}{f}")
                drained_by(pe, "kcT0", "kcT1", "vcT0", "vcT1")
                w = [use("cmp_k"), use("cmp_v")]
                bank = open_bank("cmp_hid")
                for j in range(CMP_LEN // 2):
                    for kv in range(2):
                        mm = nc.tensor.matmul(bank[64 * kv:64 * kv + 4 * N_CMP, 0:CMP_HIDDEN], windows[:, kv, j // 8, :, j % 8], w[kv][:, j, :],
                                              start=j == 0, stop=j == CMP_LEN // 2 - 1)
                close_bank(mm, "cmp_hid")
                unit_last_fill["cmp_k"] = unit_last_fill["cmp_v"] = "cmp_hid"
                drained_by(pe, *[f"nq_rotT{j}" for j in range(4)], "ksT0", "ksT1", "kwT0", "kwT1")
                scores(blocks2[0])
                scores(blocks2[1])
                drained_by(pe, "cmp_hid")
                bank = open_bank("cmp_hidT")
                for c in range(2):
                    mm = nc.tensor.transpose(bank[:, c * P:c * P + P], cmp_hid[:, c * P:c * P + P], ident)
                close_bank(mm, "cmp_hidT")
                drained_by(pe, "cmp_hidT")
                pe.wait_ge(sem("cmp_w2_landed"), 48)
                bank = open_bank("cmp_kT")
                for c in range(2):
                    mm = nc.tensor.matmul(bank[:, 0:4 * N_CMP], cmp_wk2[:, c, :, :].rearrange("p u n -> p (u n)"), cmp_hidT[:, c, 0:4 * N_CMP],
                                          start=c == 0, stop=c == 1)
                close_bank(mm, "cmp_kT")
                bank = open_bank("cmp_v")
                for g in range(NSA_KV):
                    for c in range(2):
                        mm = nc.tensor.matmul(bank[0:N_CMP, g * 64:g * 64 + 64], cmp_hidT[:, c, 64 + g * N_CMP:64 + g * N_CMP + N_CMP],
                                              cmp_wv2[:, c, :], start=c == 0, stop=c == 1)
                close_bank(mm, "cmp_v")
                pe.wait_ge(sem("y_a_ready"), 1)
                transposes("y_aT", normed)
                drained_by(pe, "cmp_kT", *[f"nqT{j}" for j in range(4)])
                for t in range(TT):
                    for odd in range(2):
                        bank = open_bank(f"cmpS{t}{odd}")
                        for i in range(NSA_HEADS // 2):
                            r, g = 64 * odd, i // 2
                            mm = nc.tensor.matmul(bank[:, i * N_CMP:i * N_CMP + N_CMP], nqT[r:r + 64, i, t * P:t * P + P],
                                                  cmp_kT[r:r + 64, g * N_CMP:g * N_CMP + N_CMP], start=True, stop=True)
                        close_bank(mm, f"cmpS{t}{odd}")
                drained_by(pe, *[f"y_aT{j}" for j in range(4)])
                token_major("branch_a0", "branch_a0", y_aT)
                for t in range(TT):
                    pe.wait_ge(sem("cmp_probs_ready"), t + 1)
                    bank = open_bank(f"cmpT{t}")
                    for g in range(NSA_KV):
                        mm = nc.tensor.transpose(bank[:, g * P:g * P + P],
                                                 cmp_p[:, t, 4 * g:4 * g + 4, :].rearrange("p h n -> p (h n)"), ident)
                    close_bank(mm, f"cmpT{t}")
                scores(blocks2[2])
                turn_probs(blocks2[0])
                drained_by(pe, "cmpT0", "cmpT1")
                pe.wait_ge(sem("cmp_v_ready"), 1)
                for t in range(TT):
                    for f in range(2):
                        bank = open_bank(f"cmpO{t}{f}")
                        for j in range(2):
                            mm = nc.tensor.matmul(bank[:, j * 256:j * 256 + 256], cmp_pT[:, t, 2 * f + j, :], cmp_v[:, 2 * f + j, :],
                                                  start=True, stop=True)
                        close_bank(mm, f"cmpO{t}{f}")
                token_major("branch_a1", "branch_a1", y_aT)
                for i in range(3, len(blocks2) + 3):
                    if i < len(blocks2):
                        scores(blocks2[i])
                    if i - 2 < len(blocks2):
                        turn_probs(blocks2[i - 2])
                    weigh_values(blocks2[i - 3])
                    if i == len(blocks2) + 1:
                        pe.wait_ge(sem("y_b_ready"), 1)
                        turn_half("y_bT", y_b, 0)

                def y_b_second():
                    pe.wait_ge(sem("y_b_ready"), 2)
                    turn_half("y_bT", y_b, 1)

                def merged(t):
                    pe.wait_ge(sem("merged_ready"), t + 1)
                    turn_half("mergedT", mix_a, t)

                def merged_first():
                    merged(0)

                half_turned("y_bT", 0)
                token_pair(["branch_b0", "branch_b1"], y_bT,
                           {(0, 1): y_b_second, (1, 0): lambda: half_turned("y_bT", 1), (1, 1): merged_first})
                half_turned("mergedT", 0)
                token_pair(["out2_0", "out2_1"], xT, {(0, 1): lambda: merged(1), (1, 0): lambda: half_turned("mergedT", 1),
                                                      (1, 1): lambda: normed_half("mlpT", 0, 9)})
                half_turned("mlpT", 0)
                feature_pair(["up0", "up1"], xT, lambda: normed_half("mlpT", 1, 10), lambda: half_turned("mlpT", 1))
                for c in range(2, 8):
                    feature_major(f"up{c}", f"up{c}", xT)
                pe.wait_ge(sem("p_landed"), 16)
                bank = open_bank("pT")
                for k in range(2):
                    for t in range(TT):
                        mm = nc.tensor.transpose(bank[:, k * T + t * P:k * T + t * P + P], p_tok[:, t, k * P:k * P + P], ident)
                close_bank(mm, "pT")
                for c in range(2):
                    tiles = [open_bank(f"down{c}{t}") for t in range(TT)]
                    for k4 in range(4):
                        w = use(f"down{c}{k4}")
                        if c == 0:
                            pe.wait_ge(sem("ff_ready"), 4 * k4 + 4)
                        for t in range(TT):
                            for k in range(KT):
                                mm = nc.tensor.matmul(tiles[t], ffT[k4][:, k, t * P:t * P + P], w[:, k, :],
                                                      start=k4 == 0 and k == 0, stop=k4 == 3 and k == KT - 1)
                            if k4 == 3:
                                close_bank(mm, f"down{c}{t}")
                        if k4 < 3:
                            mm.then_inc(sem("down_used"), 1)
                        unit_last_fill[f"down{c}{k4}"] = f"down{c}1" if k4 == 3 else 3 * c + k4 + 1
                drained_by(pe, "pT")
                w = use("ple")
                for c in range(2):
                    for t in range(TT):
                        bank = open_bank(f"ple{c}{t}")
                        for k in range(2):
                            mm = nc.tensor.matmul(bank, pT[:, k, t * P:t * P + P], w[:, k, c * 512:c * 512 + 512], start=k == 0, stop=k == 1)
                        close_bank(mm, f"ple{c}{t}")
                unit_last_fill["ple"] = "ple11"
                def x_half(t):
                    pe.wait_ge(sem("x_ready"), t + 1)
                    turn_half("pleT", x, t)

                x_half(0)
                half_turned("pleT", 0)
                token_pair(["ple_gate0", "ple_gate1"], xT, {(0, 1): lambda: x_half(1), (1, 0): lambda: half_turned("pleT", 1)})

            counts, roots = {}, []

            def counted(eng, ins, name, wait):
                counts[name] = counts.get(name, 0) + 1
                ins.then_inc(sem(name), 1)
                if wait:
                    eng.wait_ge(sem(name), counts[name])

            def drains(eng, ins, fill, wait):
                n = fills[fill]
                ins.then_inc(sem(f"bank_drained{n % BANKS}"), 1)
                if wait:
                    eng.wait_ge(sem(f"bank_drained{n % BANKS}"), n // BANKS + 1)

            @block.vector
            def _(dve):
                V = nc.vector

                def step(ins, name="dve_step", wait=True):
                    counted(dve, ins, name, wait)

                def drain(ins, fill, wait=False):
                    drains(dve, ins, fill, wait)

                def wide(ap, shape):
                    return ap.to_broadcast(shape)

                def inverse_root(v):
                    roots.append(v)
                    dve.wait_ge(sem("root_ready"), len(roots))
                    step(V.reciprocal(v, v))

                def inverse_rms(dst, sums, width):
                    step(V.tensor_scalar(dst, sums, 1.0 / width, EPS, ALU.mult, ALU.add), "variance_ready", wait=False)
                    inverse_root(dst)

                def normalize(src, dst, k, name):
                    sums, inv = stat(k, 2), stat(k + 2, 2)
                    for t in range(TT):
                        step(V.tensor_tensor_reduce(dst[:, t, :], src[:, t, :], src[:, t, :], 1.0, 0.0, ALU.mult, ALU.add,
                                                    sums[:, t:t + 1]))
                    inverse_rms(inv, sums, src.shape[2])
                    for t in range(TT):
                        step(V.tensor_scalar(dst[:, t, :], src[:, t, :], inv[:, t:t + 1], None, ALU.mult), name)

                def normalize_half(src, dst, k, t, name="x_normed"):
                    v = stat(k + t, 1)
                    step(V.tensor_tensor_reduce(dst[:, t, :], src[:, t, :], src[:, t, :], 1.0, 0.0, ALU.mult, ALU.add, v))
                    inverse_rms(v, v, src.shape[2])
                    step(V.tensor_scalar(dst[:, t, :], src[:, t, :], v, None, ALU.mult), name)

                def scaled_norm(src, dst, k, t, gain, junk):
                    v = stat(k + t, 1)
                    step(V.tensor_tensor_reduce(junk, src[:, t, :], src[:, t, :], 1.0, 0.0, ALU.mult, ALU.add, v))
                    inverse_rms(v, v, src.shape[2])
                    step(V.scalar_tensor_tensor(out=dst, in0=src[:, t, :], scalar=v, in1=gain, op0=ALU.mult, op1=ALU.mult))

                def half_turned(tag, dst, t, gain=None):
                    bank = filled_by(dve, f"{tag}{t}1")
                    o = dst[:, 4:8, t * P:t * P + P]
                    ins = V.tensor_copy(o, grid(bank, 4)) if gain is None else \
                        V.tensor_tensor(o, grid(bank, 4), wide(col(gain, 4, 4).unsqueeze(2), [P, 4, P]), ALU.mult)
                    drain(ins, f"{tag}{t}1")

                def turned(tag, dst, gain=None):
                    for j in (1, 3):
                        bank = filled_by(dve, f"{tag}{j}")
                        for k in (2 * j, 2 * j + 1):
                            src = bank[:, (k % 2) * T:(k % 2) * T + T]
                            ins = V.tensor_copy(dst[:, k, :], src) if gain is None else \
                                V.tensor_scalar(dst[:, k, :], src, col(gain, k), None, ALU.mult)
                        drain(ins, f"{tag}{j}")

                def softmax(blk):
                    nk = blk["nk"]
                    per = 512 // nk
                    mask = const("causal")[:, T - nk:T].unsqueeze(1)
                    for f in range(HEADS // per):
                        bank = filled_by(dve, f"{blk['name']}S{f}")
                        drain(V.tensor_tensor(blk["p"][:, f * per:f * per + per, :], grid(bank, per), wide(mask, [P, per, nk]), ALU.add),
                              f"{blk['name']}S{f}", wait=True)
                    top, _, _ = block_stats(blk)
                    step(V.tensor_reduce(top, blk["p"], AX.X, ALU.max))
                    step(V.tensor_scalar(top, top, -blk["scale"], None, ALU.mult), "max_ready")

                def probs_turned(blk):
                    flat = blk["pt"]
                    for f in range(1, HEADS * blk["nk"] // P // 4, 2):
                        bank = filled_by(dve, f"{blk['name']}T{f}")
                        drain(V.tensor_copy(flat[:, 4 * f:4 * f + 4, :], grid(bank, 4)), f"{blk['name']}T{f}")

                def by_head(flat):
                    return flat.rearrange("p (i r e) -> p i r e", r=2, e=HEAD_DIM)

                def factors(inv):
                    return wide(inv.rearrange("p (r i) -> p i r", r=2).unsqueeze(3), [P, HEADS // 2, 2, HEAD_DIM])

                def inverse_sums(blk):
                    dve.wait_ge(sem("probs_ready"), blk["n"] + 1)
                    _, sums, inv = block_stats(blk)
                    step(V.reciprocal(inv, sums))

                bank = filled_by(dve, "params")
                V.tensor_copy(cols[:, 0:n_rows], bank[:, 0:n_rows])
                drain(V.tensor_copy(cols[:, P:P + 4 * TAPS], bank[:, P:P + 4 * TAPS]), "params", wait=True)
                for t in range(TT):
                    dve.wait_ge(sem(f"x_landed{t}"), 16)
                    normalize_half(x, normed, 4, t)
                for t in range(TT):
                    half_turned("mixT", xT, t, "norm_mix_g")
                step(V.memset(z[:, :, 0:TAPS - 1], 0.0))
                for f in range(2):
                    drained_by(dve, f"conv_g{f}")
                    bank = filled_by(dve, f"conv_a{f}")
                    for cb in (2 * f, 2 * f + 1):
                        ins = V.scalar_tensor_tensor(out=z[:, cb, TAPS - 1:ZW], in0=bank[:, (cb % 2) * T:(cb % 2) * T + T],
                                                     scalar=col("b_glu", cb), in1=glu[:, cb, :], op0=ALU.add, op1=ALU.mult)
                    drain(ins, f"conv_a{f}", wait=True)
                for cb in range(DVE_CONV):
                    step(V.tensor_scalar(conv[:, cb, :], z[:, cb, 0:T], tap(0, cb), col("b_dw", cb), ALU.mult, ALU.add), wait=False)

                def convolve(taps):
                    for w in taps:
                        for cb in range(DVE_CONV):
                            dve.wait_ge(sem("dve_step"), counts["dve_step"] - DVE_CONV + 1)
                            ins = V.scalar_tensor_tensor(out=conv[:, cb, :], in0=z[:, cb, w:w + T], scalar=tap(w, cb),
                                                         in1=conv[:, cb, :], op0=ALU.mult, op1=ALU.add)
                            step(ins, "conv_ready" if w == TAPS - 1 and cb == DVE_CONV - 1 else "dve_step", wait=False)

                dve.wait_ge(sem("mem_landed"), 16)
                normalize(mem_tok, mem_normed, 0, "mem_normed")
                convolve(range(1, 6))
                for f in range(2):
                    bank = filled_by(dve, f"q{f}")
                    drain(V.tensor_copy(qT1[:, 2 * f:2 * f + 2, :], grid(bank, 2)), f"q{f}")
                convolve(range(6, 11))
                dve.wait_ge(sem("forget_landed"), 32)
                bank = filled_by(dve, "forget")
                tmp = page(4, 0, 1024)[0:HEADS, :].rearrange("p (n t) -> p n t", n=4)
                drain(V.tensor_scalar(tmp[:, 0, :], bank[0:HEADS, 0:T], forget_b[:, 0:1], None, ALU.add), "forget", wait=True)
                step(V.tensor_scalar(tmp[:, 1, :], tmp[:, 0, :], -1.0, None, ALU.mult))
                step(V.tensor_tensor(tmp[:, 1, :], tmp[:, 1, :], tmp[:, 0, :], ALU.max), "forget_abs")
                step(V.tensor_scalar(tmp[:, 0, :], tmp[:, 0, :], 0.0, None, ALU.min))
                dve.wait_ge(sem("forget_log"), 1)
                step(V.tensor_tensor(log_f, tmp[:, 0, :], tmp[:, 2, :], ALU.subtract))
                step(V.tensor_tensor_scan(tmp[:, 3, :], const("ones")[0:HEADS, 0:T], log_f, 0.0, ALU.mult, ALU.add))
                step(V.tensor_scalar(key_bias, tmp[:, 3, :], -(HEAD_DIM ** 0.5), None, ALU.mult), "key_bias_ready")
                convolve(range(11, 16))
                turned("memT", memT, "mem_norm_g")
                for c in range(2):
                    for f in range(2):
                        bank = filled_by(dve, f"mem_k{c}{f}")
                        drain(V.tensor_copy(mem_k[:, 4 * c + 2 * f:4 * c + 2 * f + 2, :], grid(bank, 2)), f"mem_k{c}{f}")
                        convolve(range(16 + 4 * (2 * c + f), min(20 + 4 * (2 * c + f), TAPS)))
                softmax(blocks1[0])
                softmax(blocks1[1])
                for blk in blocks1:
                    inverse_sums(blk)
                    probs_turned(blk)

                def attn1_out(blk):
                    t = blk["t"]
                    _, _, inv = block_stats(blk)
                    bank = filled_by(dve, f"{blk['name']}O")
                    drain(V.tensor_tensor(by_head(attn1[:, t, :]), by_head(bank), factors(inv), ALU.mult), f"{blk['name']}O", wait=True)
                    junk = page(9, 0, 512)
                    sums, inv_rms = stat(8 + t, 1), stat(10 + t, 1)
                    step(V.tensor_tensor_reduce(junk, attn1[:, t, :], attn1[:, t, :], 1.0, 0.0, ALU.mult, ALU.add, sums))
                    inverse_rms(inv_rms, sums, D_ATTN)
                    step(V.tensor_scalar(attn1[:, t, :], attn1[:, t, :], inv_rms, None, ALU.mult), "attn1_normed")

                bank = filled_by(dve, "conv_mean")
                mean = page(9, 512, 256)
                drain(V.tensor_scalar(mean, bank[:, 0:T], 1.0 / D_CONV, None, ALU.mult), "conv_mean", wait=True)
                step(V.tensor_tensor(conv, conv, wide(mean.unsqueeze(1), [P, 4, T]), ALU.subtract))
                step(V.tensor_tensor(glu, conv, conv, ALU.mult), "conv_ready")
                attn1_out(blocks1[0])
                attn1_out(blocks1[1])
                bank = filled_by(dve, "conv_var")
                drain(V.tensor_scalar(mean, bank[:, 0:T], 1.0 / D_CONV, None, ALU.mult), "conv_var", wait=True)
                step(V.tensor_scalar(mean, mean, EPS, None, ALU.add), "variance_ready", wait=False)
                inverse_root(mean)
                step(V.tensor_tensor(conv, conv, wide(mean.unsqueeze(1), [P, 4, T]), ALU.mult), "conv_normed")
                for t in range(TT):
                    bank = filled_by(dve, f"attn1T{t}")
                    for k in range(4):
                        ins = V.tensor_scalar(catT[:, k, t * P:t * P + P], bank[:, k * P:k * P + P], col("attn_out_g", k), None, ALU.mult)
                    drain(ins, f"attn1T{t}")

                def add_to_x(tag, t):
                    for c in range(2):
                        bank = filled_by(dve, f"{tag}{c}{t}")
                        drain(V.tensor_tensor(x[:, t, c * 512:c * 512 + 512], x[:, t, c * 512:c * 512 + 512], bank, ALU.add),
                              f"{tag}{c}{t}", wait=True)

                for t in range(TT):
                    add_to_x("out", t)
                    normalize_half(x, normed, 12, t)
                    half_turned("normT", xT, t, "norm_mem_g")
                for c in range(2):
                    bank = filled_by(dve, f"mem_q{c}1")
                    drain(V.tensor_copy(qT2[:, 4 * c + 2:4 * c + 4, :], grid(bank, 2)), f"mem_q{c}1")
                top2 = grid(stat(16, 8), TT)
                sum2, inv2 = grid(stat(24, 8), TT), grid(stat(32, 8), TT)
                for t in range(TT):
                    for f in range(2):
                        bank = filled_by(dve, f"crossS{t}{f}")
                        step(V.tensor_reduce(top2[:, t, 2 * f:2 * f + 2], grid(bank, 2), AX.X, ALU.max))
                        step(V.tensor_scalar(top2[:, t, 2 * f:2 * f + 2], top2[:, t, 2 * f:2 * f + 2], -(MEM_DIM ** -0.5), None, ALU.mult),
                             "cross_max_ready")
                for t in range(TT):
                    drained_by(dve, f"crossS{t}0", f"crossS{t}1")
                    step(V.reciprocal(inv2[:, t, :], sum2[:, t, :]))
                    step(V.tensor_tensor(prob2[:, t, :, :], prob2[:, t, :, :], wide(inv2[:, t, :].unsqueeze(2), [P, MEM_HEADS, T]), ALU.mult),
                         "cross_probs_ready")
                for t in range(TT):
                    bank = filled_by(dve, f"crossT{t}1")
                    drain(V.tensor_copy(prob2T[:, 2:4, :, t * P:t * P + P], bank.rearrange("p (h m q) -> p h m q", h=2, m=2)), f"crossT{t}1")
                for f in (1, 3):
                    bank = filled_by(dve, f"crossO{f}")
                    drain(V.tensor_copy(oT2[:, 2 * f:2 * f + 2, :], grid(bank, 2)), f"crossO{f}")
                chosen = grid(scratch_route[:, 0:64], TT)
                r = lambda k, n: scratch_route[:, 64 + k:64 + k + n]
                dve.wait_ge(sem("route_landed"), 16 * (GROUPS + 3))

                def first_largest(values, n, k, top):
                    hot, run = r(k, n), r(k + 32, n)
                    step(V.tensor_reduce(top, values, AX.X, ALU.max))
                    step(V.tensor_scalar(hot, values, top, None, ALU.is_equal))
                    step(V.tensor_tensor_scan(run, const("ones")[:, 0:n], hot, 0.0, ALU.mult, ALU.add))
                    step(V.tensor_scalar(run, run, 1.0, None, ALU.is_equal))
                    step(V.tensor_tensor(hot, hot, run, ALU.mult))
                    return hot

                for t in range(TT):
                    add_to_x("mem_o", t)
                    normalize_half(x, normed, 40, t)
                    half_turned("ffnT", xT, t, "norm_ffn_g")
                    bank = filled_by(dve, f"route{t}")
                    drain(V.tensor_tensor(logits[:, t, :], bank[:, 0:36], route_b[:, :], ALU.add), f"route{t}", wait=True)
                    base = 512 * t
                    tops = stat(44 + 8 * t, 8)
                    group = first_largest(logits[:, t, 0:4], 4, base, tops[:, 0:1])
                    step(V.tensor_scalar(tops[:, 1:2], tops[:, 0:1], -1.0, None, ALU.mult), "group_max_ready")
                    step(V.tensor_scalar(r(base + 64, 4), group, -1.0, BIG, ALU.add, ALU.mult))
                    masked = r(base + 96, 32)
                    step(V.tensor_tensor(grid(masked, 4), grid(logits[:, t, 4:36], 4), wide(r(base + 64, 4).unsqueeze(2), [P, 4, 8]), ALU.add))
                    one = first_largest(masked, 32, base + 128, tops[:, 2:3])
                    rest = r(base + 192, 32)
                    step(V.scalar_tensor_tensor(out=rest, in0=one, scalar=-3.0 * BIG, in1=masked, op0=ALU.mult, op1=ALU.add))
                    two = first_largest(rest, 32, base + 224, tops[:, 3:4])
                    step(V.tensor_tensor(chosen[:, t, :], one, two, ALU.add), "choice_ready" if t == 1 else "dve_step")
                    step(V.tensor_tensor(tops[:, 4:5], tops[:, 3:4], tops[:, 2:3], ALU.subtract), "second_ready")
                    dve.wait_ge(sem("route_exp"), 2 * t + 2)
                    step(V.scalar_tensor_tensor(out=tops[:, 6:7], in0=tops[:, 4:5], scalar=1.0, in1=tops[:, 5:6], op0=ALU.add, op1=ALU.mult))
                    step(V.reciprocal(tops[:, 6:7], tops[:, 6:7]))
                    step(V.scalar_tensor_tensor(out=gate[:, t, :], in0=two, scalar=tops[:, 4:5], in1=one, op0=ALU.mult, op1=ALU.add))
                    step(V.tensor_scalar(gate[:, t, :], gate[:, t, :], tops[:, 6:7], None, ALU.mult))
                bank = filled_by(dve, "rank")
                step(V.scalar_tensor_tensor(out=pos[:, :, :], in0=grid(bank[:, 0:64], TT), scalar=1.0, in1=chosen, op0=ALU.add, op1=ALU.mult))
                step(V.tensor_scalar(pos[:, :, :], pos[:, :, :], -1.0, None, ALU.add))
                drain(V.tensor_reduce(stat(60, 1), bank[:, 64:96], AX.X, ALU.max), "rank", wait=True)
                step(V.tensor_copy(busiest[:, :], stat(60, 1)), "busiest_ready")

                def experts(tag, first, n_pairs):
                    s = lambda name: sem(f"{tag}_{name}")

                    def pick(n, e, dst, gated_too):
                        expert = bass.ds(2 * ((n + first) % PAIRS) + e, 1)
                        slots = const("slots")[:, bass.ds(CAP * ((n + first) // PAIRS), CAP)]
                        for t in range(TT):
                            o = dst[:, t, e * CAP:e * CAP + CAP]
                            if gated_too:
                                ins = V.tensor_scalar(o, slots, pos[:, t, expert], gate[:, t, expert], ALU.is_equal, ALU.mult)
                            else:
                                ins = V.tensor_scalar(o, slots, pos[:, t, expert], None, ALU.is_equal)
                        return ins

                    def build_choose(n):
                        pick(n, 0, choose, False)
                        pick(n, 1, choose, False).then_inc(s("choose_ready"), 1)

                    def build_gated(n):
                        pick(n, 0, choose_gated, True)
                        pick(n, 1, choose_gated, True).then_inc(s("gated_choose_ready"), 1)

                    def drain_picked(n):
                        for f, b in ((0, 0), (1, 7)):
                            dve.wait_ge(s("picked_filled"), 2 * n + f + 1)
                            V.tensor_tensor(picked[:, 4 * f:4 * f + 4, :], grid(ps[:, b, :], 4),
                                            wide(col("norm_ffn_g", 4 * f, 4).unsqueeze(2), [P, 4, P]), ALU.mult).then_inc(s("picked_drained"), 1)

                    def drain_sums(n):
                        for t in range(TT):
                            for c in range(2):
                                dve.wait_ge(s("sum_filled"), 4 * n + 2 * t + c + 1)
                                V.tensor_tensor(x[:, t, c * 512:c * 512 + 512], x[:, t, c * 512:c * 512 + 512], ps[:, 5 + c, :],
                                                ALU.add).then_inc(s("sum_drained"), 1)

                    def gate_hidden(n):
                        dve.wait_ge(s("silu_ready"), n + 1)
                        dve.wait_ge(s("up_filled"), 2 * n + 2)
                        V.tensor_tensor(hidden, hidden, ps[:, 2, :], ALU.mult).then_inc(s("hidden_ready"), 1)

                    V.memset(spread, 0.0).then_inc(s("spread_ready"), 1)
                    for c in range(2):
                        V.memset(expert_out[:, c * 512:c * 512 + 512], 0.0).then_inc(s("out_ready"), 1)
                    build_choose(0)
                    build_gated(0)
                    drain_picked(0)
                    build_choose(1)
                    with dve.Fori(0, n_pairs) as i:
                        drain_sums(i)
                        gate_hidden(i)
                        dve.wait_ge(s("sum_drained"), 4 * i + 4)
                        drain_picked(i + 1)
                        build_choose(i + 2)
                        dve.wait_ge(s("spread_filled"), i + 1)
                        build_gated(i + 1)
                    drain_sums(n_pairs)
                    dve.wait_ge(s("sum_drained"), 4 * n_pairs + 4)

                experts("moe", 0, PAIRS)
                count = dve.value_load(busiest[0:1, 0:1], min_val=0, max_val=T)
                with dve.If(count > CAP):
                    experts("more", PAIRS, MORE)

                dve.wait_ge(sem("final_gain_landed"), 16)
                for t in range(TT):
                    scaled_norm(x, x[:, t, :], 40, t, gain_final, normed[:, t, :])
                    normalize_half(x, normed, 44, t)
                step(V.memset(cmp_hid, 0.0), "cmp_hid_cleared")
                e0, e1, lb, rest = stat(0, 8), stat(8, 8), stat(16, 8), stat(24, 8)
                l0, l1 = col("hg_lb_logits_2", 0, 8), col("hg_lb_logits_2", 8, 8)
                step(V.tensor_tensor(lb, l0, l1, ALU.max))
                step(V.tensor_tensor(e0, l0, lb, ALU.subtract))
                step(V.tensor_tensor(e1, l1, lb, ALU.subtract), "lb_ready")
                dve.wait_ge(sem("lb_exp"), 2)
                step(V.tensor_tensor(rest, e0, e1, ALU.add))
                step(V.reciprocal(rest, rest))
                step(V.tensor_tensor(lb, e0, rest, ALU.mult))
                step(V.tensor_scalar(rest, lb, -1.0, 1.0, ALU.mult, ALU.add))
                for t in range(TT):
                    half_turned("mix2T", xT, t, "norm_pre_mix_2")
                for c in range(2):
                    for f in range(2):
                        at = (4 * c + 2 * f) * T
                        dve.wait_ge(sem("hq_sigmoid"), 2 * c + f + 1)
                        bank = filled_by(dve, f"hq{c}{f}")
                        drain(V.scalar_tensor_tensor(out=hq[:, at:at + 512], in0=bank, scalar=P ** -0.5, in1=hx[0][:, at:at + 512],
                                                     op0=ALU.mult, op1=ALU.mult), f"hq{c}{f}", wait=True)
                drained_by(dve, "hf00", "hf01", "hf10", "hf11")
                for h in range(HG_HEADS):
                    step(V.tensor_scalar(hb[:, h * T:h * T + T], hb[:, h * T:h * T + T], rest[:, h:h + 1], lb[:, h:h + 1], ALU.mult, ALU.add),
                         "forget2_ready", wait=False)
                dve.wait_ge(sem("forget2_ready"), HG_HEADS)
                step(V.tensor_scalar(hk, hb, -1.0, 1.0, ALU.mult, ALU.add), "level_ready")
                dve.wait_ge(sem("log_forget"), 1)
                for h in range(HG_HEADS):
                    step(V.tensor_tensor_scan(hb[:, h * T:h * T + T], const("chunk_reset"), hx[0][:, h * T:h * T + T], 0.0, ALU.mult, ALU.add),
                         wait=h == HG_HEADS - 1)

                def level_drains(n):
                    if n and LEVELS[n - 1] == P:
                        for f in range(2):
                            bank = filled_by(dve, f"level{n}_{f}")
                            drain(V.tensor_copy(scores_cross[:, f * 512:f * 512 + 512], bank), f"level{n}_{f}")
                        return
                    mask = const("ident") if n == 0 else const(f"level{LEVELS[n - 1]}")
                    mask = mask.unsqueeze(1)
                    for f in range(4):
                        bank = filled_by(dve, f"level{n}_{f}")
                        dst = grid(scores_diag[:, f * 512:f * 512 + 512], 4)
                        if n == 0:
                            drain(V.tensor_tensor(dst, grid(bank, 4), wide(mask, [P, 4, P]), ALU.mult), f"level{n}_{f}", wait=True)
                        else:
                            drain(V.copy_predicated(dst, wide(mask.bitcast(U32), [P, 4, P]), grid(bank, 4)), f"level{n}_{f}", wait=True)

                half = ROPE_DIM // 2
                tmp = [grid(page(1, 256 * n, 256), TT) for n in range(4)]

                def rotate(src, dst, n):
                    for t in range(TT):
                        sv = src[:, t, :].rearrange("p (h e) -> p h e", e=NSA_DH)
                        dv = dst[:, t, :].rearrange("p (h e) -> p h e", e=NSA_DH)
                        cos = wide(grid(const("cos"), TT)[:, t, :].unsqueeze(1), [P, n, half])
                        sin = wide(grid(const("sin"), TT)[:, t, :].unsqueeze(1), [P, n, half])
                        a = [w[:, t, 0:n * half].rearrange("p (h e) -> p h e", e=half) for w in tmp]
                        x1, x2 = sv[:, :, 0:half], sv[:, :, half:ROPE_DIM]
                        step(V.tensor_tensor(a[0], x1, cos, ALU.mult), wait=False)
                        step(V.tensor_tensor(a[1], x2, sin, ALU.mult), wait=False)
                        step(V.tensor_tensor(a[2], x2, cos, ALU.mult), wait=False)
                        step(V.tensor_tensor(a[3], x1, sin, ALU.mult))
                        step(V.tensor_tensor(dv[:, :, 0:half], a[0], a[1], ALU.subtract), wait=False)
                        step(V.tensor_tensor(dv[:, :, half:ROPE_DIM], a[2], a[3], ALU.add), "rotated")

                for n, L in enumerate(LEVELS, 1):
                    halves = lambda flat: flat.rearrange("p (n r l) -> p n r l", r=2, l=L)
                    n_blocks = HG_HEADS * T // (2 * L)
                    b, e = halves(hb), halves(hx[n % 2])
                    mid = wide(b[:, :, 0, L - 1:L], [P, n_blocks, L])
                    if L >= CHUNK:
                        step(V.tensor_tensor(b[:, :, 1, :], b[:, :, 1, :], mid, ALU.add))
                    step(V.tensor_tensor(e[:, :, 0, :], mid, b[:, :, 0, :], ALU.subtract), wait=False)
                    step(V.tensor_tensor(e[:, :, 1, :], b[:, :, 1, :], mid, ALU.subtract), "exponent_ready")
                    level_drains(n - 1)
                    dve.wait_ge(sem("decay_ready"), n)
                    step(V.tensor_tensor(e[:, :, 0, :], e[:, :, 0, :], halves(hk)[:, :, 0, :], ALU.mult), wait=False)
                    step(V.tensor_tensor(e[:, :, 1, :], e[:, :, 1, :], halves(hq)[:, :, 1, :], ALU.mult), "level_ready")
                    if n == 4:
                        dve.wait_ge(sem("gnorm_landed"), 16)
                        drained_by(dve, *[f"hg{c}{t}" for c in range(2) for t in range(TT)])
                        for t in range(TT):
                            g = grid(hg[:, t, :], HG_HEADS)
                            step(V.tensor_tensor(g, g, wide(gnorm.unsqueeze(1), [P, HG_HEADS, P]), ALU.mult), wait=False)
                    if n == 5:
                        drained_by(dve, *[f"nq{c}{t}" for c in range(2) for t in range(TT)])
                        rotate(nq, nq_rot, NSA_HEADS)
                    if n in (6, 7):
                        drained_by(dve, *[f"kv{c}{t}" for c in range(3) for t in range(TT)])
                        k_rot = nkv[:, :, 512 * (n - 5):512 * (n - 5) + 256]
                        rotate(k_rot, k_rot, NSA_KV)
                level_drains(len(LEVELS))
                for kv, key in enumerate("kv"):
                    for f in range(2):
                        bank = filled_by(dve, f"{key}cT{f}")
                        tokens = bank.rearrange("p (g n j u) -> p g n j u", g=2, j=8, u=2)
                        for half_ in range(2):
                            dst = windows[:, kv, half_, :, :].rearrange("p (g n) j -> p g n j", g=4)
                            for u in range(2):
                                h = slice(64 * u, 64 * u + 64)
                                pe_ = col(f"cmp_pe_{key}_2", 8 * half_, 8)[h].unsqueeze(1).unsqueeze(1)
                                ins = V.tensor_tensor(dst[h, 2 * f:2 * f + 2], tokens[h, :, half_:half_ + N_CMP, :, u],
                                                      wide(pe_, [64, 2, N_CMP, 8]), ALU.add)
                        drain(ins, f"{key}cT{f}")
                for t in range(TT):
                    for f in range(2):
                        bank = filled_by(dve, f"rec{t}{f}")
                        drain(V.tensor_copy(normed[:, t, f * 512:f * 512 + 512], bank), f"rec{t}{f}", wait=True)
                for t in range(TT):
                    o = grid(normed[:, t, :], HG_HEADS)
                    sq = grid(page(6, 1024, 1024), HG_HEADS)
                    sums = stat(0 + 16 * t, 8)
                    step(V.tensor_tensor(sq, o, o, ALU.mult))
                    step(V.tensor_reduce(sums, sq, AX.X, ALU.add))
                    inverse_rms(sums, sums, P)
                    step(V.tensor_tensor(o, o, wide(sums.unsqueeze(2), [P, HG_HEADS, P]), ALU.mult))
                    step(V.tensor_tensor(normed[:, t, :], normed[:, t, :], hg[:, t, :], ALU.mult), "y_a_ready" if t else "dve_step")
                softmax(blocks2[0])
                softmax(blocks2[1])
                bank = filled_by(dve, "cmp_kT")
                drain(V.tensor_copy(cmp_kT, bank[:, 0:4 * N_CMP]), "cmp_kT")
                filled_by(dve, "nq_rotT3")
                step(V.memset(page(13, 1024, 1024), 0.0))
                bank = filled_by(dve, "cmp_v")
                for h in range(4):
                    ins = V.tensor_copy(cmp_v[32 * h:32 * h + N_CMP, :, h * 64:h * 64 + 64], grid(bank[0:N_CMP, 0:256], 4))
                    if h < 3:
                        step(ins)
                    else:
                        drain(ins, "cmp_v", wait=True)
                step(V.memset(page(9, 0, 1024), 0.0), "cmp_v_ready")
                turned("y_aT", y_aT)

                def gate_branch_a(c):
                    dve.wait_ge(sem("mix_gates_ready"), 2)
                    for t in range(TT):
                        bank = filled_by(dve, f"branch_a{c}{t}")
                        m = mix_a[:, t, c * 512:c * 512 + 512]
                        drain(V.tensor_tensor(m, m, bank, ALU.mult), f"branch_a{c}{t}")

                seen, bias = grid(const("cmp_seen"), TT), grid(const("cmp_bias"), TT)
                tops = [stat(0, 16), stat(16, 16)]
                for t in range(TT):
                    live = cmp_p[:, t, :, 0:N_CMP]
                    for odd in range(2):
                        bank = filled_by(dve, f"cmpS{t}{odd}")
                        drain(V.tensor_tensor(live[:, odd:NSA_HEADS:2, :], grid(bank[:, 0:NSA_HEADS // 2 * N_CMP], NSA_HEADS // 2),
                                              wide(bias[:, t, :].unsqueeze(1), [P, NSA_HEADS // 2, N_CMP]), ALU.add), f"cmpS{t}{odd}", wait=True)
                    step(V.tensor_reduce(tops[t], live, AX.X, ALU.max))
                    step(V.tensor_tensor(live, live, wide(tops[t].unsqueeze(2), [P, NSA_HEADS, N_CMP]), ALU.subtract), "cmp_shifted")
                for t in range(TT):
                    live = cmp_p[:, t, :, 0:N_CMP]
                    dve.wait_ge(sem("cmp_exp_ready"), t + 1)
                    step(V.tensor_reduce(tops[t], live, AX.X, ALU.add))
                    step(V.reciprocal(tops[t], tops[t]))
                    step(V.tensor_tensor(live, live, wide(tops[t].unsqueeze(2), [P, NSA_HEADS, N_CMP]), ALU.mult))
                    step(V.tensor_tensor(live, live, wide(seen[:, t, :].unsqueeze(1), [P, NSA_HEADS, N_CMP]), ALU.mult), "cmp_probs_ready")
                gate_branch_a(0)
                softmax(blocks2[2])
                inverse_sums(blocks2[0])
                probs_turned(blocks2[0])
                dve.wait_ge(sem("sel_gates_ready"), 1)
                for t in range(TT):
                    for f in range(2):
                        bank = filled_by(dve, f"cmpO{t}{f}")
                        g = sel_gates[:, t, 8 * f:8 * f + 8].unsqueeze(2)
                        drain(V.tensor_tensor(grid(y_b[:, t, f * 512:f * 512 + 512], HEADS), grid(bank, HEADS), wide(g, [P, HEADS, 64]), ALU.mult),
                              f"cmpO{t}{f}", wait=True)

                def nsa_out(blk):
                    t, half_, branch = blk["t"], blk["half"], blk["branch"]
                    _, _, inv = block_stats(blk)
                    at = 16 * (branch + 1) + 8 * half_
                    in_order = inv.rearrange("p (r i) -> p r i", r=2)
                    step(V.tensor_tensor(in_order, in_order, sel_gates[:, t, at:at + 8].rearrange("p (i r) -> p r i", r=2), ALU.mult))
                    bank = filled_by(dve, f"{blk['name']}O")
                    tmp_ = page(9, 1024, 512)
                    drain(V.tensor_tensor(by_head(tmp_), by_head(bank), factors(inv), ALU.mult), f"{blk['name']}O", wait=True)
                    y = y_b[:, t, half_ * 512:half_ * 512 + 512]
                    step(V.tensor_tensor(y, y, tmp_, ALU.add), "y_b_ready" if branch and half_ else "dve_step")

                gate_branch_a(1)
                for i in range(3, len(blocks2) + 3):
                    if i < len(blocks2):
                        softmax(blocks2[i])
                    if i - 2 < len(blocks2):
                        inverse_sums(blocks2[i - 2])
                        probs_turned(blocks2[i - 2])
                    nsa_out(blocks2[i - 3])
                def merge(t):
                    for c in range(2):
                        bank = filled_by(dve, f"branch_b{c}{t}")
                        cut = slice(c * 512, c * 512 + 512)
                        drain(V.tensor_tensor(mix_b[:, t, cut], mix_b[:, t, cut], bank, ALU.mult), f"branch_b{c}{t}", wait=True)
                        step(V.tensor_tensor(mix_a[:, t, cut], mix_a[:, t, cut], mix_b[:, t, cut], ALU.add),
                             "merged_ready" if c else "dve_step")

                def add_normed(src, k, t, gain, done="dve_step"):
                    scaled_norm(src, normed[:, t, :], k, t, gain, normed[:, t, :])
                    step(V.tensor_tensor(x[:, t, :], x[:, t, :], normed[:, t, :], ALU.add), done)

                for t in range(TT):
                    half_turned("y_bT", y_bT, t)
                merge(0)
                half_turned("mergedT", xT, 0)
                merge(1)
                half_turned("mergedT", xT, 1)
                dve.wait_ge(sem("gains_landed"), 48)
                for t in range(TT):
                    drained_by(dve, f"out2_0{t}", f"out2_1{t}")
                    add_normed(mlp_out, 0, t, gain_mix)
                    normalize_half(x, normed, 4, t)
                    half_turned("mlpT", xT, t, "norm_pre_mlp_2")
                for c in range(8):
                    for f in range(2):
                        drained_by(dve, f"up{c}{f}")
                        k = 4 * (c % 2) + 2 * f
                        dst = ffT[c // 2][:, k:k + 2, :]
                        step(V.tensor_tensor(dst, dst, dst, ALU.mult), "ff_ready", wait=False)
                bank = filled_by(dve, "pT")
                drain(V.tensor_copy(pT, grid(bank, 2)), "pT")
                for t in range(TT):
                    drained_by(dve, f"down0{t}", f"down1{t}")
                    add_normed(mlp_out, 8, t, gain_mlp, "x_ready")
                for t in range(TT):
                    half_turned("pleT", xT, t)
                for t in range(TT):
                    for c in range(2):
                        drained_by(dve, f"ple{c}{t}", f"ple_gate{c}{t}")
                        e = ple[:, t, c * 512:c * 512 + 512]
                        step(V.tensor_tensor(e, e, ple_gate[:, t, c * 512:c * 512 + 512], ALU.mult))
                    add_normed(ple, 12, t, gain_ple, "result_ready")

            @block.scalar
            def _(act):
                S = nc.scalar

                def step(ins, name="act_step", wait=True):
                    counted(act, ins, name, wait)

                def drain(ins, fill, wait=False):
                    drains(act, ins, fill, wait)

                def half_turned(tag, dst, t, gain=None):
                    bank = filled_by(act, f"{tag}{t}0")
                    if gain is None:
                        ins = S.copy(dst[:, 0:4, t * P:t * P + P], grid(bank, 4))
                    else:
                        for k in range(4):
                            ins = S.activation(dst[:, k, t * P:t * P + P], bank[:, k * P:k * P + P], ACT.Copy, scale=col(gain, k))
                    drain(ins, f"{tag}{t}0")

                def turned(tag, dst, gain=None):
                    for j in (0, 2):
                        bank = filled_by(act, f"{tag}{j}")
                        for k in (2 * j, 2 * j + 1):
                            src = bank[:, (k % 2) * T:(k % 2) * T + T]
                            ins = S.copy(dst[:, k, :], src) if gain is None else \
                                S.activation(dst[:, k, :], src, ACT.Copy, scale=col(gain, k))
                        drain(ins, f"{tag}{j}")

                def root(times=1):
                    for _ in range(times):
                        n = counts.get("root_ready", 0)
                        act.wait_ge(sem("variance_ready"), n + 1)
                        step(S.activation(roots[n], roots[n], ACT.Sqrt), "root_ready", wait=False)

                def exponentials(blk):
                    act.wait_ge(sem("max_ready"), blk["n"] + 1)
                    top, sums, _ = block_stats(blk)
                    for h in range(HEADS):
                        ins = S.activation(blk["p"][:, h, :], blk["p"][:, h, :], ACT.Exp, bias=top[:, h:h + 1], scale=blk["scale"],
                                           accum_out=sums[:, h:h + 1])
                    step(ins, "probs_ready")

                def probs_turned(blk):
                    for f in range(0, HEADS * blk["nk"] // P // 4, 2):
                        bank = filled_by(act, f"{blk['name']}T{f}")
                        drain(S.copy(blk["pt"][:, 4 * f:4 * f + 4, :], grid(bank, 4)), f"{blk['name']}T{f}")

                def copy_out(fill, dst, func=ACT.Copy):
                    bank = filled_by(act, fill)
                    drain(S.activation(dst, bank, func), fill)

                root(2)
                drained_by(act, "params")
                for t in range(TT):
                    half_turned("mixT", xT, t, "norm_mix_g")
                for f in range(2):
                    bank = filled_by(act, f"conv_g{f}")
                    for cb in (2 * f, 2 * f + 1):
                        ins = S.activation(glu[:, cb, :], bank[:, (cb % 2) * T:(cb % 2) * T + T], ACT.Sigmoid, bias=col("b_glu", 4 + cb))
                    drain(ins, f"conv_g{f}")
                root()
                for f in range(2):
                    bank = filled_by(act, f"k{f}")
                    drain(S.copy(kT1[:, 2 * f:2 * f + 2, :], grid(bank, 2)), f"k{f}")
                for t in range(TT):
                    copy_out(f"v{t}", v1[:, t, :])
                act.wait_ge(sem("forget_abs"), 1)
                tmp = page(4, 0, 1024)[0:HEADS, :].rearrange("p (n t) -> p n t", n=4)
                step(S.activation(tmp[:, 2, :], tmp[:, 1, :], ACT.Exp, scale=-1.0))
                step(S.activation(tmp[:, 2, :], tmp[:, 2, :], ACT.Ln, bias=1.0), "forget_log")
                turned("memT", memT, "mem_norm_g")
                exponentials(blocks1[0])
                exponentials(blocks1[1])
                for t in range(TT):
                    copy_out(f"mem_v0{t}", mem_v[:, t, 0:512])
                probs_turned(blocks1[0])
                probs_turned(blocks1[1])
                root(3)
                act.wait_ge(sem("conv_normed"), 1)
                for cb in range(4):
                    step(S.activation(catT[:, 4 + cb, :], conv[:, cb, :], ACT.Silu, bias=col("conv_ln_b", cb), scale=col("conv_ln_g", cb)),
                         "conv_done", wait=False)
                for t in range(TT):
                    copy_out(f"mem_v1{t}", mem_v[:, t, 512:1024])
                for t in range(TT):
                    root()
                    half_turned("normT", xT, t, "norm_mem_g")
                for c in range(2):
                    bank = filled_by(act, f"mem_q{c}0")
                    drain(S.copy(qT2[:, 4 * c:4 * c + 2, :], grid(bank, 2)), f"mem_q{c}0")
                top2, sum2 = grid(stat(16, 8), TT), grid(stat(24, 8), TT)
                for t in range(TT):
                    for f in range(2):
                        act.wait_ge(sem("cross_max_ready"), 2 * t + f + 1)
                        bank = filled_by(act, f"crossS{t}{f}")
                        for j in range(2):
                            h = 2 * f + j
                            ins = S.activation(prob2[:, t, h, :], bank[:, j * T:j * T + T], ACT.Exp, bias=top2[:, t, h:h + 1],
                                               scale=MEM_DIM ** -0.5, accum_out=sum2[:, t, h:h + 1])
                        drain(ins, f"crossS{t}{f}")
                for t in range(TT):
                    bank = filled_by(act, f"crossT{t}0")
                    drain(S.copy(prob2T[:, 0:2, :, t * P:t * P + P], bank.rearrange("p (h m q) -> p h m q", h=2, m=2)), f"crossT{t}0")
                for f in (0, 2):
                    bank = filled_by(act, f"crossO{f}")
                    drain(S.copy(oT2[:, 2 * f:2 * f + 2, :], grid(bank, 2)), f"crossO{f}")
                for t in range(TT):
                    root()
                    half_turned("ffnT", xT, t, "norm_ffn_g")
                    tops = stat(44 + 8 * t, 8)
                    act.wait_ge(sem("group_max_ready"), t + 1)
                    step(S.activation(stat(504, 4), logits[:, t, 0:4], ACT.Exp, bias=tops[:, 1:2], accum_out=tops[:, 5:6]), "route_exp")
                    act.wait_ge(sem("second_ready"), t + 1)
                    step(S.activation(tops[:, 4:5], tops[:, 4:5], ACT.Exp), "route_exp")

                def experts(tag, n_pairs):
                    s = lambda name: sem(f"{tag}_{name}")

                    act.wait_ge(s("out_ready"), 2)
                    with act.Fori(0, n_pairs) as i:
                        act.wait_ge(s("gate_filled"), 2 * i + 2)
                        S.activation(hidden, ps[:, 1, :], ACT.Silu).then_inc(s("silu_ready"), 1)
                        act.wait_ge(s("hidden_turned"), i + 1)
                        S.copy(hiddenT, grid(ps[:, 1, :], 4)).then_inc(s("hiddenT_ready"), 1)
                        act.wait_ge(s("spread_filled"), i + 1)
                        S.copy(spread, ps[:, 5, 0:T]).then_inc(s("spread_ready"), 1)
                        act.wait_ge(s("down_filled"), 2 * i + 2)
                        for c in range(2):
                            S.copy(expert_out[:, c * 512:c * 512 + 512], ps[:, 3 + c, :]).then_inc(s("out_ready"), 1)

                experts("moe", PAIRS)
                act.wait_ge(sem("busiest_ready"), 1)
                count = act.value_load(busiest[0:1, 0:1], min_val=0, max_val=T)
                with act.If(count > CAP):
                    experts("more", MORE)

                root(4)
                e0, e1 = stat(0, 8), stat(8, 8)
                act.wait_ge(sem("lb_ready"), 1)
                step(S.activation(e0, e0, ACT.Exp), "lb_exp", wait=False)
                step(S.activation(e1, e1, ACT.Exp), "lb_exp")
                for t in range(TT):
                    half_turned("mix2T", xT, t, "norm_pre_mix_2")
                for c in range(2):
                    for f in range(2):
                        at = (4 * c + 2 * f) * T
                        bank = filled_by(act, f"hq{c}{f}")
                        step(S.activation(hx[0][:, at:at + 512], bank, ACT.Sigmoid), "hq_sigmoid", wait=False)
                for c in range(2):
                    for f in range(2):
                        at = (4 * c + 2 * f) * T
                        copy_out(f"hf{c}{f}", hb[:, at:at + 512], ACT.Sigmoid)
                for c in range(2):
                    for t in range(TT):
                        copy_out(f"hi{c}{t}", hv[:, t, c * 512:c * 512 + 512])
                for c in range(2):
                    for t in range(TT):
                        copy_out(f"hg{c}{t}", hg[:, t, c * 512:c * 512 + 512], ACT.Silu)
                act.wait_ge(sem("forget2_ready"), HG_HEADS)
                drained_by(act, "hq00", "hq01", "hq10", "hq11")
                step(S.activation(hx[0], hb, ACT.Ln), "log_forget")

                def decay_of(n):
                    act.wait_ge(sem("exponent_ready"), n)
                    step(S.activation(hx[n % 2], hx[n % 2], ACT.Exp), "decay_ready", wait=False)

                def late(n):
                    name = ["nq0", "nq1", "kv0", "kv1", "kv2", "ga0", "ga1", "gb0", "gb1"][n]
                    for t in range(TT):
                        if name[0] == "n":
                            bank = filled_by(act, f"{name}{t}")
                            S.activation(nq[:, t, n * 512:n * 512 + 512], bank, ACT.Copy, scale=NSA_DH ** -0.5)
                            drain(S.activation(nq_rot[:, t, n * 512:n * 512 + 512], bank, ACT.Copy, scale=NSA_DH ** -0.5), f"{name}{t}")
                            continue
                        if name[0] == "k":
                            dst = nkv[:, t, (n - 2) * 512:(n - 2) * 512 + 512]
                        else:
                            dst = (mix_a if name[1] == "a" else mix_b)[:, t, (n - 5) % 2 * 512:(n - 5) % 2 * 512 + 512]
                        copy_out(f"{name}{t}", dst)
                    if n == 2:
                        bank = filled_by(act, "sel_gates")
                        drain(S.copy(sel_gates, grid(bank[:, 0:96], TT)), "sel_gates", wait=True)

                late(0)
                for n in range(1, len(LEVELS) + 1):
                    decay_of(n)
                    late(n)
                for key, dst, n in (("nqT", nqT, 4), ("nq_rotT", nq_rotT, 4), ("ksT", ksT, 2), ("kwT", kwT, 2)):
                    for f in range(n):
                        bank = filled_by(act, f"{key}{f}")
                        drain(S.copy(dst[:, 2 * f:2 * f + 2, :], grid(bank, 2)), f"{key}{f}")
                root(2)
                act.wait_ge(sem("cmp_hid_cleared"), 1)
                bank = filled_by(act, "cmp_hid")
                for r in (0, 64):
                    ins = S.activation(cmp_hid[r:r + 4 * N_CMP, :], bank[r:r + 4 * N_CMP, 0:CMP_HIDDEN], ACT.Gelu_apprx_tanh)
                drain(ins, "cmp_hid")
                exponentials(blocks2[0])
                bank = filled_by(act, "cmp_hidT")
                drain(S.copy(cmp_hidT, grid(bank[:, 0:2 * P], 2)), "cmp_hidT")
                exponentials(blocks2[1])
                drained_by(act, *[f"g{b}{c}{t}" for b in "ab" for c in range(2) for t in range(TT)])
                step(S.activation(sel_gates, sel_gates, ACT.Sigmoid), "sel_gates_ready", wait=False)
                step(S.activation(page(16), page(16), ACT.Sigmoid), "mix_gates_ready", wait=False)
                step(S.activation(page(17), page(17), ACT.Sigmoid), "mix_gates_ready", wait=False)
                turned("y_aT", y_aT)
                for t in range(TT):
                    act.wait_ge(sem("cmp_shifted"), t + 1)
                    live = cmp_p[:, t, :, 0:N_CMP]
                    step(S.activation(live, live, ACT.Exp), "cmp_exp_ready", wait=False)
                for t in range(TT):
                    bank = filled_by(act, f"cmpT{t}")
                    drain(S.copy(cmp_pT[:, t, :, :], grid(bank, NSA_KV)), f"cmpT{t}")
                for i in range(2, len(blocks2) + 2):
                    probs_turned(blocks2[i - 2])
                    if i < len(blocks2):
                        exponentials(blocks2[i])
                for t in range(TT):
                    half_turned("y_bT", y_bT, t)
                half_turned("mergedT", xT, 0)

                def residual(t):
                    for c in range(2):
                        copy_out(f"out2_{c}{t}", mlp_out[:, t, c * 512:c * 512 + 512])
                        if t == 0 and c == 0:
                            half_turned("mergedT", xT, 1)
                    root(2)
                    half_turned("mlpT", xT, t, "norm_pre_mlp_2")

                residual(0)
                residual(1)
                for c in range(8):
                    for f in range(2):
                        k = 4 * (c % 2) + 2 * f
                        bank = filled_by(act, f"up{c}{f}")
                        drain(S.activation(ffT[c // 2][:, k:k + 2, :], grid(bank, 2), ACT.Relu), f"up{c}{f}")
                copy_out("down00", mlp_out[:, 0, 0:512])
                copy_out("down01", mlp_out[:, 1, 0:512])
                for t in range(TT):
                    copy_out(f"down1{t}", mlp_out[:, t, 512:1024])
                    root()
                for c in range(2):
                    for t in range(TT):
                        copy_out(f"ple{c}{t}", ple[:, t, c * 512:c * 512 + 512])
                for t in range(TT):
                    half_turned("pleT", xT, t)
                for t in range(TT):
                    for c in range(2):
                        copy_out(f"ple_gate{c}{t}", ple_gate[:, t, c * 512:c * 512 + 512], ACT.Sigmoid)
                    root()
                assert counts["root_ready"] == len(roots)

            @block.gpsimd
            def _(pool):
                with nc.allow_non_contiguous_dma("small weights, read once"):
                    f0 = 3 * D_ATTN
                    pool.dma_start(forget_w[:, :, :], rows(d["w_in"][0], KT)[:, :, f0:f0 + HEADS]).then_inc(sem("forget_landed"), 16)
                    pool.dma_start(forget_b[:, :], d["b_forget"].rearrange("l h -> h l")).then_inc(sem("forget_landed"), 16)
                    pool.dma_start(route_w[:, :, 0:GROUPS], rows(d["w_route_group"][0], KT)).then_inc(sem("route_landed"), 16)
                    for g in range(GROUPS):
                        pool.dma_start(route_w[:, :, 4 + 8 * g:12 + 8 * g], rows(d["w_route_expert"][0, g], KT)).then_inc(sem("route_landed"), 16)
                    pool.dma_start(route_b[:, 0:4], d["b_route_group"][0].partition_broadcast(P)).then_inc(sem("route_landed"), 16)
                    pool.dma_start(route_b[:, 4:36], d["b_route_expert"][0].rearrange("g e -> (g e)").partition_broadcast(P)).then_inc(sem("route_landed"), 16)
                for f in range(2):
                    drained_by(pool, f"conv_a{f}")
                others = range(DVE_CONV, 4)
                for cb in others:
                    nc.gpsimd.tensor_scalar(conv[:, cb, :], z[:, cb, 0:T], tap(0, cb), col("b_dw", cb), ALU.mult, ALU.add).then_inc(sem("pool_added"), 1)
                for w in range(1, TAPS):
                    for n, cb in enumerate(others):
                        nc.gpsimd.tensor_scalar(glu[:, cb, :], z[:, cb, w:w + T], tap(w, cb), None, ALU.mult).then_inc(sem("pool_scaled"), 1)
                    for n, cb in enumerate(others):
                        pool.wait_ge(sem("pool_scaled"), len(others) * (w - 1) + n + 1)
                        pool.wait_ge(sem("pool_added"), len(others) * (w - 1) + n + 1)
                        ins = nc.gpsimd.tensor_tensor(conv[:, cb, :], conv[:, cb, :], glu[:, cb, :], ALU.add)
                        ins.then_inc(sem("conv_pool_ready" if w == TAPS - 1 and cb == 3 else "pool_added"), 1)
                    if w < TAPS - 1:
                        pool.wait_ge(sem("pool_added"), len(others) * (w + 1))
                filled_by(pool, "route1")
                pool.dma_start(gain_final, d["final_g"].partition_broadcast(P)).then_inc(sem("final_gain_landed"), 16)
                filled_by(pool, "hq00")
                pool.dma_start(gnorm, d["hg_gnorm_2"][0].partition_broadcast(P)).then_inc(sem("gnorm_landed"), 16)
                pool.dma_start(w_gates, rows(d["w_in_2"][0], KT)[:, :, 6656:6704]).then_inc(sem("gates_landed"), 16)
                with nc.allow_non_contiguous_dma("small weights, read once"):
                    for u in range(2):
                        pool.dma_start(cmp_wk2[:, :, u, :], rows(d["cmp_wk2_2"][0], 2)).then_inc(sem("cmp_w2_landed"), 16)
                    pool.dma_start(cmp_wv2, rows(d["cmp_wv2_2"][0], 2)).then_inc(sem("cmp_w2_landed"), 16)
                filled_by(pool, "y_bT10")
                for dst, name in ((gain_mix, "norm_post_mix_2"), (gain_mlp, "norm_post_mlp_2"), (gain_ple, "norm_ple_2")):
                    pool.dma_start(dst, d[name][0].partition_broadcast(P)).then_inc(sem("gains_landed"), 16)
                pool.dma_start(p_tok, d["p_2"][0, 0].rearrange("(t p) n -> p t n", p=P)).then_inc(sem("p_landed"), 16)

            @block.sync
            def _(sp):
                for t in range(TT):
                    sp.dma_start(x[:, t, :], d["x"][0, t * P:t * P + P, :]).then_inc(sem(f"x_landed{t}"), 16)
                sp.dma_start(consts[:, :], d["consts"]).then_inc(sem("consts_landed"), 16)
                row = 0
                for name, n in PARAM_ROWS:
                    v = d[name]
                    src = v.rearrange("l (r a) e -> (l r) (a e)", a=2) if name.startswith("cmp_pe") else v.rearrange("l (r e) -> (l r) e", e=P)
                    sp.dma_start(page(8, 0, P)[row:row + n, :], src).then_inc(sem("params_landed"), 16)
                    row += n
                sp.dma_start(page(8, P, P)[0:4 * TAPS, :], d["w_dw"].rearrange("l w (r e) -> (l w r) e", e=P)).then_inc(sem("params_landed"), 16)

                def load(n):
                    name, src, slot, k, w = units[n]
                    last = [m for m in range(n) if units[m][2] == slot]
                    if last and not (n >= n_early and last[-1] < n_early):
                        done = unit_last_fill[units[last[-1]][0]]
                        if isinstance(done, int):
                            sp.wait_ge(sem("down_used"), done)
                        else:
                            filled_by(sp, done)
                    sp.dma_start(slot_view(slot, k, w), src).then_inc(sem(f"weights_landed{slot}"), 16)

                for n in range(n_early):
                    load(n)
                    if n == 1:
                        sp.dma_start(mem_tok, d["mem"][0].rearrange("(t p) n -> p t n", p=P)).then_inc(sem("mem_landed"), 16)

                wg = d["w_gate"][0].rearrange("e (k p) n -> p e k n", p=P)
                wu = d["w_up"][0].rearrange("e (k p) n -> p e k n", p=P)
                wd = d["w_down"][0].rearrange("e (k p) n -> p e k n", p=P)

                def load_expert(which, e, landed):
                    src = (wg, wu, wd)[which // 2]
                    sp.dma_start(expert_w[which].unsqueeze(1), src[:, bass.ds(e, 1), :, :]).then_inc(landed[expert_slot[which]], 16)

                def load_pairs(tag, n_pairs, landed, first_waits):
                    for which in range(6):
                        first_waits(expert_slot[which])
                        load_expert(which, which % 2, landed)
                    with sp.Fori(1, n_pairs) as i:
                        for which in range(6):
                            sp.wait_ge(sem(f"{tag}_{('gate', 'up', 'down')[which // 2]}_filled"), 2 * i)
                            load_expert(which, 2 * (i % PAIRS) + which % 2, landed)

                def early_done(slot):
                    last = [m for m in range(n_early) if units[m][2] == slot][-1]
                    filled_by(sp, unit_last_fill[units[last][0]])

                def experts_done(tag, n_pairs):
                    for name in ("gate", "up", "down"):
                        sp.wait_ge(sem(f"{tag}_{name}_filled"), 2 * n_pairs)

                load_pairs("moe", PAIRS, [sem(f"weights_landed{b}") for b in range(6)], early_done)
                sp.wait_ge(sem("busiest_ready"), 1)
                count = sp.value_load(busiest[0:1, 0:1], min_val=0, max_val=T)
                experts_done("moe", PAIRS)
                with sp.If(count > CAP):
                    load_pairs("more", MORE, [sem(f"more_landed{b}") for b in range(6)], lambda slot: None)
                    experts_done("more", MORE)
                for n in range(n_early, len(units)):
                    load(n)
                for t in range(TT):
                    sp.wait_ge(sem("result_ready"), t + 1)
                    sp.dma_start(out[0, t * P:t * P + P, :], x[:, t, :]).then_inc(sem("out_stored"), 16)
                sp.wait_ge(sem("out_stored"), 16 * TT)


_INPUTS = ["x", "mem", "norm_mix_g", "w_in", "b_forget", "b_glu", "w_dw", "b_dw", "conv_ln_g", "conv_ln_b", "attn_out_g",
           "w_out", "norm_mem_g", "mem_norm_g", "w_mq", "w_mkv", "w_mo", "norm_ffn_g", "w_route_group", "b_route_group",
           "w_route_expert", "b_route_expert", "w_gate", "w_up", "w_down", "final_g", "p_2", "w_in_2", "w_branch_a_2",
           "w_branch_b_2", "w_out_2", "norm_pre_mix_2", "norm_post_mix_2", "norm_pre_mlp_2", "norm_post_mlp_2",
           "hg_lb_logits_2", "hg_gnorm_2", "cmp_pe_k_2", "cmp_pe_v_2", "cmp_wk1_2", "cmp_wk2_2", "cmp_wv1_2", "cmp_wv2_2",
           "w_up_2", "w_down_2", "w_ple_2", "w_ple_gate_2", "norm_ple_2"]


def kernel(**inputs):
    import concourse.bacc as bacc
    from concourse.bass_utils import run_bass_kernel_spmd

    nc = bacc.Bacc("TRN2", target_bir_lowering=False, num_devices=1)
    arrays, d = {}, {}
    for name in _INPUTS:
        a = np.ascontiguousarray(inputs[name])
        arrays[f"in_{name}"] = a
        d[name] = nc.dram_tensor(f"in_{name}", a.shape, mybir.dt.from_np(a.dtype), kind="ExternalInput").ap()
    table, const_cols = shape_constants()
    arrays["in_consts"] = table
    d["consts"] = nc.dram_tensor("in_consts", table.shape, F32, kind="ExternalInput").ap()
    out = nc.dram_tensor("out", (1, T, D), F32, kind="ExternalOutput").ap()
    two_blocks_kernel(nc, d, const_cols, out)
    r = run_bass_kernel_spmd(nc, [arrays], core_ids=[0])
    return r.results[0]["out"]
```

```python
from contextlib import ExitStack

import numpy as np
import concourse.bass as bass
from concourse import mybir

F32 = mybir.dt.float32
F32R = mybir.dt.float32r
I32 = mybir.dt.int32
U32 = mybir.dt.uint32
ALU = mybir.AluOpType
ACT = mybir.ActivationFunctionType
AX = mybir.AxisListType

P = 128
T, D = 256, 1024
TT, KT = T // P, D // P
EPS = 1e-6
BIG = 1e30
HEADS, HEAD_DIM = 8, 64
D_ATTN = HEADS * HEAD_DIM
D_CONV = D - D_ATTN
TAPS = 31
MEM_HEADS, MEM_DIM = 4, 256
GROUPS, PER_GROUP = 4, 8
EXPERTS = GROUPS * PER_GROUP
D_EXPERT = 512
CAP = 64
PASSES = T // CAP
PAIRS = EXPERTS // 2
MORE = PAIRS * (PASSES - 1)
HG_HEADS, CHUNK = 8, 64
NSA_HEADS, NSA_KV, NSA_DH = 16, 4, 64
CMP_LEN, CMP_STRIDE = 32, 16
N_CMP = (T - CMP_LEN) // CMP_STRIDE + 1
CMP_HIDDEN = 256
ROPE_DIM, ROPE_THETA = 16, 500000.0
D_FF = 4 * D
BANKS = 8
SLOT = 4096
PAGE = 2048
HEAD_OF = [0, 2, 4, 6, 1, 3, 5, 7]
DVE_CONV = 3
LEVELS = [1, 2, 4, 8, 16, 32, 64, 128]

PARAM_ROWS = [("norm_mix_g", 8), ("norm_mem_g", 8), ("mem_norm_g", 8), ("norm_ffn_g", 8),
              ("norm_pre_mix_2", 8), ("norm_pre_mlp_2", 8), ("attn_out_g", 4), ("b_glu", 8),
              ("b_dw", 4), ("conv_ln_g", 4), ("conv_ln_b", 4), ("hg_lb_logits_2", 16),
              ("cmp_pe_k_2", 16), ("cmp_pe_v_2", 16)]


def shape_constants():
    cols, parts = {}, []

    def put(name, a):
        a = np.asarray(a, np.float32).reshape(P, -1)
        start = sum(x.shape[1] for x in parts)
        cols[name] = (start, start + a.shape[1])
        parts.append(a)

    p = np.arange(P)
    put("ident", np.eye(P))
    put("ones", np.ones((P, T)))
    put("causal", np.concatenate([np.zeros((P, P)), np.where(p[None, :] <= p[:, None], 0.0, -BIG)], 1))
    put("earlier", p[:, None] < p[None, :])
    for L in LEVELS[:-1]:
        same = p[:, None] // (2 * L) == p[None, :] // (2 * L)
        put(f"level{L}", same & (p[:, None] // L % 2 == 0) & (p[None, :] // L % 2 == 1))
    put("chunk_reset", np.tile(np.arange(T) % CHUNK != 0, (P, 1)))
    put("slots", np.tile(np.arange(T + CAP), (P, 1)))
    half = ROPE_DIM // 2
    inv = (ROPE_THETA ** (-np.arange(half) * 2.0 / ROPE_DIM)).astype(np.float32)
    angle = np.arange(T, dtype=np.float32)[:, None] * inv[None, :]
    to_half = lambda a: a.reshape(TT, P, -1).transpose(1, 0, 2)
    put("cos", to_half(np.cos(angle)))
    put("sin", to_half(np.sin(angle)))
    end = np.arange(N_CMP) * CMP_STRIDE + CMP_LEN - 1
    seen = to_half((end[None, :] <= np.arange(T)[:, None]).astype(np.float32))
    put("cmp_seen", seen)
    put("cmp_bias", (seen - 1.0) * np.float32(BIG))
    return np.concatenate(parts, 1), cols


def parameter_columns(inputs):
    return np.ascontiguousarray(np.concatenate([inputs[name].reshape(-1, P) for name, _ in PARAM_ROWS] + [inputs["w_dw"].reshape(-1, P)]).T)


def two_blocks_kernel(nc, d, const_cols, out):
    ctx = ExitStack()
    with ctx:
        sb = lambda name, shape, dt=F32: ctx.enter_context(nc.sbuf_tensor(name, shape, dt))
        n_const = d["consts"].shape[1]
        with ExitStack() as names:
            parts_of_page = [names.enter_context(nc.sbuf_tensor(f"parts{n}", [P, PAGE], F32R)) for n in range(24)]
        ring = sb("ring", [P, 6 * SLOT])
        arena = sb("arena", [P, 12 * PAGE])
        consts = sb("consts", [P, n_const])
        cols = sb("cols", list(d["params"].shape))
        small = sb("small", [P, 512])
        route_w = sb("route_w", [P, KT, 36])
        route_b = sb("route_b", [P, 36])
        forget_w = sb("forget_w", [P, KT, HEADS])
        forget_b = sb("forget_b", [HEADS, 1])
        pos = sb("pos", [P, TT, EXPERTS])
        gate = sb("gate", [P, TT, EXPERTS])
        busiest = sb("busiest", [P, 1], I32)
        ps = ctx.enter_context(nc.psum_tensor("ps", [P, BANKS, 512], F32))

        sems = {}

        def sem(name):
            if name not in sems:
                sems[name] = ctx.enter_context(nc.semaphore(name))
            return sems[name]

        for b in range(BANKS):
            sem(f"bank_filled{b}"), sem(f"bank_drained{b}")

        def page(i, start=0, size=PAGE):
            if i < 12:
                return arena[:, i * PAGE + start:i * PAGE + start + size]
            at = 3 * SLOT + (i - 12) * PAGE
            return ring[:, at + start:at + start + size]

        def parts(i):
            return parts_of_page[12 + i if i < 12 else i - 6][:, :]

        def grid(flat, a):
            return flat.rearrange("p (a b) -> p a b", a=a)

        def const(name):
            a, b = const_cols[name]
            return consts[:, a:b]

        ident = const("ident")
        param_col, at = {}, 0
        for name, n in PARAM_ROWS:
            param_col[name] = at
            at += n
        taps_start = at

        def col(name, k=0, n=1):
            return cols[:, param_col[name] + k:param_col[name] + k + n]

        def tap(w, cb):
            k = taps_start + w * 4 + cb
            return cols[:, k:k + 1]

        x = grid(page(0), TT)
        normed = grid(page(1), TT)
        xT = grid(page(2), KT)
        qk1 = page(3)
        qT1, kT1 = grid(qk1[:, 0:1024], 4), grid(qk1[:, 1024:2048], 4)
        memT = grid(page(11), KT)
        mem_k, mem_v = grid(page(4), KT), grid(page(5), TT)
        mem_tok = grid(page(9), TT)
        mem_normed = grid(page(10), TT)
        v1 = grid(page(6, 0, 1024), TT)
        glu = grid(page(6, 1024, 1024), 4)
        ZW = TAPS - 1 + T
        z = grid(page(7, 0, 4 * ZW), 4)
        attn1 = grid(page(8, 1024, 1024), TT)
        conv = grid(page(8, 0, 1024), 4)
        catT = grid(page(2), KT)
        decay = page(7, 4 * ZW, 512)
        log_f, key_bias = decay[0:HEADS, 0:256], decay[0:HEADS, 256:512]
        qT2 = grid(page(3), KT)
        prob2 = page(6).rearrange("p (t h m) -> p t h m", t=TT, h=MEM_HEADS)
        prob2T = page(7).rearrange("p (h m q) -> p h m q", h=MEM_HEADS, m=TT)
        oT2 = grid(page(8), KT)
        logits = grid(page(11, 0, 72), TT)
        scratch_route = page(11, 128, 896)
        picked = grid(page(3, 0, 1024), KT)
        choose = grid(page(3, 1024, 256), TT)
        choose_gated = grid(page(3, 1280, 256), TT)
        spread = page(3, 1536, 256)
        hidden = page(4, 0, D_EXPERT)
        hiddenT = grid(page(4, 512, 512), 4)
        expert_out = page(4, 1024, 1024)
        hq, hb, hk = page(3), page(4), page(5)
        hx = [page(6), page(7)]
        scores_diag, scores_cross = page(8), page(9, 0, 1024)
        hv, hg = grid(page(10), TT), grid(page(11), TT)
        gnorm = page(9, 1024, 128)
        w_gates = page(9, 1152, KT * 48).rearrange("p (k n) -> p k n", k=KT)
        sel_gates = grid(page(9, 1536, 96), TT)
        nq, nq_rot = grid(page(12), TT), grid(page(13), TT)
        nkv = ring[:, 3 * SLOT + 2 * PAGE:3 * SLOT + 2 * PAGE + TT * 1536].rearrange("p (t n) -> p t n", t=TT)
        mix_a, mix_b = grid(page(16), TT), grid(page(10), TT)
        y_a = grid(page(8), TT)
        nqT, nq_rotT = grid(page(3), KT), grid(page(4), KT)
        ksT, kwT = grid(page(5, 0, 1024), 4), grid(page(5, 1024, 1024), 4)
        windows = page(7, 0, 4 * 4 * N_CMP * 8).rearrange("p (s b m j) -> p s b m j", s=2, b=2, j=8)
        y_b = grid(page(1), TT)
        y_aT = grid(page(11), KT)
        y_bT = grid(page(2), KT)
        cmp_p = page(9, 0, 1024).rearrange("p (t h n) -> p t h n", t=TT, h=NSA_HEADS)
        cmp_pT = page(13, 0, 1024).rearrange("p (t g q) -> p t g q", t=TT, g=NSA_KV)
        CMP = page(15)
        cmp_wk2 = CMP[:, 1024:1280].rearrange("p (c u n) -> p c u n", c=2, u=2)
        cmp_wv2 = CMP[:, 1280:1408].rearrange("p (c n) -> p c n", c=2)
        cmp_hid = CMP[:, 1408:1664]
        cmp_hidT = CMP[:, 1664:1920].rearrange("p (c n) -> p c n", c=2)
        cmp_kT = CMP[:, 1920:1980]
        cmp_v = page(13, 1024, 1024).rearrange("p (g n) -> p g n", g=NSA_KV)
        ffT = [grid(page(3 + n), KT) for n in range(4)]
        mlp_out = grid(page(7), TT)
        p_tok = grid(page(8, 0, 512), TT)
        pT = grid(page(8, 512, 512), TT)
        ple = grid(page(9), TT)
        ple_gate = grid(page(10), TT)
        mix_high, mix_rest = [grid(parts(n), KT) for n in (5, 1)]
        mem_high, mem_rest = grid(parts_of_page[8][:, :], KT), grid(parts(11), KT)
        cross_high, cross_rest = [grid(parts(n), KT) for n in (8, 11)]
        proj_high, proj_rest = [grid(parts(n), KT) for n in (17, 1)]
        x_high, x_rest = [grid(parts(n), KT) for n in (9, 10)]
        ff_high = [grid(parts(14 + n), KT) for n in range(4)]
        ff_rest = [grid(parts(3 + n), KT) for n in range(4)]
        gain_final, gain_mix = page(11, 1024, 1024), page(12, 0, 1024)
        gain_mlp, gain_ple = page(12, 1024, 1024), page(13, 0, 1024)

        rows = lambda w, k: w.rearrange("(k p) n -> p k n", k=k)
        units, unit_at = [], {}

        def unit(name, src, k, n, n_slots):
            slot = len(units) % 4
            if n_slots == 3:
                m = len(units) - n_early
                slot = (2, 1)[m] if m < 2 else m % 2 if m < 17 else (m - 16) % 3
            unit_at[name] = (len(units), slot, k, n)
            units.append((name, src, slot, k, n))

        off_c = 3 * D_ATTN + HEADS
        for name, start in (("conv_g", off_c + D_CONV), ("conv_a", off_c), ("q", 0), ("k", D_ATTN), ("v", 2 * D_ATTN)):
            unit(name, rows(d["w_in"][0], KT)[:, :, start:start + 512], KT, 512, 4)
        for c in range(4):
            unit(f"mem_kv{c}", rows(d["w_mkv"][0], KT)[:, :, c * 512:c * 512 + 512], KT, 512, 4)
        for key, w in (("out", "w_out"), ("mem_q", "w_mq"), ("mem_o", "w_mo")):
            for c in range(2):
                unit(f"{key}{c}", rows(d[w][0], KT)[:, :, c * 512:c * 512 + 512], KT, 512, 4)
        n_early = len(units)
        expert_places = [("pages", 9), ("pages", 5), ("pages", 7)] + [("slot", n) for n in (4, 5, 3, 0, 1, 2)]
        N_PLACES = len(expert_places)
        PERIOD = 3
        off = [0, 512, 1024, 1536, 2048, 2560, 3072, 3584, 4096, 4608, 5120, 5632, 6144, 6704, 7216, 7728, 8240]
        names2 = ["hq0", "hq1", "hf0", "hf1", "hi0", "hi1", "hg0", "hg1", "nq0", "nq1",
                  "kv0", "kv1", "kv2", "ga0", "ga1", "gb0", "gb1"]
        for name, start in zip(names2, off):
            unit(name, rows(d["w_in_2"][0], KT)[:, :, start:start + 512], KT, 512, 3)
        for c in "kv":
            unit(f"cmp_{c}", rows(d[f"cmp_w{c}1_2"][0], 16), 16, CMP_HIDDEN, 3)
        for c in range(2):
            unit(f"branch_a{c}", rows(d["w_branch_a_2"][0], KT)[:, :, c * 512:c * 512 + 512], KT, 512, 3)
        for key, w in (("branch_b", "w_branch_b_2"), ("out2_", "w_out_2")):
            for c in range(2):
                unit(f"{key}{c}", rows(d[w][0], KT)[:, :, c * 512:c * 512 + 512], KT, 512, 3)
        for c in range(8):
            unit(f"up{c}", rows(d["w_up_2"][0], KT)[:, :, c * 512:c * 512 + 512], KT, 512, 3)
        for c in range(2):
            for k in range(4):
                unit(f"down{c}{k}", rows(d["w_down_2"][0][k * D:k * D + D], KT)[:, :, c * 512:c * 512 + 512], KT, 512, 3)
        unit("ple", rows(d["w_ple_2"][0], 2), 2, D, 3)
        for c in range(2):
            unit(f"ple_gate{c}", rows(d["w_ple_gate_2"][0], KT)[:, :, c * 512:c * 512 + 512], KT, 512, 3)

        split_stages = {"mixer": ["q", "k", "v"] + [f"mem_kv{c}" for c in range(4)],
                        "cross": ["mem_q1"],
                        "proj": names2[2:],
                        "mlp": [f"up{c}" for c in range(1, 8)] + [f"down{c}{k}" for c in range(2) for k in range(4)]}
        w_high = {"mixer": [grid(parts_of_page[n][:, :], KT // 2) for n in (10, 11)],
                  "cross": [grid(parts(n), KT // 2) for n in (6, 7)],
                  "proj": [grid(parts_of_page[n][:, :], KT // 2) for n in (4, 5)],
                  "mlp": [grid(parts(n), KT // 2) for n in (11, 2)]}
        last_in_place = {"mixer": [None, None], "cross": [None, None], "proj": ["hq0", "hq0"], "mlp": [None, "up0"]}
        split_at = {name: (stage, u) for stage, names in split_stages.items() for u, name in enumerate(names)}

        def by_halves(name):
            return split_at.get(name, ("", 0))[0] == "proj"

        landed_value, loads = {}, [0] * 6
        for n, (name, _, slot, _, _) in enumerate(units):
            if n == n_early:
                before_experts = list(loads)
                for m in range(6 * PAIRS):
                    kind, at = expert_places[m % N_PLACES]
                    if kind == "slot":
                        loads[at] += 16
            if not by_halves(name):
                loads[slot] += 16
                landed_value[name] = loads[slot]

        def slot_view(slot, k, n):
            return ring[:, slot * SLOT:slot * SLOT + k * n].rearrange("p (k n) -> p k n", k=k)

        def expert_view(m):
            kind, at = expert_places[m % N_PLACES]
            flat = arena[:, at * PAGE:at * PAGE + SLOT] if kind == "pages" else ring[:, at * SLOT:at * SLOT + SLOT]
            return grid(flat, 4 if m % 6 >= 4 else KT)

        def expert_landed(tag, m):
            kind, at = expert_places[m % N_PLACES]
            if kind == "slot" and tag == "moe":
                return sem(f"weights_landed{at}"), before_experts[at]
            return sem(f"{tag}_landed{m % N_PLACES}"), 0

        fills, unit_last_fill = {}, {}

        def filled_by(eng, name):
            n = fills[name]
            eng.wait_ge(sem(f"bank_filled{n % BANKS}"), n // BANKS + 1)
            return ps[:, n % BANKS, :]

        def drained_by(eng, *names):
            for name in names:
                n = fills[name]
                eng.wait_ge(sem(f"bank_drained{n % BANKS}"), n // BANKS + 1)

        blocks1 = [dict(name=f"fa{t}", t=t, nk=P * (t + 1), n=t, scale=HEAD_DIM ** -0.5,
                        p=page(9 + t, 0, HEADS * P * (t + 1)).rearrange("p (h k) -> p h k", h=HEADS),
                        pt=(page(9, 1024, 1024) if t == 0 else page(1)).rearrange("p (n q) -> p n q", q=P),
                        q=lambda h, t=t: qT1[64 * (h % 2):64 * (h % 2) + 64, h // 2, t * P:t * P + P],
                        k=lambda h, nk: kT1[64 * (h % 2):64 * (h % 2) + 64, h // 2, 0:nk],
                        v=lambda h, j: v1[:, j, h * 64:h * 64 + 64], bias=True) for t in range(TT)]
        blocks2 = []
        for branch, (kT, v0) in enumerate(((ksT, 768), (kwT, 1280))):
            for t in range(TT):
                for half in range(2):
                    n = len(blocks2)
                    blocks2.append(dict(
                        name=f"nsa{branch}{t}{half}", t=t, nk=P * (t + 1), n=2 + n, scale=1.0, branch=branch, half=half,
                        p=page((6, 7, 17)[n % 3], 0, HEADS * P * (t + 1)).rearrange("p (h k) -> p h k", h=HEADS),
                        pt=page((8, 12)[n % 2], 0, HEADS * P * (t + 1)).rearrange("p (n q) -> p n q", q=P),
                        q=lambda h, t=t, half=half: nq_rotT[64 * (h % 2):64 * (h % 2) + 64, 4 * half + h // 2, t * P:t * P + P],
                        k=lambda h, nk, kT=kT, half=half: kT[64 * (h % 2):64 * (h % 2) + 64, 2 * half + h // 4, 0:nk],
                        v=lambda h, j, v0=v0, half=half: nkv[:, j, v0 + (2 * half + h // 4) * 64:v0 + (2 * half + h // 4) * 64 + 64],
                        bias=False))

        def split_half(name, h):
            _, slot, k, n = unit_at[name]
            return slot_view(slot, k, n)[:, 4 * h:4 * h + 4, :]

        def rest_half(name, h):
            return grid(parts_of_page[2 * unit_at[name][1] + h][:, :], 4)

        def stat(k, n):
            return small[:, k:k + n]

        def block_stats(blk):
            return [stat(64 + 24 * blk["n"] + 8 * j, 8) for j in range(3)]

        with nc.Block() as block:

            @block.tensor
            def _(pe):
                def open_bank(name):
                    n = fills[name] = len(fills)
                    if n >= BANKS:
                        pe.wait_ge(sem(f"bank_drained{n % BANKS}"), n // BANKS)
                    return ps[:, n % BANKS, :]

                def close_bank(ins, name):
                    ins.then_inc(sem(f"bank_filled{fills[name] % BANKS}"), 1)

                def use(name):
                    _, slot, k, n = unit_at[name]
                    pe.wait_ge(sem(f"weights_landed{slot}"), landed_value[name])
                    return slot_view(slot, k, n)

                def feature_major(name, tag, rhs):
                    w = use(name)
                    for c in range(2):
                        bank = open_bank(f"{tag}{c}")
                        for half in range(2):
                            at = (2 * c + half) * P
                            for k in range(KT):
                                mm = nc.tensor.matmul(bank[:, half * T:half * T + T], w[:, k, at:at + P], rhs[:, k, :],
                                                      start=k == 0, stop=k == KT - 1)
                        close_bank(mm, f"{tag}{c}")
                    unit_last_fill[name] = f"{tag}1"

                def token_major(name, tag, lhs):
                    w = use(name)
                    for t in range(TT):
                        bank = open_bank(f"{tag}{t}")
                        for k in range(KT):
                            mm = nc.tensor.matmul(bank, lhs[:, k, t * P:t * P + P], w[:, k, :],
                                                  start=k == 0, stop=k == KT - 1)
                        close_bank(mm, f"{tag}{t}")
                    unit_last_fill[name] = f"{tag}1"

                def transposes(tag, src):
                    for j in range(4):
                        bank = open_bank(f"{tag}{j}")
                        for k in (2 * j, 2 * j + 1):
                            for t in range(TT):
                                at = (k % 2) * T + t * P
                                mm = nc.tensor.transpose(bank[:, at:at + P], src[:, t, k * P:k * P + P], ident)
                        close_bank(mm, f"{tag}{j}")

                def part_pairs(name, h, high, rest):
                    stage, u = split_at[name]
                    pe.wait_ge(sem(f"{stage}_rest_ready"), 2 * u + h + 1)
                    w = w_high[stage][h], rest_half(name, h)
                    return [(w[0], high), (w[1], high), (w[0], rest)]

                def half_used(mm, name):
                    mm.then_inc(sem(f"{split_at[name][0]}_half_used"), 1)

                def split_feature_major(name, tag, high, rest, between=None):
                    banks = [open_bank(f"{tag}{f}") for f in range(2)]
                    for h in range(2):
                        if h and between:
                            between()
                        pairs = part_pairs(name, h, high, rest)
                        for f in range(2):
                            for half in range(2):
                                at = (2 * f + half) * P
                                for k in range(4):
                                    for n, (w, v) in enumerate(pairs):
                                        mm = nc.tensor.matmul(banks[f][:, half * T:half * T + T], w[:, k, at:at + P], v[:, 4 * h + k, :],
                                                              start=h + half + k + n == 0,
                                                              stop=h + half == 2 and k == 3 and n == 2)
                            if h:
                                close_bank(mm, f"{tag}{f}")
                        if h == 0:
                            half_used(mm, name)
                    unit_last_fill[name] = f"{tag}1"

                def split_token_major(name, tag, high, rest, between=None):
                    banks = [open_bank(f"{tag}{t}") for t in range(TT)]
                    for h in range(2):
                        if h and between:
                            between()
                        pairs = part_pairs(name, h, high, rest)
                        for t in range(TT):
                            for k in range(4):
                                for n, (w, v) in enumerate(pairs):
                                    mm = nc.tensor.matmul(banks[t], v[:, 4 * h + k, t * P:t * P + P], w[:, k, :],
                                                          start=h + k + n == 0, stop=h == 1 and k == 3 and n == 2)
                            if h:
                                close_bank(mm, f"{tag}{t}")
                        if h == 0:
                            half_used(mm, name)
                    unit_last_fill[name] = f"{tag}1"

                def turn_half(tag, src, t):
                    for f in range(2):
                        bank = open_bank(f"{tag}{t}{f}")
                        for j in range(4):
                            k = 4 * f + j
                            mm = nc.tensor.transpose(bank[:, j * P:j * P + P], src[:, t, k * P:k * P + P], ident)
                        close_bank(mm, f"{tag}{t}{f}")

                def half_turned(tag, t):
                    drained_by(pe, f"{tag}{t}0", f"{tag}{t}1")

                def token_pair(names, lhs, before_part):
                    w = [use(name) for name in names]
                    for t in range(TT):
                        for c, name in enumerate(names):
                            if (t, c) in before_part:
                                before_part[t, c]()
                            bank = open_bank(f"{name}{t}")
                            for k in range(KT):
                                mm = nc.tensor.matmul(bank, lhs[:, k, t * P:t * P + P], w[c][:, k, :], start=k == 0, stop=k == KT - 1)
                            close_bank(mm, f"{name}{t}")
                    for name in names:
                        unit_last_fill[name] = f"{name}1"

                def feature_pair(names, rhs, turn_second, second_turned):
                    w = [use(names[0])]
                    banks = {}
                    for t in range(TT):
                        if t == 1:
                            if len(names) == 1:
                                turn_second()
                            second_turned()
                        for u, name in enumerate(names):
                            if t == 0 and u == 1:
                                turn_second()
                                w.append(use(name))
                            for c in range(2):
                                if t == 0:
                                    banks[u, c] = open_bank(f"{name}{c}")
                                for half in range(2):
                                    at, to = (2 * c + half) * P, half * T + t * P
                                    for k in range(KT):
                                        mm = nc.tensor.matmul(banks[u, c][:, to:to + P], w[u][:, k, at:at + P], rhs[:, k, t * P:t * P + P],
                                                              start=k == 0, stop=k == KT - 1)
                                if t == 1:
                                    close_bank(mm, f"{name}{c}")
                    for name in names:
                        unit_last_fill[name] = f"{name}1"

                def normed_half(tag, t, count):
                    pe.wait_ge(sem("x_normed"), count)
                    turn_half(tag, normed, t)

                def scores(blk):
                    nk = blk["nk"]
                    per = 512 // nk
                    for f in range(HEADS // per):
                        name = f"{blk['name']}S{f}"
                        bank = open_bank(name)
                        for j in range(per):
                            h = HEAD_OF[f * per + j]
                            o = bank[:, j * nk:j * nk + nk]
                            mm = nc.tensor.matmul(o, blk["q"](h), blk["k"](h, nk), start=True, stop=not blk["bias"])
                            if blk["bias"]:
                                mm = nc.tensor.matmul(o, ident[0:HEADS, h:h + 1].to_broadcast([HEADS, P]),
                                                      key_bias[:, 0:nk], start=False, stop=True)
                        close_bank(mm, name)

                def turn_probs(blk):
                    pe.wait_ge(sem("probs_ready"), blk["n"] + 1)
                    tiles = HEADS * blk["nk"] // P
                    flat = blk["p"].rearrange("p h (j k) -> p (h j) k", k=P)
                    for f in range(tiles // 4):
                        name = f"{blk['name']}T{f}"
                        bank = open_bank(name)
                        for j in range(4):
                            mm = nc.tensor.transpose(bank[:, j * P:j * P + P], flat[:, 4 * f + j, :], ident)
                        close_bank(mm, name)

                def weigh_values(blk):
                    nj = blk["nk"] // P
                    drained_by(pe, *[f"{blk['name']}T{f}" for f in range(HEADS * nj // 4)])
                    bank = open_bank(f"{blk['name']}O")
                    for n, h in enumerate(HEAD_OF):
                        for j in range(nj):
                            mm = nc.tensor.matmul(bank[:, h * 64:h * 64 + 64], blk["pt"][:, n * nj + j, :], blk["v"](h, j),
                                                  start=j == 0, stop=j == nj - 1)
                    close_bank(mm, f"{blk['name']}O")

                pe.wait_ge(sem("ident_landed"), 16)
                normed_half("mixT", 0, 1)
                half_turned("mixT", 0)
                feature_pair(["conv_g", "conv_a"], xT, lambda: normed_half("mixT", 1, 2), lambda: half_turned("mixT", 1))
                pe.wait_ge(sem("mixer_x_rest_ready"), 1)
                split_feature_major("q", "q", mix_high, mix_rest)
                split_feature_major("k", "k", mix_high, mix_rest)
                pe.wait_ge(sem("mem_normed"), 2)
                transposes("memT", mem_normed)
                pe.wait_ge(sem("forget_landed"), 32)
                bank = open_bank("forget")
                for k in range(KT):
                    mm = nc.tensor.matmul(bank[0:HEADS, 0:T], forget_w[:, k, :], xT[:, k, :], start=k == 0, stop=k == KT - 1)
                close_bank(mm, "forget")
                split_token_major("v", "v", mix_high, mix_rest)
                pe.wait_ge(sem("mem_x_rest_ready"), 1)
                for c in range(2):
                    split_feature_major(f"mem_kv{c}", f"mem_k{c}", mem_high, mem_rest)
                pe.wait_ge(sem("key_bias_ready"), 1)
                drained_by(pe, "q0", "q1", "k0", "k1", "v0", "v1")
                for blk in blocks1:
                    scores(blk)
                split_token_major("mem_kv2", "mem_v0", mem_high, mem_rest)
                for blk in blocks1:
                    turn_probs(blk)
                pe.wait_ge(sem("consts_landed"), 16)
                def channel_sums(name, src):
                    bank = open_bank(name)
                    for cb in range(4):
                        mm = nc.tensor.matmul(bank[:, 0:T], const("ones")[:, 0:P], src[:, cb, :], start=cb == 0, stop=cb == 3)
                    close_bank(mm, name)

                pe.wait_ge(sem("conv_ready"), 1)
                pe.wait_ge(sem("conv_pool_ready"), 1)
                channel_sums("conv_mean", conv)
                for blk in blocks1:
                    weigh_values(blk)
                pe.wait_ge(sem("conv_ready"), 2)
                channel_sums("conv_var", glu)
                def turn_attention():
                    for t in range(TT):
                        pe.wait_ge(sem("attn1_normed"), t + 1)
                        bank = open_bank(f"attn1T{t}")
                        for k in range(4):
                            mm = nc.tensor.transpose(bank[:, k * P:k * P + P], attn1[:, t, k * P:k * P + P], ident)
                        close_bank(mm, f"attn1T{t}")

                split_token_major("mem_kv3", "mem_v1", mem_high, mem_rest, turn_attention)
                drained_by(pe, "attn1T0", "attn1T1")
                pe.wait_ge(sem("conv_done"), 4)
                token_pair(["out0", "out1"], catT, {(1, 1): lambda: normed_half("normT", 0, 3)})
                half_turned("normT", 0)
                feature_pair(["mem_q0"], xT, lambda: normed_half("normT", 1, 4), lambda: half_turned("normT", 1))
                pe.wait_ge(sem("cross_x_rest_ready"), 1)

                def cross_scores(f):
                    drained_by(pe, f"mem_q{f}0", f"mem_q{f}1")
                    for t in range(TT):
                        bank = open_bank(f"crossS{t}{f}")
                        for j in range(2):
                            h = 2 * f + j
                            for c in range(2):
                                mm = nc.tensor.matmul(bank[:, j * T:j * T + T], qT2[:, 2 * h + c, t * P:t * P + P],
                                                      mem_k[:, 2 * h + c, :], start=c == 0, stop=c == 1)
                        close_bank(mm, f"crossS{t}{f}")

                split_feature_major("mem_q1", "mem_q1", cross_high, cross_rest, lambda: cross_scores(0))

                def turn_cross_probs(f):
                    for t in range(TT):
                        pe.wait_ge(sem("cross_probs_ready"), 2 * f + t + 1)
                        bank = open_bank(f"crossT{t}{f}")
                        for j in range(4):
                            h, m = 2 * f + j // 2, j % 2
                            mm = nc.tensor.transpose(bank[:, j * P:j * P + P], prob2[:, t, h, m * P:m * P + P], ident)
                        close_bank(mm, f"crossT{t}{f}")

                def cross_outputs(f):
                    drained_by(pe, f"crossT0{f}", f"crossT1{f}")
                    for h in (2 * f, 2 * f + 1):
                        bank = open_bank(f"crossO{h}")
                        for c in range(2):
                            for m in range(TT):
                                mm = nc.tensor.matmul(bank[:, c * T:c * T + T], mem_v[:, m, (2 * h + c) * P:(2 * h + c) * P + P],
                                                      prob2T[:, h, m, :], start=m == 0, stop=m == TT - 1)
                        close_bank(mm, f"crossO{h}")

                turn_cross_probs(0)
                cross_scores(1)
                cross_outputs(0)
                turn_cross_probs(1)
                cross_outputs(1)
                drained_by(pe, *[f"crossO{f}" for f in range(4)])
                def route(t):
                    half_turned("ffnT", t)
                    bank = open_bank(f"route{t}")
                    for k in range(KT):
                        mm = nc.tensor.matmul(bank[:, 0:36], xT[:, k, t * P:t * P + P], route_w[:, k, :], start=k == 0, stop=k == KT - 1)
                    close_bank(mm, f"route{t}")

                def route_first():
                    normed_half("ffnT", 0, 5)
                    pe.wait_ge(sem("route_landed"), 16 * (GROUPS + 3))
                    route(0)

                token_pair(["mem_o0", "mem_o1"], oT2, {(1, 1): route_first})
                normed_half("ffnT", 1, 6)
                route(1)
                pe.wait_ge(sem("choice_ready"), 1)
                chosen = grid(scratch_route[:, 0:64], TT)
                bank = open_bank("rank")
                ones = const("ones")[:, 0:P]
                nc.tensor.matmul(bank[:, 0:32], const("earlier"), chosen[:, 0, :], start=True, stop=True)
                nc.tensor.matmul(bank[:, 32:64], const("earlier"), chosen[:, 1, :], start=True, stop=False)
                nc.tensor.matmul(bank[:, 32:64], ones, chosen[:, 0, :], start=False, stop=True)
                nc.tensor.matmul(bank[:, 64:96], ones, chosen[:, 0, :], start=True, stop=False)
                close_bank(nc.tensor.matmul(bank[:, 64:96], ones, chosen[:, 1, :], start=False, stop=True), "rank")

                def experts(tag, n_pairs):
                    s = lambda name: sem(f"{tag}_{name}")

                    def gather(n, first=False):
                        pe.wait_ge(s("choose_ready"), n + 1)
                        for f, b in ((0, 0), (1, 7)):
                            if not first:
                                pe.wait_ge(s("picked_drained"), 2 * n - 1 + f)
                            for k in range(4 * f, 4 * f + 4):
                                for t in range(TT):
                                    mm = nc.tensor.matmul(ps[:, b, (k % 4) * P:(k % 4) * P + P], normed[:, t, k * P:k * P + P],
                                                          choose[:, t, :], start=t == 0, stop=t == TT - 1)
                            mm.then_inc(s("picked_filled"), 1)

                    def product(group, r, first, tiles, name):
                        src = hiddenT if first == 4 else picked
                        for m in (6 * r + first, 6 * r + first + 1):
                            landed, before = expert_landed(tag, m)
                            pe.wait_ge(landed, before + 16 * (6 * PERIOD // N_PLACES * group + m // N_PLACES + 1))
                        w = [expert_view(6 * r + first + e) for e in range(2)]
                        n_k = src.shape[1]
                        for c, bank in enumerate(tiles):
                            for k in range(n_k):
                                for e in range(2):
                                    mm = nc.tensor.matmul(ps[e * CAP:e * CAP + CAP, bank, :], src[:, k, e * CAP:e * CAP + CAP],
                                                          w[e][:, k, c * 512:c * 512 + 512], start=k == 0, stop=k == n_k - 1)
                                    if c == len(tiles) - 1 and k == n_k - 1:
                                        mm.then_inc(s(name), 1)

                    def scatter(n):
                        pe.wait_ge(s("spread_ready"), n + 1)
                        pe.wait_ge(s("out_ready"), 2 * n + 2)
                        for t in range(TT):
                            for c in range(2):
                                if t:
                                    pe.wait_ge(s("sum_drained"), 4 * n + c + 1)
                                nc.tensor.matmul(ps[:, 5 + c, :], spread[:, t * P:t * P + P],
                                                 expert_out[:, c * 512:c * 512 + 512], start=True, stop=True).then_inc(s("sum_filled"), 1)

                    gather(0, first=True)
                    def pair(group, r):
                        n = PERIOD * group + r
                        pe.wait_ge(s("picked_drained"), 2 * n + 2)
                        product(group, r, 0, [1], "gate_filled")
                        scatter(n)
                        product(group, r, 2, [2], "up_filled")
                        gather(n + 1)
                        pe.wait_ge(s("hidden_ready"), n + 1)
                        for k in range(4):
                            mm = nc.tensor.transpose(ps[:, 1, k * P:k * P + P], hidden[:, k * P:k * P + P], ident)
                        mm.then_inc(s("hidden_turned"), 1)
                        pe.wait_ge(s("gated_choose_ready"), n + 1)
                        pe.wait_ge(s("sum_drained"), 4 * n + 4)
                        for t in range(TT):
                            mm = nc.tensor.transpose(ps[:, 5, t * P:t * P + P], choose_gated[:, t, :], ident)
                        mm.then_inc(s("spread_filled"), 1)
                        pe.wait_ge(s("hiddenT_ready"), n + 1)
                        product(group, r, 4, [3, 4], "down_filled")
                    with pe.Fori(0, n_pairs // PERIOD) as group:
                        for r in range(PERIOD):
                            pair(group, r)
                    for r in range(n_pairs % PERIOD):
                        pair(n_pairs // PERIOD, r)
                    scatter(n_pairs)
                    pe.wait_ge(s("sum_drained"), 4 * n_pairs + 4)

                for b in range(BANKS):
                    pe.wait_ge(sem(f"bank_drained{b}"), len([v for v in fills.values() if v % BANKS == b]))
                experts("moe", PAIRS)
                pe.wait_ge(sem("busiest_ready"), 1)
                count = pe.value_load(busiest[0:1, 0:1], min_val=0, max_val=T)
                with pe.If(count > CAP):
                    experts("more", MORE)

                normed_half("mix2T", 0, 7)
                half_turned("mix2T", 0)
                feature_pair(["hq0", "hq1"], xT, lambda: normed_half("mix2T", 1, 8), lambda: half_turned("mix2T", 1))
                pe.wait_ge(sem("proj_x_rest_ready"), 1)
                for c in range(2):
                    split_feature_major(f"hf{c}", f"hf{c}", proj_high, proj_rest)

                def level(n):
                    pe.wait_ge(sem("level_ready"), n + 1)
                    if n and LEVELS[n - 1] == P:
                        src = grid(hx[n % 2], HG_HEADS)
                        for f in range(2):
                            bank = open_bank(f"level{n}_{f}")
                            for j in range(4):
                                h = 4 * f + j
                                mm = nc.tensor.matmul(bank[:, j * P:j * P + P], src[:, h, 0:P], src[:, h, P:T], start=True, stop=True)
                            close_bank(mm, f"level{n}_{f}")
                        return
                    left, right = (grid(hk, HG_HEADS), grid(hq, HG_HEADS)) if n == 0 else [grid(hx[n % 2], HG_HEADS)] * 2
                    for f in range(4):
                        bank = open_bank(f"level{n}_{f}")
                        for j in range(4):
                            h, t = 2 * f + j // 2, j % 2
                            mm = nc.tensor.matmul(bank[:, j * P:j * P + P], left[:, h, t * P:t * P + P], right[:, h, t * P:t * P + P],
                                                  start=True, stop=True)
                        close_bank(mm, f"level{n}_{f}")

                for n in range(len(LEVELS) + 1):
                    split_token_major(split_stages["proj"][2 + n], split_stages["proj"][2 + n], proj_high, proj_rest)
                    if n == 6:
                        pe.wait_ge(sem("gates_landed"), 16)
                        bank = open_bank("sel_gates")
                        for t in range(TT):
                            for k in range(KT):
                                mm = nc.tensor.matmul(bank[:, t * 48:t * 48 + 48], xT[:, k, t * P:t * P + P], w_gates[:, k, :],
                                                      start=k == 0, stop=k == KT - 1)
                        close_bank(mm, "sel_gates")
                    level(n)
                for c in range(2):
                    split_token_major(f"ga{c}", f"ga{c}", proj_high, proj_rest)
                drained_by(pe, *[f"level{len(LEVELS)}_{f}" for f in range(2)])
                drained_by(pe, *[f"hi{c}{t}" for c in range(2) for t in range(TT)])
                diag = scores_diag.rearrange("p (h t q) -> p h t q", h=HG_HEADS, t=TT)
                cross = grid(scores_cross, HG_HEADS)
                for t in range(TT):
                    for f in range(2):
                        bank = open_bank(f"rec{t}{f}")
                        for j in range(4):
                            h = 4 * f + j
                            o = bank[:, j * P:j * P + P]
                            mm = nc.tensor.matmul(o, diag[:, h, t, :], hv[:, t, h * P:h * P + P], start=True, stop=t == 0)
                            if t:
                                mm = nc.tensor.matmul(o, cross[:, h, :], hv[:, 0, h * P:h * P + P], start=False, stop=True)
                        close_bank(mm, f"rec{t}{f}")
                for c in range(2):
                    split_token_major(f"gb{c}", f"gb{c}", proj_high, proj_rest)
                def both_halves(key, start):
                    for f in range(2):
                        bank = open_bank(f"{key}T{f}")
                        for j in range(2):
                            g = 2 * f + j
                            for t in range(TT):
                                for u in range(2):
                                    mm = nc.tensor.matmul(bank[64 * u:64 * u + 64, j * T + t * P:j * T + t * P + P],
                                                          nkv[:, t, start + g * 64:start + g * 64 + 64], ident, start=True, stop=True)
                        close_bank(mm, f"{key}T{f}")

                drained_by(pe, *[f"{u}{t}" for u in ("nq0", "nq1", "kv0") for t in range(TT)])
                both_halves("kc", 0)
                both_halves("vc", 256)
                transposes("nqT", nq)
                pe.wait_ge(sem("rotated"), 3 * TT)
                transposes("nq_rotT", nq_rot)
                both_halves("ks", 512)
                both_halves("kw", 1024)
                drained_by(pe, "kcT0", "kcT1", "vcT0", "vcT1")
                w = [use("cmp_k"), use("cmp_v")]
                bank = open_bank("cmp_hid")
                for j in range(CMP_LEN // 2):
                    for kv in range(2):
                        mm = nc.tensor.matmul(bank[64 * kv:64 * kv + 4 * N_CMP, 0:CMP_HIDDEN], windows[:, kv, j // 8, :, j % 8], w[kv][:, j, :],
                                              start=j == 0, stop=j == CMP_LEN // 2 - 1)
                close_bank(mm, "cmp_hid")
                unit_last_fill["cmp_k"] = unit_last_fill["cmp_v"] = "cmp_hid"
                drained_by(pe, *[f"nq_rotT{j}" for j in range(4)], "ksT0", "ksT1", "kwT0", "kwT1")
                scores(blocks2[0])
                scores(blocks2[1])
                drained_by(pe, "cmp_hid")
                bank = open_bank("cmp_hidT")
                for c in range(2):
                    mm = nc.tensor.transpose(bank[:, c * P:c * P + P], cmp_hid[:, c * P:c * P + P], ident)
                close_bank(mm, "cmp_hidT")
                pe.wait_ge(sem("y_a_ready"), 1)
                transposes("y_aT", y_a)
                drained_by(pe, "cmp_hidT")
                pe.wait_ge(sem("cmp_w2_landed"), 48)
                bank = open_bank("cmp_kT")
                for c in range(2):
                    mm = nc.tensor.matmul(bank[:, 0:4 * N_CMP], cmp_wk2[:, c, :, :].rearrange("p u n -> p (u n)"), cmp_hidT[:, c, 0:4 * N_CMP],
                                          start=c == 0, stop=c == 1)
                close_bank(mm, "cmp_kT")
                bank = open_bank("cmp_v")
                for g in range(NSA_KV):
                    for c in range(2):
                        mm = nc.tensor.matmul(bank[0:N_CMP, g * 64:g * 64 + 64], cmp_hidT[:, c, 64 + g * N_CMP:64 + g * N_CMP + N_CMP],
                                              cmp_wv2[:, c, :], start=c == 0, stop=c == 1)
                close_bank(mm, "cmp_v")
                drained_by(pe, "cmp_kT", *[f"nqT{j}" for j in range(4)])
                for t in range(TT):
                    for odd in range(2):
                        bank = open_bank(f"cmpS{t}{odd}")
                        for i in range(NSA_HEADS // 2):
                            r, g = 64 * odd, i // 2
                            mm = nc.tensor.matmul(bank[:, i * N_CMP:i * N_CMP + N_CMP], nqT[r:r + 64, i, t * P:t * P + P],
                                                  cmp_kT[r:r + 64, g * N_CMP:g * N_CMP + N_CMP], start=True, stop=True)
                        close_bank(mm, f"cmpS{t}{odd}")
                drained_by(pe, *[f"y_aT{j}" for j in range(4)])
                token_major("branch_a0", "branch_a0", y_aT)
                for t in range(TT):
                    pe.wait_ge(sem("cmp_probs_ready"), t + 1)
                    bank = open_bank(f"cmpT{t}")
                    for g in range(NSA_KV):
                        mm = nc.tensor.transpose(bank[:, g * P:g * P + P],
                                                 cmp_p[:, t, 4 * g:4 * g + 4, :].rearrange("p h n -> p (h n)"), ident)
                    close_bank(mm, f"cmpT{t}")
                scores(blocks2[2])
                turn_probs(blocks2[0])
                drained_by(pe, "cmpT0", "cmpT1")
                pe.wait_ge(sem("cmp_v_ready"), 1)
                for t in range(TT):
                    for f in range(2):
                        bank = open_bank(f"cmpO{t}{f}")
                        for j in range(2):
                            mm = nc.tensor.matmul(bank[:, j * 256:j * 256 + 256], cmp_pT[:, t, 2 * f + j, :], cmp_v[:, 2 * f + j, :],
                                                  start=True, stop=True)
                        close_bank(mm, f"cmpO{t}{f}")
                token_major("branch_a1", "branch_a1", y_aT)
                for i in range(3, len(blocks2) + 3):
                    if i < len(blocks2):
                        scores(blocks2[i])
                    if i - 2 < len(blocks2):
                        turn_probs(blocks2[i - 2])
                    weigh_values(blocks2[i - 3])
                    if i == len(blocks2) + 1:
                        pe.wait_ge(sem("y_b_ready"), 1)
                        turn_half("y_bT", y_b, 0)

                def y_b_second():
                    pe.wait_ge(sem("y_b_ready"), 2)
                    turn_half("y_bT", y_b, 1)

                def merged(t):
                    pe.wait_ge(sem("merged_ready"), t + 1)
                    turn_half("mergedT", mix_a, t)

                def merged_first():
                    merged(0)

                half_turned("y_bT", 0)
                token_pair(["branch_b0", "branch_b1"], y_bT,
                           {(0, 1): y_b_second, (1, 0): lambda: half_turned("y_bT", 1), (1, 1): merged_first})
                half_turned("mergedT", 0)
                token_pair(["out2_0", "out2_1"], xT, {(0, 1): lambda: merged(1), (1, 0): lambda: half_turned("mergedT", 1),
                                                      (1, 1): lambda: normed_half("mlpT", 0, 9)})
                half_turned("mlpT", 0)
                feature_pair(["up0"], xT, lambda: normed_half("mlpT", 1, 10), lambda: half_turned("mlpT", 1))
                pe.wait_ge(sem("x_rest_ready"), 1)
                for c in range(1, 8):
                    split_feature_major(f"up{c}", f"up{c}", x_high, x_rest)
                pe.wait_ge(sem("p_landed"), 16)
                bank = open_bank("pT")
                for k in range(2):
                    for t in range(TT):
                        mm = nc.tensor.transpose(bank[:, k * T + t * P:k * T + t * P + P], p_tok[:, t, k * P:k * P + P], ident)
                close_bank(mm, "pT")
                for c in range(2):
                    tiles = [open_bank(f"down{c}{t}") for t in range(TT)]
                    for k4 in range(4):
                        if c == 0:
                            pe.wait_ge(sem("ff_ready"), 4 * k4 + 4)
                        for h in range(2):
                            pairs = part_pairs(f"down{c}{k4}", h, ff_high[k4], ff_rest[k4])
                            for t in range(TT):
                                for k in range(4):
                                    for n, (w, v) in enumerate(pairs):
                                        mm = nc.tensor.matmul(tiles[t], v[:, 4 * h + k, t * P:t * P + P], w[:, k, :],
                                                              start=k4 + h + k + n == 0, stop=k4 == 3 and h == 1 and k == 3 and n == 2)
                                if k4 == 3 and h == 1:
                                    close_bank(mm, f"down{c}{t}")
                            if h == 0:
                                half_used(mm, f"down{c}{k4}")
                        if k4 < 3:
                            mm.then_inc(sem("down_used"), 1)
                        unit_last_fill[f"down{c}{k4}"] = f"down{c}1" if k4 == 3 else 3 * c + k4 + 1
                drained_by(pe, "pT")
                w = use("ple")
                for c in range(2):
                    for t in range(TT):
                        bank = open_bank(f"ple{c}{t}")
                        for k in range(2):
                            mm = nc.tensor.matmul(bank, pT[:, k, t * P:t * P + P], w[:, k, c * 512:c * 512 + 512], start=k == 0, stop=k == 1)
                        close_bank(mm, f"ple{c}{t}")
                unit_last_fill["ple"] = "ple11"
                def x_half(t):
                    pe.wait_ge(sem("x_ready"), t + 1)
                    turn_half("pleT", x, t)

                x_half(0)
                half_turned("pleT", 0)
                token_pair(["ple_gate0", "ple_gate1"], xT, {(0, 1): lambda: x_half(1), (1, 0): lambda: half_turned("pleT", 1)})

            counts, roots = {}, []

            def counted(eng, ins, name, wait):
                counts[name] = counts.get(name, 0) + 1
                ins.then_inc(sem(name), 1)
                if wait:
                    eng.wait_ge(sem(name), counts[name])

            def drains(eng, ins, fill, wait):
                n = fills[fill]
                ins.then_inc(sem(f"bank_drained{n % BANKS}"), 1)
                if wait:
                    eng.wait_ge(sem(f"bank_drained{n % BANKS}"), n // BANKS + 1)

            @block.vector
            def _(dve):
                V = nc.vector

                def step(ins, name="dve_step", wait=True):
                    counted(dve, ins, name, wait)

                def drain(ins, fill, wait=False):
                    drains(dve, ins, fill, wait)

                def wide(ap, shape):
                    return ap.to_broadcast(shape)

                def inverse_root(v):
                    roots.append(v)
                    dve.wait_ge(sem("root_ready"), len(roots))
                    step(V.reciprocal(v, v))

                def inverse_rms(dst, sums, width):
                    step(V.tensor_scalar(dst, sums, 1.0 / width, EPS, ALU.mult, ALU.add), "variance_ready", wait=False)
                    inverse_root(dst)

                def normalize(src, dst, k, name):
                    sums, inv = stat(k, 2), stat(k + 2, 2)
                    for t in range(TT):
                        step(V.tensor_tensor_reduce(dst[:, t, :], src[:, t, :], src[:, t, :], 1.0, 0.0, ALU.mult, ALU.add,
                                                    sums[:, t:t + 1]))
                    inverse_rms(inv, sums, src.shape[2])
                    for t in range(TT):
                        step(V.tensor_scalar(dst[:, t, :], src[:, t, :], inv[:, t:t + 1], None, ALU.mult), name)

                def normalize_half(src, dst, k, t, name="x_normed"):
                    v = stat(k + t, 1)
                    step(V.tensor_tensor_reduce(dst[:, t, :], src[:, t, :], src[:, t, :], 1.0, 0.0, ALU.mult, ALU.add, v))
                    inverse_rms(v, v, src.shape[2])
                    step(V.tensor_scalar(dst[:, t, :], src[:, t, :], v, None, ALU.mult), name)

                def scaled_norm(src, dst, k, t, gain, junk):
                    v = stat(k + t, 1)
                    step(V.tensor_tensor_reduce(junk, src[:, t, :], src[:, t, :], 1.0, 0.0, ALU.mult, ALU.add, v))
                    inverse_rms(v, v, src.shape[2])
                    step(V.scalar_tensor_tensor(out=dst, in0=src[:, t, :], scalar=v, in1=gain, op0=ALU.mult, op1=ALU.mult))

                def half_turned(tag, dst, t, gain=None):
                    bank = filled_by(dve, f"{tag}{t}1")
                    o = dst[:, 4:8, t * P:t * P + P]
                    ins = V.tensor_copy(o, grid(bank, 4)) if gain is None else \
                        V.tensor_tensor(o, grid(bank, 4), wide(col(gain, 4, 4).unsqueeze(2), [P, 4, P]), ALU.mult)
                    drain(ins, f"{tag}{t}1")

                def turned(tag, dst, gain=None):
                    for j in (1, 3):
                        bank = filled_by(dve, f"{tag}{j}")
                        for k in (2 * j, 2 * j + 1):
                            src = bank[:, (k % 2) * T:(k % 2) * T + T]
                            ins = V.tensor_copy(dst[:, k, :], src) if gain is None else \
                                V.tensor_scalar(dst[:, k, :], src, col(gain, k), None, ALU.mult)
                        drain(ins, f"{tag}{j}")

                def softmax(blk):
                    nk = blk["nk"]
                    per = 512 // nk
                    top, _, _ = block_stats(blk)
                    for f in range(HEADS // per):
                        bank = filled_by(dve, f"{blk['name']}S{f}")
                        for j in range(per):
                            n = f * per + j
                            ins = V.tensor_tensor_reduce(blk["p"][:, n, :], bank[:, j * nk:j * nk + nk], const("causal")[:, T - nk:T], 1.0, -3.0 * BIG,
                                                         ALU.add, ALU.max, top[:, n:n + 1])
                        drain(ins, f"{blk['name']}S{f}", wait=f == HEADS // per - 1)
                    step(V.tensor_scalar(top, top, -blk["scale"], None, ALU.mult), "max_ready")

                def probs_turned(blk):
                    flat = blk["pt"]
                    for f in range(1, HEADS * blk["nk"] // P // 4, 2):
                        bank = filled_by(dve, f"{blk['name']}T{f}")
                        drain(V.tensor_copy(flat[:, 4 * f:4 * f + 4, :], grid(bank, 4)), f"{blk['name']}T{f}")

                def split_rest(stage, u, h):
                    if u < len(split_stages[stage]):
                        name = split_stages[stage][u]
                        dve.wait_ge(sem(f"{stage}_high_ready"), 2 * u + h + 1)
                        step(V.tensor_tensor(rest_half(name, h), split_half(name, h), w_high[stage][h].bitcast(F32), ALU.subtract),
                             f"{stage}_rest_ready", wait=False)

                def by_head(flat):
                    return flat.rearrange("p (i r e) -> p i r e", r=2, e=HEAD_DIM)

                def factors(inv):
                    return wide(inv.rearrange("p (r i) -> p i r", r=2).unsqueeze(3), [P, HEADS // 2, 2, HEAD_DIM])

                def inverse_sums(blk):
                    dve.wait_ge(sem("probs_ready"), blk["n"] + 1)
                    _, sums, inv = block_stats(blk)
                    step(V.reciprocal(inv, sums))

                for t in range(TT):
                    dve.wait_ge(sem(f"x_landed{t}"), 16)
                    normalize_half(x, normed, 4, t)
                dve.wait_ge(sem("params_landed"), 16)
                for t in range(TT):
                    half_turned("mixT", xT, t, "norm_mix_g")
                dve.wait_ge(sem("mixer_x_high_ready"), 1)
                step(V.tensor_tensor(mix_rest, xT, mix_high.bitcast(F32), ALU.subtract), "mixer_x_rest_ready", wait=False)
                dve.wait_ge(sem("mem_landed"), 16)
                normalize(mem_tok, mem_normed, 0, "mem_normed")
                for h in range(2):
                    split_rest("mixer", 0, h)
                step(V.memset(z[:, :, 0:TAPS - 1], 0.0))
                for f in range(2):
                    drained_by(dve, f"conv_g{f}")
                    bank = filled_by(dve, f"conv_a{f}")
                    for cb in (2 * f, 2 * f + 1):
                        ins = V.scalar_tensor_tensor(out=z[:, cb, TAPS - 1:ZW], in0=bank[:, (cb % 2) * T:(cb % 2) * T + T],
                                                     scalar=col("b_glu", cb), in1=glu[:, cb, :], op0=ALU.add, op1=ALU.mult)
                    drain(ins, f"conv_a{f}", wait=True)
                for cb in range(DVE_CONV):
                    step(V.tensor_scalar(conv[:, cb, :], z[:, cb, 0:T], tap(0, cb), col("b_dw", cb), ALU.mult, ALU.add), wait=False)

                def convolve(taps):
                    for w in taps:
                        for cb in range(DVE_CONV):
                            dve.wait_ge(sem("dve_step"), counts["dve_step"] - DVE_CONV + 1)
                            ins = V.scalar_tensor_tensor(out=conv[:, cb, :], in0=z[:, cb, w:w + T], scalar=tap(w, cb),
                                                         in1=conv[:, cb, :], op0=ALU.mult, op1=ALU.add)
                            step(ins, "conv_ready" if w == TAPS - 1 and cb == DVE_CONV - 1 else "dve_step", wait=False)

                convolve(range(1, 3))
                split_rest("mixer", 1, 0)
                convolve(range(3, 5))
                split_rest("mixer", 1, 1)
                for f in range(2):
                    bank = filled_by(dve, f"q{f}")
                    drain(V.tensor_copy(qT1[:, 2 * f:2 * f + 2, :], grid(bank, 2)), f"q{f}")
                convolve(range(5, 8))
                split_rest("mixer", 2, 0)
                turned("memT", memT, "mem_norm_g")
                split_rest("mixer", 2, 1)
                convolve(range(8, 10))
                dve.wait_ge(sem("forget_landed"), 32)
                bank = filled_by(dve, "forget")
                tmp = page(4, 0, 1024)[0:HEADS, :].rearrange("p (n t) -> p n t", n=4)
                drain(V.tensor_scalar(tmp[:, 0, :], bank[0:HEADS, 0:T], forget_b[:, 0:1], None, ALU.add), "forget", wait=True)
                step(V.tensor_scalar(tmp[:, 1, :], tmp[:, 0, :], -1.0, None, ALU.mult))
                step(V.tensor_tensor(tmp[:, 1, :], tmp[:, 1, :], tmp[:, 0, :], ALU.max), "forget_abs")
                step(V.tensor_scalar(tmp[:, 0, :], tmp[:, 0, :], 0.0, None, ALU.min))
                dve.wait_ge(sem("mem_x_high_ready"), 1)
                step(V.tensor_tensor(mem_rest, memT, mem_high.bitcast(F32), ALU.subtract), "mem_x_rest_ready", wait=False)
                convolve(range(10, 11))
                split_rest("mixer", 3, 0)
                convolve(range(11, 12))
                dve.wait_ge(sem("forget_log"), 1)
                step(V.tensor_tensor(log_f, tmp[:, 0, :], tmp[:, 2, :], ALU.subtract))
                dve.wait_ge(sem("consts_landed"), 16)
                step(V.tensor_tensor_scan(tmp[:, 3, :], const("ones")[0:HEADS, 0:T], log_f, 0.0, ALU.mult, ALU.add))
                step(V.tensor_scalar(key_bias, tmp[:, 3, :], -(HEAD_DIM ** 0.5), None, ALU.mult), "key_bias_ready")
                convolve(range(12, 14))
                split_rest("mixer", 3, 1)
                convolve(range(14, 18))
                split_rest("mixer", 4, 0)
                convolve(range(18, 20))
                for c in range(2):
                    for f in range(2):
                        bank = filled_by(dve, f"mem_k{c}{f}")
                        drain(V.tensor_copy(mem_k[:, 4 * c + 2 * f:4 * c + 2 * f + 2, :], grid(bank, 2)), f"mem_k{c}{f}")
                        n = 2 * c + f + 1
                        if n < 4:
                            split_rest("mixer", 4 + n // 2, n % 2)
                        convolve(range(20 + 3 * (2 * c + f), min(23 + 3 * (2 * c + f), TAPS)))
                softmax(blocks1[0])
                softmax(blocks1[1])
                split_rest("mixer", 6, 0)
                for blk in blocks1:
                    inverse_sums(blk)
                    probs_turned(blk)
                split_rest("mixer", 6, 1)

                def attn1_out(blk):
                    t = blk["t"]
                    _, _, inv = block_stats(blk)
                    bank = filled_by(dve, f"{blk['name']}O")
                    drain(V.tensor_tensor(by_head(attn1[:, t, :]), by_head(bank), factors(inv), ALU.mult), f"{blk['name']}O", wait=True)
                    junk = page(9, 0, 512)
                    sums, inv_rms = stat(8 + t, 1), stat(10 + t, 1)
                    step(V.tensor_tensor_reduce(junk, attn1[:, t, :], attn1[:, t, :], 1.0, 0.0, ALU.mult, ALU.add, sums))
                    inverse_rms(inv_rms, sums, D_ATTN)
                    step(V.tensor_scalar(attn1[:, t, :], attn1[:, t, :], inv_rms, None, ALU.mult), "attn1_normed")

                bank = filled_by(dve, "conv_mean")
                mean = page(9, 512, 256)
                drain(V.tensor_scalar(mean, bank[:, 0:T], 1.0 / D_CONV, None, ALU.mult), "conv_mean", wait=True)
                step(V.tensor_tensor(conv, conv, wide(mean.unsqueeze(1), [P, 4, T]), ALU.subtract))
                step(V.tensor_tensor(glu, conv, conv, ALU.mult), "conv_ready")
                attn1_out(blocks1[0])
                attn1_out(blocks1[1])
                bank = filled_by(dve, "conv_var")
                drain(V.tensor_scalar(mean, bank[:, 0:T], 1.0 / D_CONV, None, ALU.mult), "conv_var", wait=True)
                step(V.tensor_scalar(mean, mean, EPS, None, ALU.add), "variance_ready", wait=False)
                inverse_root(mean)
                step(V.tensor_tensor(conv, conv, wide(mean.unsqueeze(1), [P, 4, T]), ALU.mult), "conv_normed")
                for t in range(TT):
                    bank = filled_by(dve, f"attn1T{t}")
                    for k in range(4):
                        ins = V.tensor_scalar(catT[:, k, t * P:t * P + P], bank[:, k * P:k * P + P], col("attn_out_g", k), None, ALU.mult)
                    drain(ins, f"attn1T{t}")

                def add_to_x(tag, t):
                    for c in range(2):
                        bank = filled_by(dve, f"{tag}{c}{t}")
                        drain(V.tensor_tensor(x[:, t, c * 512:c * 512 + 512], x[:, t, c * 512:c * 512 + 512], bank, ALU.add),
                              f"{tag}{c}{t}", wait=True)

                for h in range(2):
                    split_rest("cross", 0, h)
                for t in range(TT):
                    add_to_x("out", t)
                    normalize_half(x, normed, 12, t)
                    half_turned("normT", xT, t, "norm_mem_g")
                dve.wait_ge(sem("cross_x_high_ready"), 1)
                step(V.tensor_tensor(cross_rest, xT, cross_high.bitcast(F32), ALU.subtract), "cross_x_rest_ready", wait=False)
                top2 = grid(stat(16, 8), TT)
                sum2, inv2 = grid(stat(24, 8), TT), grid(stat(32, 8), TT)
                for f in range(2):
                    bank = filled_by(dve, f"mem_q{f}1")
                    drain(V.tensor_copy(qT2[:, 4 * f + 2:4 * f + 4, :], grid(bank, 2)), f"mem_q{f}1")
                    for t in range(TT if f else 0):
                        bank = filled_by(dve, f"crossT{t}0")
                        drain(V.tensor_copy(prob2T[:, 0:2, :, t * P:t * P + P], bank.rearrange("p (h m q) -> p h m q", h=2, m=2)), f"crossT{t}0")
                    two = slice(2 * f, 2 * f + 2)
                    for t in range(TT):
                        bank = filled_by(dve, f"crossS{t}{f}")
                        step(V.tensor_reduce(top2[:, t, two], grid(bank, 2), AX.X, ALU.max))
                        step(V.tensor_scalar(top2[:, t, two], top2[:, t, two], -(MEM_DIM ** -0.5), None, ALU.mult), "cross_max_ready")
                    for t in range(TT):
                        drained_by(dve, f"crossS{t}{f}")
                        step(V.reciprocal(inv2[:, t, two], sum2[:, t, two]))
                        step(V.tensor_tensor(prob2[:, t, two, :], prob2[:, t, two, :], wide(inv2[:, t, two].unsqueeze(2), [P, 2, T]), ALU.mult),
                             "cross_probs_ready")
                for f in (1, 3):
                    bank = filled_by(dve, f"crossO{f}")
                    drain(V.tensor_copy(oT2[:, 2 * f:2 * f + 2, :], grid(bank, 2)), f"crossO{f}")
                chosen = grid(scratch_route[:, 0:64], TT)
                r = lambda k, n: scratch_route[:, 64 + k:64 + k + n]
                dve.wait_ge(sem("route_landed"), 16 * (GROUPS + 3))

                def first_largest(values, n, k, top):
                    hot, run = r(k, n), r(k + 32, n)
                    step(V.tensor_reduce(top, values, AX.X, ALU.max))
                    step(V.tensor_scalar(hot, values, top, None, ALU.is_equal))
                    step(V.tensor_tensor_scan(run, const("ones")[:, 0:n], hot, 0.0, ALU.mult, ALU.add))
                    step(V.scalar_tensor_tensor(out=hot, in0=run, scalar=1.0, in1=hot, op0=ALU.is_equal, op1=ALU.mult))
                    return hot

                picks = []
                for t in range(TT):
                    add_to_x("mem_o", t)
                    normalize_half(x, normed, 40, t)
                    half_turned("ffnT", xT, t, "norm_ffn_g")
                    bank = filled_by(dve, f"route{t}")
                    drain(V.tensor_tensor(logits[:, t, :], bank[:, 0:36], route_b[:, :], ALU.add), f"route{t}", wait=True)
                    base = 512 * t
                    tops = stat(44 + 8 * t, 8)
                    group = first_largest(logits[:, t, 0:4], 4, base, tops[:, 0:1])
                    step(V.tensor_scalar(tops[:, 1:2], tops[:, 0:1], -1.0, None, ALU.mult), "group_max_ready")
                    step(V.tensor_scalar(r(base + 64, 4), group, -1.0, BIG, ALU.add, ALU.mult))
                    masked = r(base + 96, 32)
                    step(V.tensor_tensor(grid(masked, 4), grid(logits[:, t, 4:36], 4), wide(r(base + 64, 4).unsqueeze(2), [P, 4, 8]), ALU.add))
                    one = first_largest(masked, 32, base + 128, tops[:, 2:3])
                    rest = r(base + 192, 32)
                    step(V.scalar_tensor_tensor(out=rest, in0=one, scalar=-3.0 * BIG, in1=masked, op0=ALU.mult, op1=ALU.add))
                    two = first_largest(rest, 32, base + 224, tops[:, 3:4])
                    step(V.tensor_tensor(chosen[:, t, :], one, two, ALU.add), "choice_ready" if t == 1 else "dve_step")
                    step(V.tensor_tensor(tops[:, 4:5], tops[:, 3:4], tops[:, 2:3], ALU.subtract), "second_ready")
                    picks.append((one, two))
                for t, (one, two) in enumerate(picks):
                    tops = stat(44 + 8 * t, 8)
                    dve.wait_ge(sem("route_exp"), 2 * t + 2)
                    step(V.scalar_tensor_tensor(out=tops[:, 6:7], in0=tops[:, 4:5], scalar=1.0, in1=tops[:, 5:6], op0=ALU.add, op1=ALU.mult))
                    step(V.reciprocal(tops[:, 6:7], tops[:, 6:7]))
                    step(V.scalar_tensor_tensor(out=gate[:, t, :], in0=two, scalar=tops[:, 4:5], in1=one, op0=ALU.mult, op1=ALU.add))
                    step(V.tensor_scalar(gate[:, t, :], gate[:, t, :], tops[:, 6:7], None, ALU.mult))
                bank = filled_by(dve, "rank")
                step(V.scalar_tensor_tensor(out=pos[:, :, :], in0=grid(bank[:, 0:64], TT), scalar=1.0, in1=chosen, op0=ALU.add, op1=ALU.mult))
                step(V.tensor_scalar(pos[:, :, :], pos[:, :, :], -1.0, None, ALU.add))
                drain(V.tensor_reduce(stat(60, 1), bank[:, 64:96], AX.X, ALU.max), "rank", wait=True)
                step(V.tensor_copy(busiest[:, :], stat(60, 1)), "busiest_ready")

                def experts(tag, first, n_pairs):
                    s = lambda name: sem(f"{tag}_{name}")

                    def pick(n, e, dst, gated_too):
                        expert = bass.ds(2 * ((n + first) % PAIRS) + e, 1)
                        slots = const("slots")[:, bass.ds(CAP * ((n + first) // PAIRS), CAP)]
                        for t in range(TT):
                            o = dst[:, t, e * CAP:e * CAP + CAP]
                            if gated_too:
                                ins = V.tensor_scalar(o, slots, pos[:, t, expert], gate[:, t, expert], ALU.is_equal, ALU.mult)
                            else:
                                ins = V.tensor_scalar(o, slots, pos[:, t, expert], None, ALU.is_equal)
                        return ins

                    def build_choose(n):
                        pick(n, 0, choose, False)
                        pick(n, 1, choose, False).then_inc(s("choose_ready"), 1)

                    def build_gated(n):
                        pick(n, 0, choose_gated, True)
                        pick(n, 1, choose_gated, True).then_inc(s("gated_choose_ready"), 1)

                    def drain_picked(n):
                        for f, b in ((0, 0), (1, 7)):
                            dve.wait_ge(s("picked_filled"), 2 * n + f + 1)
                            V.tensor_tensor(picked[:, 4 * f:4 * f + 4, :], grid(ps[:, b, :], 4),
                                            wide(col("norm_ffn_g", 4 * f, 4).unsqueeze(2), [P, 4, P]), ALU.mult).then_inc(s("picked_drained"), 1)

                    def drain_sums(n):
                        for t in range(TT):
                            for c in range(2):
                                dve.wait_ge(s("sum_filled"), 4 * n + 2 * t + c + 1)
                                V.tensor_tensor(x[:, t, c * 512:c * 512 + 512], x[:, t, c * 512:c * 512 + 512], ps[:, 5 + c, :],
                                                ALU.add).then_inc(s("sum_drained"), 1)

                    def gate_hidden(n):
                        dve.wait_ge(s("silu_ready"), n + 1)
                        dve.wait_ge(s("up_filled"), 2 * n + 2)
                        V.tensor_tensor(hidden, hidden, ps[:, 2, :], ALU.mult).then_inc(s("hidden_ready"), 1)

                    build_choose(0)
                    build_gated(0)
                    V.memset(spread, 0.0).then_inc(s("spread_ready"), 1)
                    for c in range(2):
                        V.memset(expert_out[:, c * 512:c * 512 + 512], 0.0).then_inc(s("out_ready"), 1)
                    drain_picked(0)
                    build_choose(1)
                    with dve.Fori(0, n_pairs) as i:
                        drain_sums(i)
                        gate_hidden(i)
                        dve.wait_ge(s("sum_drained"), 4 * i + 4)
                        drain_picked(i + 1)
                        build_choose(i + 2)
                        dve.wait_ge(s("spread_filled"), i + 1)
                        build_gated(i + 1)
                    drain_sums(n_pairs)
                    dve.wait_ge(s("sum_drained"), 4 * n_pairs + 4)

                experts("moe", 0, PAIRS)
                count = dve.value_load(busiest[0:1, 0:1], min_val=0, max_val=T)
                with dve.If(count > CAP):
                    experts("more", PAIRS, MORE)

                dve.wait_ge(sem("final_gain_landed"), 16)
                for t in range(TT):
                    scaled_norm(x, x[:, t, :], 40, t, gain_final, normed[:, t, :])
                    if t:
                        half_turned("mix2T", xT, 0, "norm_pre_mix_2")
                    normalize_half(x, normed, 44, t)
                half_turned("mix2T", xT, 1, "norm_pre_mix_2")
                e0, e1, lb, rest = stat(0, 8), stat(8, 8), stat(16, 8), stat(24, 8)
                l0, l1 = col("hg_lb_logits_2", 0, 8), col("hg_lb_logits_2", 8, 8)
                step(V.tensor_tensor(lb, l0, l1, ALU.max))
                step(V.tensor_tensor(e0, l0, lb, ALU.subtract))
                step(V.tensor_tensor(e1, l1, lb, ALU.subtract), "lb_ready")
                dve.wait_ge(sem("lb_exp"), 2)
                step(V.tensor_tensor(rest, e0, e1, ALU.add))
                step(V.reciprocal(rest, rest))
                step(V.tensor_tensor(lb, e0, rest, ALU.mult))
                step(V.tensor_scalar(rest, lb, -1.0, 1.0, ALU.mult, ALU.add))
                dve.wait_ge(sem("proj_x_high_ready"), 1)
                step(V.tensor_tensor(proj_rest, xT, proj_high.bitcast(F32), ALU.subtract), "proj_x_rest_ready", wait=False)
                for c in range(2):
                    for f in range(2):
                        at = (4 * c + 2 * f) * T
                        dve.wait_ge(sem("hq_sigmoid"), 2 * c + f + 1)
                        bank = filled_by(dve, f"hq{c}{f}")
                        drain(V.scalar_tensor_tensor(out=hq[:, at:at + 512], in0=bank, scalar=P ** -0.5, in1=hx[0][:, at:at + 512],
                                                     op0=ALU.mult, op1=ALU.mult), f"hq{c}{f}", wait=True)
                    for h in range(2):
                        split_rest("proj", c, h)
                for h in range(2):
                    split_rest("proj", 2, h)
                drained_by(dve, "hf00", "hf01", "hf10", "hf11")
                for h in range(HG_HEADS):
                    step(V.tensor_scalar(hb[:, h * T:h * T + T], hb[:, h * T:h * T + T], rest[:, h:h + 1], lb[:, h:h + 1], ALU.mult, ALU.add),
                         "forget2_ready", wait=False)
                dve.wait_ge(sem("forget2_ready"), HG_HEADS)
                step(V.tensor_scalar(hk, hb, -1.0, 1.0, ALU.mult, ALU.add), "level_ready")
                for h in range(2):
                    split_rest("proj", 3, h)
                dve.wait_ge(sem("log_forget"), 1)
                for h in range(HG_HEADS):
                    step(V.tensor_tensor_scan(hb[:, h * T:h * T + T], const("chunk_reset"), hx[0][:, h * T:h * T + T], 0.0, ALU.mult, ALU.add),
                         wait=h == HG_HEADS - 1)

                def level_drains(n):
                    if n and LEVELS[n - 1] == P:
                        for f in range(2):
                            bank = filled_by(dve, f"level{n}_{f}")
                            drain(V.tensor_copy(scores_cross[:, f * 512:f * 512 + 512], bank), f"level{n}_{f}")
                        return
                    mask = const("ident") if n == 0 else const(f"level{LEVELS[n - 1]}")
                    mask = mask.unsqueeze(1)
                    for f in range(4):
                        bank = filled_by(dve, f"level{n}_{f}")
                        dst = grid(scores_diag[:, f * 512:f * 512 + 512], 4)
                        if n == 0:
                            drain(V.tensor_tensor(dst, grid(bank, 4), wide(mask, [P, 4, P]), ALU.mult), f"level{n}_{f}", wait=True)
                        else:
                            drain(V.copy_predicated(dst, wide(mask.bitcast(U32), [P, 4, P]), grid(bank, 4)), f"level{n}_{f}", wait=True)

                half = ROPE_DIM // 2
                tmp = [CMP[:, 1408 + 128 * n:1536 + 128 * n] for n in range(4)]

                def rotate(src, dst, n):
                    for t in range(TT):
                        sv = src[:, t, :].rearrange("p (h e) -> p h e", e=NSA_DH)
                        dv = dst[:, t, :].rearrange("p (h e) -> p h e", e=NSA_DH)
                        cos = wide(grid(const("cos"), TT)[:, t, :].unsqueeze(1), [P, n, half])
                        sin = wide(grid(const("sin"), TT)[:, t, :].unsqueeze(1), [P, n, half])
                        a = [w[:, 0:n * half].rearrange("p (h e) -> p h e", e=half) for w in tmp]
                        x1, x2 = sv[:, :, 0:half], sv[:, :, half:ROPE_DIM]
                        step(V.tensor_tensor(a[0], x1, cos, ALU.mult), wait=False)
                        step(V.tensor_tensor(a[1], x2, sin, ALU.mult), wait=False)
                        step(V.tensor_tensor(a[2], x2, cos, ALU.mult), wait=False)
                        step(V.tensor_tensor(a[3], x1, sin, ALU.mult))
                        step(V.tensor_tensor(dv[:, :, 0:half], a[0], a[1], ALU.subtract), wait=False)
                        step(V.tensor_tensor(dv[:, :, half:ROPE_DIM], a[2], a[3], ALU.add), "rotated")

                for n, L in enumerate(LEVELS, 1):
                    halves = lambda flat: flat.rearrange("p (n r l) -> p n r l", r=2, l=L)
                    n_blocks = HG_HEADS * T // (2 * L)
                    b, e = halves(hb), halves(hx[n % 2])
                    mid = wide(b[:, :, 0, L - 1:L], [P, n_blocks, L])
                    if L >= CHUNK:
                        step(V.tensor_tensor(b[:, :, 1, :], b[:, :, 1, :], mid, ALU.add))
                    step(V.tensor_tensor(e[:, :, 0, :], mid, b[:, :, 0, :], ALU.subtract), wait=False)
                    step(V.tensor_tensor(e[:, :, 1, :], b[:, :, 1, :], mid, ALU.subtract), "exponent_ready")
                    level_drains(n - 1)
                    dve.wait_ge(sem("decay_ready"), n)
                    step(V.tensor_tensor(e[:, :, 0, :], e[:, :, 0, :], halves(hk)[:, :, 0, :], ALU.mult), wait=False)
                    step(V.tensor_tensor(e[:, :, 1, :], e[:, :, 1, :], halves(hq)[:, :, 1, :], ALU.mult), "level_ready")
                    if n == 4:
                        dve.wait_ge(sem("gnorm_landed"), 16)
                        drained_by(dve, *[f"hg{c}{t}" for c in range(2) for t in range(TT)])
                        for t in range(TT):
                            g = grid(hg[:, t, :], HG_HEADS)
                            step(V.tensor_tensor(g, g, wide(gnorm.unsqueeze(1), [P, HG_HEADS, P]), ALU.mult), wait=False)
                    for h in range(2):
                        split_rest("proj", 3 + n, h)
                    if n == 7:
                        drained_by(dve, *[f"nq{c}{t}" for c in range(2) for t in range(TT)])
                        rotate(nq, nq_rot, NSA_HEADS)
                level_drains(len(LEVELS))
                for h in range(2):
                    split_rest("proj", 12, h)
                drained_by(dve, *[f"kv{c}{t}" for c in range(3) for t in range(TT)])
                for k_rot in (nkv[:, :, 512:768], nkv[:, :, 1024:1280]):
                    rotate(k_rot, k_rot, NSA_KV)
                step(V.memset(cmp_hid, 0.0), "cmp_hid_cleared")
                for u in (13, 14):
                    for h in range(2):
                        split_rest("proj", u, h)
                filled_by(dve, "rec11")
                for t in range(TT):
                    for f in range(2):
                        bank = filled_by(dve, f"rec{t}{f}")
                        drain(V.tensor_copy(y_a[:, t, f * 512:f * 512 + 512], bank), f"rec{t}{f}", wait=True)
                def gate_recurrence(t):
                    o = grid(y_a[:, t, :], HG_HEADS)
                    sq = grid(page(6, 1024, 1024), HG_HEADS)
                    sums = stat(0 + 16 * t, 8)
                    step(V.tensor_tensor(sq, o, o, ALU.mult))
                    step(V.tensor_reduce(sums, sq, AX.X, ALU.add))
                    inverse_rms(sums, sums, P)
                    step(V.tensor_tensor(o, o, wide(sums.unsqueeze(2), [P, HG_HEADS, P]), ALU.mult))
                    step(V.tensor_tensor(y_a[:, t, :], y_a[:, t, :], hg[:, t, :], ALU.mult), "y_a_ready" if t else "dve_step")

                gate_recurrence(0)
                for kv, key in enumerate("kv"):
                    for f in range(2):
                        bank = filled_by(dve, f"{key}cT{f}")
                        tokens = bank.rearrange("p (g n j u) -> p g n j u", g=2, j=8, u=2)
                        for half_ in range(2):
                            dst = windows[:, kv, half_, :, :].rearrange("p (g n) j -> p g n j", g=4)
                            for u in range(2):
                                h = slice(64 * u, 64 * u + 64)
                                pe_ = col(f"cmp_pe_{key}_2", 8 * half_, 8)[h].unsqueeze(1).unsqueeze(1)
                                ins = V.tensor_tensor(dst[h, 2 * f:2 * f + 2], tokens[h, :, half_:half_ + N_CMP, :, u],
                                                      wide(pe_, [64, 2, N_CMP, 8]), ALU.add)
                        drain(ins, f"{key}cT{f}")
                gate_recurrence(1)
                softmax(blocks2[0])
                softmax(blocks2[1])
                turned("y_aT", y_aT)
                bank = filled_by(dve, "cmp_kT")
                drain(V.tensor_copy(cmp_kT, bank[:, 0:4 * N_CMP]), "cmp_kT")
                filled_by(dve, "nq_rotT3")
                step(V.memset(page(13, 1024, 1024), 0.0))
                bank = filled_by(dve, "cmp_v")
                for h in range(4):
                    ins = V.tensor_copy(cmp_v[32 * h:32 * h + N_CMP, :, h * 64:h * 64 + 64], grid(bank[0:N_CMP, 0:256], 4))
                    if h < 3:
                        step(ins)
                    else:
                        drain(ins, "cmp_v", wait=True)
                step(V.memset(page(9, 0, 1024), 0.0), "cmp_v_ready")

                def gate_branch_a(c):
                    dve.wait_ge(sem("mix_gates_ready"), 2)
                    for t in range(TT):
                        bank = filled_by(dve, f"branch_a{c}{t}")
                        m = mix_a[:, t, c * 512:c * 512 + 512]
                        drain(V.tensor_tensor(m, m, bank, ALU.mult), f"branch_a{c}{t}")

                seen, bias = grid(const("cmp_seen"), TT), grid(const("cmp_bias"), TT)
                tops = [stat(0, 16), stat(16, 16)]
                for t in range(TT):
                    live = cmp_p[:, t, :, 0:N_CMP]
                    for odd in range(2):
                        bank = filled_by(dve, f"cmpS{t}{odd}")
                        drain(V.tensor_tensor(live[:, odd:NSA_HEADS:2, :], grid(bank[:, 0:NSA_HEADS // 2 * N_CMP], NSA_HEADS // 2),
                                              wide(bias[:, t, :].unsqueeze(1), [P, NSA_HEADS // 2, N_CMP]), ALU.add), f"cmpS{t}{odd}", wait=True)
                    step(V.tensor_reduce(tops[t], live, AX.X, ALU.max))
                    step(V.tensor_tensor(live, live, wide(tops[t].unsqueeze(2), [P, NSA_HEADS, N_CMP]), ALU.subtract), "cmp_shifted")
                for t in range(TT):
                    live = cmp_p[:, t, :, 0:N_CMP]
                    dve.wait_ge(sem("cmp_exp_ready"), t + 1)
                    step(V.tensor_reduce(tops[t], live, AX.X, ALU.add))
                    step(V.reciprocal(tops[t], tops[t]))
                    step(V.tensor_tensor(live, live, wide(tops[t].unsqueeze(2), [P, NSA_HEADS, N_CMP]), ALU.mult))
                    step(V.tensor_tensor(live, live, wide(seen[:, t, :].unsqueeze(1), [P, NSA_HEADS, N_CMP]), ALU.mult), "cmp_probs_ready")
                gate_branch_a(0)
                softmax(blocks2[2])
                inverse_sums(blocks2[0])
                probs_turned(blocks2[0])
                dve.wait_ge(sem("sel_gates_ready"), 1)
                for t in range(TT):
                    for f in range(2):
                        bank = filled_by(dve, f"cmpO{t}{f}")
                        g = sel_gates[:, t, 8 * f:8 * f + 8].unsqueeze(2)
                        drain(V.tensor_tensor(grid(y_b[:, t, f * 512:f * 512 + 512], HEADS), grid(bank, HEADS), wide(g, [P, HEADS, 64]), ALU.mult),
                              f"cmpO{t}{f}", wait=True)

                def nsa_out(blk):
                    t, half_, branch = blk["t"], blk["half"], blk["branch"]
                    _, _, inv = block_stats(blk)
                    at = 16 * (branch + 1) + 8 * half_
                    in_order = inv.rearrange("p (r i) -> p r i", r=2)
                    step(V.tensor_tensor(in_order, in_order, sel_gates[:, t, at:at + 8].rearrange("p (i r) -> p r i", r=2), ALU.mult))
                    bank = filled_by(dve, f"{blk['name']}O")
                    tmp_ = page(9, 1024, 512)
                    drain(V.tensor_tensor(by_head(tmp_), by_head(bank), factors(inv), ALU.mult), f"{blk['name']}O", wait=True)
                    y = y_b[:, t, half_ * 512:half_ * 512 + 512]
                    step(V.tensor_tensor(y, y, tmp_, ALU.add), "y_b_ready" if branch and half_ else "dve_step")

                gate_branch_a(1)
                for i in range(3, len(blocks2) + 3):
                    if i < len(blocks2):
                        softmax(blocks2[i])
                    if i - 2 < len(blocks2):
                        inverse_sums(blocks2[i - 2])
                        probs_turned(blocks2[i - 2])
                    nsa_out(blocks2[i - 3])
                def merge(t):
                    for c in range(2):
                        bank = filled_by(dve, f"branch_b{c}{t}")
                        cut = slice(c * 512, c * 512 + 512)
                        drain(V.tensor_tensor(mix_b[:, t, cut], mix_b[:, t, cut], bank, ALU.mult), f"branch_b{c}{t}", wait=True)
                        step(V.tensor_tensor(mix_a[:, t, cut], mix_a[:, t, cut], mix_b[:, t, cut], ALU.add),
                             "merged_ready" if c else "dve_step")

                def add_normed(src, k, t, gain, done="dve_step"):
                    scaled_norm(src, normed[:, t, :], k, t, gain, normed[:, t, :])
                    step(V.tensor_tensor(x[:, t, :], x[:, t, :], normed[:, t, :], ALU.add), done)

                for t in range(TT):
                    half_turned("y_bT", y_bT, t)
                merge(0)
                half_turned("mergedT", xT, 0)
                merge(1)
                half_turned("mergedT", xT, 1)
                dve.wait_ge(sem("gains_landed"), 48)
                for t in range(TT):
                    drained_by(dve, f"out2_0{t}", f"out2_1{t}")
                    add_normed(mlp_out, 0, t, gain_mix)
                    normalize_half(x, normed, 4, t)
                    half_turned("mlpT", xT, t, "norm_pre_mlp_2")
                dve.wait_ge(sem("x_high_ready"), 1)
                step(V.tensor_tensor(x_rest, xT, x_high.bitcast(F32), ALU.subtract), "x_rest_ready")
                for f in range(2):
                    split_rest("mlp", 0, f)
                for c in range(8):
                    blocks = [ffT[c // 2][:, 4 * (c % 2) + 2 * f:4 * (c % 2) + 2 * f + 2, :] for f in range(2)]
                    highs, rests = [[part[c // 2][:, 4 * (c % 2) + 2 * f:4 * (c % 2) + 2 * f + 2, :] for f in range(2)]
                                    for part in (ff_high, ff_rest)]
                    for f in range(2):
                        if c:
                            split_rest("mlp", c, f)
                        drained_by(dve, f"up{c}{f}")
                        step(V.tensor_tensor(blocks[f], blocks[f], blocks[f], ALU.mult), "ff_squared", wait=False)
                    for f in range(2):
                        dve.wait_ge(sem("ff_high_ready"), 2 * c + f + 1)
                        step(V.tensor_tensor(rests[f], blocks[f], highs[f].bitcast(F32), ALU.subtract), "ff_ready", wait=False)
                for u in range(8, len(split_stages["mlp"])):
                    for h in range(2):
                        split_rest("mlp", u, h)
                bank = filled_by(dve, "pT")
                drain(V.tensor_copy(pT, grid(bank, 2)), "pT")
                for t in range(TT):
                    drained_by(dve, f"down0{t}", f"down1{t}")
                    add_normed(mlp_out, 8, t, gain_mlp, "x_ready")
                for t in range(TT):
                    half_turned("pleT", xT, t)
                for t in range(TT):
                    for c in range(2):
                        drained_by(dve, f"ple{c}{t}", f"ple_gate{c}{t}")
                        e = ple[:, t, c * 512:c * 512 + 512]
                        step(V.tensor_tensor(e, e, ple_gate[:, t, c * 512:c * 512 + 512], ALU.mult))
                    add_normed(ple, 12, t, gain_ple, "result_ready")

            @block.scalar
            def _(act):
                S = nc.scalar

                def step(ins, name="act_step", wait=True):
                    counted(act, ins, name, wait)

                def drain(ins, fill, wait=False):
                    drains(act, ins, fill, wait)

                def half_turned(tag, dst, t, gain=None):
                    bank = filled_by(act, f"{tag}{t}0")
                    if gain is None:
                        ins = S.copy(dst[:, 0:4, t * P:t * P + P], grid(bank, 4))
                    else:
                        for k in range(4):
                            ins = S.activation(dst[:, k, t * P:t * P + P], bank[:, k * P:k * P + P], ACT.Copy, scale=col(gain, k))
                    drain(ins, f"{tag}{t}0")

                def turned(tag, dst, gain=None):
                    for j in (0, 2):
                        bank = filled_by(act, f"{tag}{j}")
                        for k in (2 * j, 2 * j + 1):
                            src = bank[:, (k % 2) * T:(k % 2) * T + T]
                            ins = S.copy(dst[:, k, :], src) if gain is None else \
                                S.activation(dst[:, k, :], src, ACT.Copy, scale=col(gain, k))
                        drain(ins, f"{tag}{j}")

                def root(times=1):
                    for _ in range(times):
                        n = counts.get("root_ready", 0)
                        act.wait_ge(sem("variance_ready"), n + 1)
                        step(S.activation(roots[n], roots[n], ACT.Sqrt), "root_ready", wait=False)

                def exponentials(blk):
                    act.wait_ge(sem("max_ready"), blk["n"] + 1)
                    top, sums, _ = block_stats(blk)
                    for h in range(HEADS):
                        ins = S.activation(blk["p"][:, h, :], blk["p"][:, h, :], ACT.Exp, bias=top[:, h:h + 1], scale=blk["scale"],
                                           accum_out=sums[:, h:h + 1])
                    step(ins, "probs_ready")

                def probs_turned(blk):
                    for f in range(0, HEADS * blk["nk"] // P // 4, 2):
                        bank = filled_by(act, f"{blk['name']}T{f}")
                        drain(S.copy(blk["pt"][:, 4 * f:4 * f + 4, :], grid(bank, 4)), f"{blk['name']}T{f}")

                def split_high(stage, u, h):
                    if u == len(split_stages[stage]):
                        return
                    name = split_stages[stage][u]
                    slot = unit_at[name][1]
                    if by_halves(name):
                        act.wait_ge(sem(f"half_landed{2 * slot + h}"), 16 * (u // 2 + 1))
                    else:
                        act.wait_ge(sem(f"weights_landed{slot}"), landed_value[name])
                    if u and h == 0:
                        act.wait_ge(sem(f"{stage}_half_used"), u)
                    else:
                        last = split_stages[stage][u - 1] if u else last_in_place[stage][h]
                        if last:
                            done = unit_last_fill[last]
                            if isinstance(done, int):
                                act.wait_ge(sem("down_used"), done)
                            else:
                                filled_by(act, done)
                    step(S.copy(w_high[stage][h], split_half(name, h)), f"{stage}_high_ready", wait=False)

                def copy_out(fill, dst, func=ACT.Copy):
                    bank = filled_by(act, fill)
                    drain(S.activation(dst, bank, func), fill)

                root(2)
                act.wait_ge(sem("params_landed"), 16)
                for t in range(TT):
                    half_turned("mixT", xT, t, "norm_mix_g")
                drained_by(act, *[f"mixT{t}{f}" for t in range(TT) for f in range(2)])
                step(S.copy(mix_high, xT), "mixer_x_high_ready", wait=False)
                root()
                for h in range(2):
                    split_high("mixer", 0, h)
                for f in range(2):
                    bank = filled_by(act, f"conv_g{f}")
                    for cb in (2 * f, 2 * f + 1):
                        ins = S.activation(glu[:, cb, :], bank[:, (cb % 2) * T:(cb % 2) * T + T], ACT.Sigmoid, bias=col("b_glu", 4 + cb))
                    drain(ins, f"conv_g{f}")
                for h in range(2):
                    split_high("mixer", 1, h)
                for f in range(2):
                    split_high("mixer", 2, f)
                    bank = filled_by(act, f"k{f}")
                    drain(S.copy(kT1[:, 2 * f:2 * f + 2, :], grid(bank, 2)), f"k{f}")
                turned("memT", memT, "mem_norm_g")
                drained_by(act, *[f"memT{j}" for j in range(4)])
                step(S.copy(mem_high, memT), "mem_x_high_ready", wait=False)
                tmp = page(4, 0, 1024)[0:HEADS, :].rearrange("p (n t) -> p n t", n=4)
                act.wait_ge(sem("forget_abs"), 1)
                step(S.activation(tmp[:, 2, :], tmp[:, 1, :], ACT.Exp, scale=-1.0))
                step(S.activation(tmp[:, 2, :], tmp[:, 2, :], ACT.Ln, bias=1.0), "forget_log")
                for t in range(TT):
                    split_high("mixer", 3, t)
                    copy_out(f"v{t}", v1[:, t, :])
                for u in (4, 5):
                    for h in range(2):
                        split_high("mixer", u, h)
                exponentials(blocks1[0])
                exponentials(blocks1[1])
                split_high("mixer", 6, 0)
                for t in range(TT):
                    copy_out(f"mem_v0{t}", mem_v[:, t, 0:512])
                probs_turned(blocks1[0])
                probs_turned(blocks1[1])
                split_high("mixer", 6, 1)
                root(3)
                act.wait_ge(sem("conv_normed"), 1)
                for cb in range(4):
                    step(S.activation(catT[:, 4 + cb, :], conv[:, cb, :], ACT.Silu, bias=col("conv_ln_b", cb), scale=col("conv_ln_g", cb)),
                         "conv_done", wait=False)
                for t in range(TT):
                    copy_out(f"mem_v1{t}", mem_v[:, t, 512:1024])
                for h in range(2):
                    split_high("cross", 0, h)
                for t in range(TT):
                    root()
                    half_turned("normT", xT, t, "norm_mem_g")
                drained_by(act, *[f"normT{t}{f}" for t in range(TT) for f in range(2)])
                step(S.copy(cross_high, xT), "cross_x_high_ready", wait=False)
                top2, sum2 = grid(stat(16, 8), TT), grid(stat(24, 8), TT)
                for f in range(2):
                    bank = filled_by(act, f"mem_q{f}0")
                    drain(S.copy(qT2[:, 4 * f:4 * f + 2, :], grid(bank, 2)), f"mem_q{f}0")
                    for t in range(TT):
                        act.wait_ge(sem("cross_max_ready"), 2 * f + t + 1)
                        bank = filled_by(act, f"crossS{t}{f}")
                        for j in range(2):
                            h = 2 * f + j
                            ins = S.activation(prob2[:, t, h, :], bank[:, j * T:j * T + T], ACT.Exp, bias=top2[:, t, h:h + 1],
                                               scale=MEM_DIM ** -0.5, accum_out=sum2[:, t, h:h + 1])
                        drain(ins, f"crossS{t}{f}")
                for f in (0, 2):
                    if f:
                        for t in range(TT):
                            bank = filled_by(act, f"crossT{t}1")
                            drain(S.copy(prob2T[:, 2:4, :, t * P:t * P + P], bank.rearrange("p (h m q) -> p h m q", h=2, m=2)), f"crossT{t}1")
                    bank = filled_by(act, f"crossO{f}")
                    drain(S.copy(oT2[:, 2 * f:2 * f + 2, :], grid(bank, 2)), f"crossO{f}")
                for t in range(TT):
                    root()
                    half_turned("ffnT", xT, t, "norm_ffn_g")
                for t in range(TT):
                    tops = stat(44 + 8 * t, 8)
                    act.wait_ge(sem("group_max_ready"), t + 1)
                    step(S.activation(stat(504, 4), logits[:, t, 0:4], ACT.Exp, bias=tops[:, 1:2], accum_out=tops[:, 5:6]), "route_exp")
                    act.wait_ge(sem("second_ready"), t + 1)
                    step(S.activation(tops[:, 4:5], tops[:, 4:5], ACT.Exp), "route_exp")

                def experts(tag, n_pairs):
                    s = lambda name: sem(f"{tag}_{name}")

                    act.wait_ge(s("out_ready"), 2)
                    with act.Fori(0, n_pairs) as i:
                        act.wait_ge(s("gate_filled"), 2 * i + 2)
                        S.activation(hidden, ps[:, 1, :], ACT.Silu).then_inc(s("silu_ready"), 1)
                        act.wait_ge(s("hidden_turned"), i + 1)
                        S.copy(hiddenT, grid(ps[:, 1, :], 4)).then_inc(s("hiddenT_ready"), 1)
                        act.wait_ge(s("spread_filled"), i + 1)
                        S.copy(spread, ps[:, 5, 0:T]).then_inc(s("spread_ready"), 1)
                        act.wait_ge(s("down_filled"), 2 * i + 2)
                        for c in range(2):
                            S.copy(expert_out[:, c * 512:c * 512 + 512], ps[:, 3 + c, :]).then_inc(s("out_ready"), 1)

                experts("moe", PAIRS)
                act.wait_ge(sem("busiest_ready"), 1)
                count = act.value_load(busiest[0:1, 0:1], min_val=0, max_val=T)
                with act.If(count > CAP):
                    experts("more", MORE)

                for t in range(TT):
                    root()
                    if t:
                        half_turned("mix2T", xT, 0, "norm_pre_mix_2")
                    root()
                half_turned("mix2T", xT, 1, "norm_pre_mix_2")
                e0, e1 = stat(0, 8), stat(8, 8)
                act.wait_ge(sem("lb_ready"), 1)
                step(S.activation(e0, e0, ACT.Exp), "lb_exp", wait=False)
                step(S.activation(e1, e1, ACT.Exp), "lb_exp")
                drained_by(act, *[f"mix2T{t}{f}" for t in range(TT) for f in range(2)])
                step(S.copy(proj_high, xT), "proj_x_high_ready", wait=False)
                for c in range(2):
                    for f in range(2):
                        at = (4 * c + 2 * f) * T
                        bank = filled_by(act, f"hq{c}{f}")
                        step(S.activation(hx[0][:, at:at + 512], bank, ACT.Sigmoid), "hq_sigmoid", wait=False)
                    if c == 0:
                        for h in range(2):
                            split_high("proj", 0, h)

                def projection(u):
                    name = split_stages["proj"][u]
                    c = int(name[2])
                    for i in range(2):
                        split_high("proj", u + 1, i)
                        cut = slice(c * 512, c * 512 + 512)
                        if name[:2] == "hf":
                            at = (4 * c + 2 * i) * T
                            copy_out(f"{name}{i}", hb[:, at:at + 512], ACT.Sigmoid)
                        elif name[:2] == "hg":
                            copy_out(f"{name}{i}", hg[:, i, cut], ACT.Silu)
                        elif name[:2] == "nq":
                            bank = filled_by(act, f"{name}{i}")
                            S.activation(nq[:, i, cut], bank, ACT.Copy, scale=NSA_DH ** -0.5)
                            drain(S.activation(nq_rot[:, i, cut], bank, ACT.Copy, scale=NSA_DH ** -0.5), f"{name}{i}")
                        else:
                            copy_out(f"{name}{i}", {"hi": hv, "kv": nkv, "ga": mix_a, "gb": mix_b}[name[:2]][:, i, cut])

                projection(0)
                projection(1)
                act.wait_ge(sem("forget2_ready"), HG_HEADS)
                drained_by(act, "hq00", "hq01", "hq10", "hq11")
                step(S.activation(hx[0], hb, ACT.Ln), "log_forget")
                projection(2)
                for n in range(1, len(LEVELS) + 1):
                    act.wait_ge(sem("exponent_ready"), n)
                    step(S.activation(hx[n % 2], hx[n % 2], ACT.Exp), "decay_ready", wait=False)
                    projection(2 + n)
                    if n == 6:
                        bank = filled_by(act, "sel_gates")
                        drain(S.copy(sel_gates, grid(bank[:, 0:96], TT)), "sel_gates", wait=True)
                for u in (11, 12, 13):
                    projection(u)
                root()
                projection(14)
                for key, dst, n in (("nqT", nqT, 4), ("nq_rotT", nq_rotT, 4), ("ksT", ksT, 2), ("kwT", kwT, 2)):
                    for f in range(n):
                        bank = filled_by(act, f"{key}{f}")
                        drain(S.copy(dst[:, 2 * f:2 * f + 2, :], grid(bank, 2)), f"{key}{f}")
                root()
                act.wait_ge(sem("cmp_hid_cleared"), 1)
                bank = filled_by(act, "cmp_hid")
                for r in (0, 64):
                    ins = S.activation(cmp_hid[r:r + 4 * N_CMP, :], bank[r:r + 4 * N_CMP, 0:CMP_HIDDEN], ACT.Gelu_apprx_tanh)
                drain(ins, "cmp_hid")
                bank = filled_by(act, "cmp_hidT")
                drain(S.copy(cmp_hidT, grid(bank[:, 0:2 * P], 2)), "cmp_hidT")
                turned("y_aT", y_aT)
                exponentials(blocks2[0])
                exponentials(blocks2[1])
                drained_by(act, *[f"g{b}{c}{t}" for b in "ab" for c in range(2) for t in range(TT)])
                step(S.activation(sel_gates, sel_gates, ACT.Sigmoid), "sel_gates_ready", wait=False)
                step(S.activation(page(16), page(16), ACT.Sigmoid), "mix_gates_ready", wait=False)
                step(S.activation(page(10), page(10), ACT.Sigmoid), "mix_gates_ready", wait=False)
                for t in range(TT):
                    act.wait_ge(sem("cmp_shifted"), t + 1)
                    live = cmp_p[:, t, :, 0:N_CMP]
                    step(S.activation(live, live, ACT.Exp), "cmp_exp_ready", wait=False)
                for t in range(TT):
                    bank = filled_by(act, f"cmpT{t}")
                    drain(S.copy(cmp_pT[:, t, :, :], grid(bank, NSA_KV)), f"cmpT{t}")
                for i in range(2, len(blocks2) + 2):
                    probs_turned(blocks2[i - 2])
                    if i < len(blocks2):
                        exponentials(blocks2[i])
                for t in range(TT):
                    half_turned("y_bT", y_bT, t)
                half_turned("mergedT", xT, 0)

                def residual(t):
                    for c in range(2):
                        copy_out(f"out2_{c}{t}", mlp_out[:, t, c * 512:c * 512 + 512])
                        if t == 0 and c == 0:
                            half_turned("mergedT", xT, 1)
                    root(2)
                    half_turned("mlpT", xT, t, "norm_pre_mlp_2")

                residual(0)
                residual(1)
                drained_by(act, "mlpT00", "mlpT01", "mlpT10", "mlpT11")
                step(S.copy(x_high, xT), "x_high_ready", wait=False)
                split_high("mlp", 0, 0)
                act.wait_ge(sem("x_rest_ready"), 1)
                split_high("mlp", 0, 1)
                for c in range(8):
                    blocks = [slice(4 * (c % 2) + 2 * f, 4 * (c % 2) + 2 * f + 2) for f in range(2)]
                    for f in range(2):
                        if c:
                            split_high("mlp", c, f)
                        bank = filled_by(act, f"up{c}{f}")
                        drain(S.activation(ffT[c // 2][:, blocks[f], :], grid(bank, 2), ACT.Relu), f"up{c}{f}")
                    for f in range(2):
                        act.wait_ge(sem("ff_squared"), 2 * c + f + 1)
                        step(S.copy(ff_high[c // 2][:, blocks[f], :], ffT[c // 2][:, blocks[f], :]), "ff_high_ready", wait=False)
                for u in range(8, len(split_stages["mlp"])):
                    for h in range(2):
                        split_high("mlp", u, h)
                        if u == 12 and h == 0:
                            copy_out("down00", mlp_out[:, 0, 0:512])
                            copy_out("down01", mlp_out[:, 1, 0:512])
                for t in range(TT):
                    copy_out(f"down1{t}", mlp_out[:, t, 512:1024])
                    root()
                for c in range(2):
                    for t in range(TT):
                        copy_out(f"ple{c}{t}", ple[:, t, c * 512:c * 512 + 512])
                for t in range(TT):
                    half_turned("pleT", xT, t)
                for t in range(TT):
                    for c in range(2):
                        copy_out(f"ple_gate{c}{t}", ple_gate[:, t, c * 512:c * 512 + 512], ACT.Sigmoid)
                    root()
                assert counts["root_ready"] == len(roots)

            @block.gpsimd
            def _(pool):
                with nc.allow_non_contiguous_dma("small weights, read once"):
                    f0 = 3 * D_ATTN
                    pool.dma_start(forget_w[:, :, :], rows(d["w_in"][0], KT)[:, :, f0:f0 + HEADS]).then_inc(sem("forget_landed"), 16)
                    pool.dma_start(forget_b[:, :], d["b_forget"].rearrange("l h -> h l")).then_inc(sem("forget_landed"), 16)
                    pool.dma_start(route_w[:, :, 0:GROUPS], rows(d["w_route_group"][0], KT)).then_inc(sem("route_landed"), 16)
                    for g in range(GROUPS):
                        pool.dma_start(route_w[:, :, 4 + 8 * g:12 + 8 * g], rows(d["w_route_expert"][0, g], KT)).then_inc(sem("route_landed"), 16)
                    pool.dma_start(route_b[:, 0:4], d["b_route_group"][0].partition_broadcast(P)).then_inc(sem("route_landed"), 16)
                    pool.dma_start(route_b[:, 4:36], d["b_route_expert"][0].rearrange("g e -> (g e)").partition_broadcast(P)).then_inc(sem("route_landed"), 16)
                for f in range(2):
                    drained_by(pool, f"conv_a{f}")
                others = range(DVE_CONV, 4)
                for cb in others:
                    nc.gpsimd.tensor_scalar(conv[:, cb, :], z[:, cb, 0:T], tap(0, cb), col("b_dw", cb), ALU.mult, ALU.add).then_inc(sem("pool_added"), 1)
                for w in range(1, TAPS):
                    for n, cb in enumerate(others):
                        nc.gpsimd.tensor_scalar(glu[:, cb, :], z[:, cb, w:w + T], tap(w, cb), None, ALU.mult).then_inc(sem("pool_scaled"), 1)
                    for n, cb in enumerate(others):
                        pool.wait_ge(sem("pool_scaled"), len(others) * (w - 1) + n + 1)
                        pool.wait_ge(sem("pool_added"), len(others) * (w - 1) + n + 1)
                        ins = nc.gpsimd.tensor_tensor(conv[:, cb, :], conv[:, cb, :], glu[:, cb, :], ALU.add)
                        ins.then_inc(sem("conv_pool_ready" if w == TAPS - 1 and cb == 3 else "pool_added"), 1)
                    if w < TAPS - 1:
                        pool.wait_ge(sem("pool_added"), len(others) * (w + 1))
                filled_by(pool, "route1")
                pool.dma_start(gain_final, d["final_g"].partition_broadcast(P)).then_inc(sem("final_gain_landed"), 16)
                filled_by(pool, "hq00")
                pool.dma_start(gnorm, d["hg_gnorm_2"][0].partition_broadcast(P)).then_inc(sem("gnorm_landed"), 16)
                pool.dma_start(w_gates, rows(d["w_in_2"][0], KT)[:, :, 6656:6704]).then_inc(sem("gates_landed"), 16)
                with nc.allow_non_contiguous_dma("small weights, read once"):
                    for u in range(2):
                        pool.dma_start(cmp_wk2[:, :, u, :], rows(d["cmp_wk2_2"][0], 2)).then_inc(sem("cmp_w2_landed"), 16)
                    pool.dma_start(cmp_wv2, rows(d["cmp_wv2_2"][0], 2)).then_inc(sem("cmp_w2_landed"), 16)
                filled_by(pool, "y_bT10")
                for dst, name in ((gain_mix, "norm_post_mix_2"), (gain_mlp, "norm_post_mlp_2"), (gain_ple, "norm_ple_2")):
                    pool.dma_start(dst, d[name][0].partition_broadcast(P)).then_inc(sem("gains_landed"), 16)
                pool.dma_start(p_tok, d["p_2"][0, 0].rearrange("(t p) n -> p t n", p=P)).then_inc(sem("p_landed"), 16)

            @block.sync
            def _(sp):
                sp.dma_start(x[:, 0, :], d["x"][0, 0:P, :]).then_inc(sem("x_landed0"), 16)
                sp.dma_start(consts[:, 0:P], d["consts"][:, 0:P]).then_inc(sem("ident_landed"), 16)
                sp.dma_start(cols[:, :], d["params"]).then_inc(sem("params_landed"), 16)
                sp.dma_start(x[:, 1, :], d["x"][0, P:T, :]).then_inc(sem("x_landed1"), 16)


                def load(n):
                    name, src, slot, k, w = units[n]
                    last = [m for m in range(n) if units[m][2] == slot]
                    last = units[last[-1]][0] if last and not (n >= n_early and last[-1] < n_early) else None
                    if last in last_in_place["proj"]:
                        last = split_stages["proj"][-1]

                    def last_used():
                        if last:
                            done = unit_last_fill[last]
                            if isinstance(done, int):
                                sp.wait_ge(sem("down_used"), done)
                            else:
                                filled_by(sp, done)

                    if by_halves(name):
                        for h in range(2):
                            if last and by_halves(last) and h == 0:
                                sp.wait_ge(sem("proj_half_used"), split_at[last][1] + 1)
                            else:
                                last_used()
                            sp.dma_start(split_half(name, h), src[:, 4 * h:4 * h + 4, :]).then_inc(sem(f"half_landed{2 * slot + h}"), 16)
                    else:
                        last_used()
                        sp.dma_start(slot_view(slot, k, w), src).then_inc(sem(f"weights_landed{slot}"), 16)

                wg = d["w_gate"][0].rearrange("e (k p) n -> p e k n", p=P)
                wu = d["w_up"][0].rearrange("e (k p) n -> p e k n", p=P)
                wd = d["w_down"][0].rearrange("e (k p) n -> p e k n", p=P)

                def load_matrix(tag, m, pair):
                    src = (wg, wu, wd)[m % 6 // 2][:, bass.ds(2 * (pair % PAIRS) + m % 2, 1), :, :]
                    sp.dma_start(expert_view(m).unsqueeze(1), src).then_inc(expert_landed(tag, m)[0], 16)

                def load_pairs(tag, n_pairs):
                    def load_next(group, u):
                        used = ("gate", "up", "down")[u % 6 // 2]
                        sp.wait_ge(sem(f"{tag}_{used}_filled"), 2 * (PERIOD * group + u // 6 + 1))
                        m = N_PLACES + u
                        load_matrix(tag, m, PERIOD * group + m // 6)

                    groups, rest = divmod(6 * n_pairs - N_PLACES, 6 * PERIOD)
                    with sp.Fori(0, groups) as group:
                        for u in range(6 * PERIOD):
                            load_next(group, u)
                    for u in range(rest):
                        load_next(groups, u)

                def experts_done(tag, n_pairs):
                    for name in ("gate", "up", "down"):
                        sp.wait_ge(sem(f"{tag}_{name}_filled"), 2 * n_pairs)

                for n in range(n_early):
                    load(n)
                    if n == 0:
                        sp.dma_start(consts[:, P:], d["consts"][:, P:]).then_inc(sem("consts_landed"), 16)
                    if n == 1:
                        sp.dma_start(mem_tok, d["mem"][0].rearrange("(t p) n -> p t n", p=P)).then_inc(sem("mem_landed"), 16)
                    if n == 12:
                        filled_by(sp, "mem_v11")
                        load_matrix("moe", 3, 0)
                        load_matrix("moe", 4, 0)
                        filled_by(sp, "out00")
                        load_matrix("moe", 0, 0)
                for m, free in ((5, "mem_q01"), (6, "mem_q11"), (1, "crossO3"), (2, "mem_o11"), (7, "mem_o01"), (8, "mem_o11")):
                    filled_by(sp, free)
                    load_matrix("moe", m, m // 6)
                load_pairs("moe", PAIRS)
                sp.wait_ge(sem("busiest_ready"), 1)
                count = sp.value_load(busiest[0:1, 0:1], min_val=0, max_val=T)
                experts_done("moe", PAIRS)
                with sp.If(count > CAP):
                    for m in range(N_PLACES):
                        load_matrix("more", m, m // 6)
                    load_pairs("more", MORE)
                    experts_done("more", MORE)
                for n in range(n_early, len(units)):
                    load(n)
                for t in range(TT):
                    sp.wait_ge(sem("result_ready"), t + 1)
                    sp.dma_start(out[0, t * P:t * P + P, :], x[:, t, :]).then_inc(sem("out_stored"), 16)
                sp.wait_ge(sem("out_stored"), 16 * TT)


_INPUTS = ["x", "mem", "w_in", "b_forget", "w_out", "w_mq", "w_mkv", "w_mo", "w_route_group", "b_route_group",
           "w_route_expert", "b_route_expert", "w_gate", "w_up", "w_down", "final_g", "p_2", "w_in_2", "w_branch_a_2",
           "w_branch_b_2", "w_out_2", "norm_post_mix_2", "norm_post_mlp_2", "hg_gnorm_2", "cmp_wk1_2", "cmp_wk2_2",
           "cmp_wv1_2", "cmp_wv2_2", "w_up_2", "w_down_2", "w_ple_2", "w_ple_gate_2", "norm_ple_2"]


def kernel(**inputs):
    import concourse.bacc as bacc
    from concourse.bass_utils import run_bass_kernel_spmd

    nc = bacc.Bacc("TRN2", target_bir_lowering=False, num_devices=1)
    arrays, d = {}, {}
    for name in _INPUTS:
        a = np.ascontiguousarray(inputs[name])
        arrays[f"in_{name}"] = a
        d[name] = nc.dram_tensor(f"in_{name}", a.shape, mybir.dt.from_np(a.dtype), kind="ExternalInput").ap()
    table, const_cols = shape_constants()
    arrays["in_consts"] = table
    d["consts"] = nc.dram_tensor("in_consts", table.shape, F32, kind="ExternalInput").ap()
    out = nc.dram_tensor("out", (1, T, D), F32, kind="ExternalOutput").ap()
    arrays["in_params"] = parameter_columns(inputs)
    d["params"] = nc.dram_tensor("in_params", arrays["in_params"].shape, F32, kind="ExternalInput").ap()
    two_blocks_kernel(nc, d, const_cols, out)
    r = run_bass_kernel_spmd(nc, [arrays], core_ids=[0])
    return r.results[0]["out"]
```
